# Optimizing a Trainium2 kernel written in Bass

```python
import functools
import jax, jax.numpy as jnp
from jax import lax
import numpy as np

D_MODEL = 1024
BATCH = 1
SEQ = 1024
DEPTH = 1
DEC_BATCH = 8
DEC_SEQ = 1
PAST_LEN = 512
PAGE_SIZE = 128

HEAD_DIM = 64
ATT_GROUPS = ((128, 1), (512, 4), (2048, 16))
N_GROUPS = len(ATT_GROUPS)
HEADS_PER_GROUP = 4
ATT_WIDTH = N_GROUPS * HEADS_PER_GROUP * HEAD_DIM
ATT_OUT = HEADS_PER_GROUP * HEAD_DIM
BLOCK = 128
RWKV_HEADS = 8
RWKV_HEAD = 64
RWKV_WIDTH = RWKV_HEADS * RWKV_HEAD
DECAY_LORA = 64
ICLR_LORA = 64
GATE_LORA = 128
RWKV_PROJ = 3 * RWKV_WIDTH + DECAY_LORA + ICLR_LORA + GATE_LORA
P_TOTAL = 3 * ATT_WIDTH + RWKV_PROJ + 2 * D_MODEL
D_FF = 2816
CONV_W = 3
RMS_EPS = 1e-6
GN_EPS = 64e-5
L2_EPS = 1e-12

kernel_name = 'hybrid_dilated_attn_rwkv7_convffn_step'

def rms_norm(x, g):
    xf = x.astype(jnp.float32)
    y = xf * lax.rsqrt(jnp.mean(xf * xf, axis=-1, keepdims=True) + RMS_EPS)
    return (y * g.astype(jnp.float32)).astype(x.dtype)

def dilated_band_attention(q, k, v, dil, n_step):
    b, s, h, dh = q.shape
    seg = dil * BLOCK
    sp = -(-s // seg) * seg
    nb = sp // seg

    def to_res(t):
        t = jnp.pad(t, ((0, 0), (0, sp - s), (0, 0), (0, 0))).reshape(b, nb * BLOCK, dil, h, dh)
        return t.transpose(0, 2, 1, 3, 4).reshape(b, dil, nb, BLOCK, h, dh)

    def with_prev(t):
        prev = jnp.pad(t, ((0, 0), (0, 0), (1, 0), (0, 0), (0, 0), (0, 0)))[:, :, :-1]
        return jnp.concatenate([prev, t], axis=3)

    qb = to_res(q).astype(jnp.float32)
    kb = with_prev(to_res(k)).astype(jnp.float32)
    vb = with_prev(to_res(v)).astype(jnp.float32)
    scores = jnp.einsum('brnqhd,brnkhd->brnhqk', qb, kb) * (dh ** -0.5)
    qi = jnp.arange(BLOCK)[:, None]
    kj = jnp.arange(2 * BLOCK)[None, :]
    rel = qi + BLOCK - kj
    band = (rel >= 0) & (rel <= n_step)
    blk = jnp.arange(nb)[:, None, None]
    mask = band[None] & ((blk > 0) | (kj[None] >= BLOCK))
    scores = jnp.where(mask[None, None, :, None], scores, -jnp.inf)
    lse = jax.nn.logsumexp(scores, axis=-1)
    o = jnp.einsum('brnhqk,brnkhd->brnqhd', jnp.exp(scores - lse[..., None]), vb)
    o = o.reshape(b, dil, nb * BLOCK, h, dh).transpose(0, 2, 1, 3, 4).reshape(b, sp, h, dh)[:, :s]
    lse = lse.transpose(0, 1, 2, 4, 3).reshape(b, dil, nb * BLOCK, h).transpose(0, 2, 1, 3).reshape(b, sp, h)[:, :s]
    return o, lse

def dilated_cached_attention(q, k_all, v_all, n_past, dil, n_step):
    t, dh = q.shape[1], q.shape[-1]
    idx = n_past + jnp.arange(t)[:, None] - dil * jnp.arange(n_step + 1)[None, :]
    valid = idx >= 0
    idx = jnp.maximum(idx, 0)
    kg = k_all[:, idx].astype(jnp.float32)
    vg = v_all[:, idx].astype(jnp.float32)
    scores = jnp.einsum('bqhd,bqjhd->bqhj', q.astype(jnp.float32), kg) * (dh ** -0.5)
    scores = jnp.where(valid[None, :, None, :], scores, -jnp.inf)
    lse = jax.nn.logsumexp(scores, axis=-1)
    o = jnp.einsum('bqhj,bqjhd->bqhd', jnp.exp(scores - lse[..., None]), vg)
    return o, lse

def merge_groups(outs, lses):
    w = jax.nn.softmax(jnp.stack(lses), axis=0)
    o = jnp.sum(w[..., None] * jnp.stack(outs), axis=0)
    return o.reshape(o.shape[0], o.shape[1], ATT_OUT)

def attend_prompt(q, k, v):
    t = q.shape[1]
    outs, lses, k_rows, v_rows = [], [], [], []
    for gi, (win, dil) in enumerate(ATT_GROUPS):
        o, l = dilated_band_attention(q[:, :, gi], k[:, :, gi], v[:, :, gi], dil, win // dil)
        outs.append(o)
        lses.append(l)
        keep = min(win, t)
        k_rows.append(k[:, t - keep:, gi])
        v_rows.append(v[:, t - keep:, gi])
    return merge_groups(outs, lses), k_rows, v_rows

def attend_cached(q, k, v, k_bufs, v_bufs):
    t = q.shape[1]
    outs, lses, k_rows, v_rows = [], [], [], []
    for gi, (win, dil) in enumerate(ATT_GROUPS):
        n_past = k_bufs[gi].shape[1]
        k_all = jnp.concatenate([k_bufs[gi].astype(k.dtype), k[:, :, gi]], axis=1)
        v_all = jnp.concatenate([v_bufs[gi].astype(v.dtype), v[:, :, gi]], axis=1)
        o, l = dilated_cached_attention(q[:, :, gi], k_all, v_all, n_past, dil, win // dil)
        outs.append(o)
        lses.append(l)
        keep = min(win, n_past + t)
        k_rows.append(k_all[:, n_past + t - keep:])
        v_rows.append(v_all[:, n_past + t - keep:])
    return merge_groups(outs, lses), k_rows, v_rows

def rwkv7_time_mix(pr, shift_prev, wkv0, mu, w0, w2, a0, a2, g2, k_k, k_a, r_k, gn_g, gn_b):
    b, t, _ = pr.shape
    f32 = jnp.float32
    p = pr.astype(f32)
    prev = jnp.concatenate([shift_prev[:, None].astype(f32), p[:, :-1]], axis=1)
    xs = p + mu.astype(f32) * (prev - p)
    cuts = [RWKV_WIDTH, 2 * RWKV_WIDTH, 3 * RWKV_WIDTH, 3 * RWKV_WIDTH + DECAY_LORA, 3 * RWKV_WIDTH + DECAY_LORA + ICLR_LORA]
    r, k, v, wl, al, gl = jnp.split(xs, cuts, axis=-1)
    w = -jax.nn.softplus(-(w0 + jnp.tanh(wl) @ w2)) - 0.5
    decay = jnp.exp(-jnp.exp(w))
    a = jax.nn.sigmoid(a0 + al @ a2)
    g = jax.nn.sigmoid(gl) @ g2

    def heads(z):
        return z.reshape(b, t, RWKV_HEADS, RWKV_HEAD)

    kk = heads(k * k_k)
    kk = kk / jnp.maximum(jnp.sqrt(jnp.sum(kk * kk, axis=-1, keepdims=True)), L2_EPS)
    k = k * (1.0 + (a - 1.0) * k_a)
    rh, kh, vh, ah, wh = heads(r), heads(k), heads(v), heads(a), heads(decay)
    seq = tuple(z.transpose(1, 0, 2, 3) for z in (rh, wh, kh, vh, -kk, kk * ah))

    def step(S, inp):
        r_t, w_t, k_t, v_t, na_t, nb_t = inp
        sa = jnp.einsum('bhij,bhj->bhi', S, na_t)
        S = S * w_t[:, :, None, :] + sa[..., None] * nb_t[:, :, None, :] + v_t[..., None] * k_t[:, :, None, :]
        return S, jnp.einsum('bhij,bhj->bhi', S, r_t)

    S, ys = lax.scan(step, wkv0.astype(f32), seq)
    y = ys.transpose(1, 0, 2, 3)
    mean = jnp.mean(y, axis=-1, keepdims=True)
    var = jnp.mean(jnp.square(y - mean), axis=-1, keepdims=True)
    yn = ((y - mean) * lax.rsqrt(var + GN_EPS)).reshape(b, t, RWKV_WIDTH) * gn_g + gn_b
    bonus = jnp.sum(rh * kh * r_k, axis=-1, keepdims=True) * vh
    out = (yn + bonus.reshape(b, t, RWKV_WIDTH)) * g
    return out.astype(pr.dtype), pr[:, -1], S

def decoder_layer(x, attend, shift_prev, wkv0, conv_prev, lw):
    b, t, _ = x.shape
    xn = rms_norm(x, lw['ln1_g'])
    proj = xn @ lw['w_in']
    c0 = 3 * ATT_WIDTH + RWKV_PROJ
    q, k, v, pr, g_att, g_rwkv = jnp.split(proj, [ATT_WIDTH, 2 * ATT_WIDTH, 3 * ATT_WIDTH, c0, c0 + D_MODEL], axis=-1)
    hs = (b, t, N_GROUPS, HEADS_PER_GROUP, HEAD_DIM)
    q = rms_norm(q.reshape(hs), lw['q_norm_g'])
    k = rms_norm(k.reshape(hs), lw['k_norm_g'])
    v = v.reshape(hs)
    o_att, k_rows, v_rows = attend(q, k, v)
    y_att = o_att.astype(x.dtype) @ lw['w_attn_out']
    o_rwkv, shift_last, wkv_last = rwkv7_time_mix(
        pr, shift_prev, wkv0, lw['rwkv_mu'], lw['rwkv_w0'], lw['rwkv_w2'], lw['rwkv_a0'], lw['rwkv_a2'],
        lw['rwkv_g2'], lw['rwkv_k_k'], lw['rwkv_k_a'], lw['rwkv_r_k'], lw['rwkv_gn_g'], lw['rwkv_gn_b'])
    y_rwkv = o_rwkv @ lw['w_rwkv_out']
    merged = jax.nn.sigmoid(g_att) * y_att + jax.nn.sigmoid(g_rwkv) * y_rwkv
    x = x + merged @ lw['w_o']
    u = rms_norm(x, lw['ln2_g']) @ lw['w_up']
    u_ext = jnp.concatenate([conv_prev.astype(u.dtype), u], axis=1)
    cw = lw['conv_w']
    c = lw['conv_b']
    for i in range(CONV_W):
        c = c + u_ext[:, i:i + t] * cw[i]
    gate, val = jnp.split(c, [D_FF], axis=-1)
    x = x + (jax.nn.silu(gate) * val) @ lw['w_down']
    return x, k_rows, v_rows, shift_last, wkv_last, u_ext[:, t:]

def setup_inputs(seed: int = 0) -> dict:
    key = jax.random.key(seed)
    ks = iter(jax.random.split(key, 48))
    f32 = jnp.float32

    def nrm(shape, scale=1.0):
        return scale * jax.random.normal(next(ks), shape, f32)

    def gain(shape):
        return 1.0 + 0.05 * jax.random.normal(next(ks), shape, f32)

    def kv_shape(win):
        return (DEPTH, DEC_BATCH, min(win, PAST_LEN), HEADS_PER_GROUP, HEAD_DIM)

    return {
        'x_prompt': nrm((BATCH, SEQ, D_MODEL)),
        'x_sample': nrm((DEC_BATCH, DEC_SEQ, D_MODEL)),
        'cache_k_w128': nrm(kv_shape(128)),
        'cache_v_w128': nrm(kv_shape(128)),
        'cache_k_w512': nrm(kv_shape(512)),
        'cache_v_w512': nrm(kv_shape(512)),
        'cache_k_w2048': nrm(kv_shape(2048)),
        'cache_v_w2048': nrm(kv_shape(2048)),
        'state_rwkv_shift': nrm((DEPTH, DEC_BATCH, RWKV_PROJ)),
        'state_rwkv_wkv': nrm((DEPTH, DEC_BATCH, RWKV_HEADS, RWKV_HEAD, RWKV_HEAD), 0.3),
        'state_ffn_conv': nrm((DEPTH, DEC_BATCH, CONV_W - 1, 2 * D_FF)),
        'ln1_g': gain((DEPTH, D_MODEL)),
        'w_in': nrm((DEPTH, D_MODEL, P_TOTAL), D_MODEL ** -0.5),
        'q_norm_g': gain((DEPTH, HEAD_DIM)),
        'k_norm_g': gain((DEPTH, HEAD_DIM)),
        'w_attn_out': nrm((DEPTH, ATT_OUT, D_MODEL), ATT_OUT ** -0.5),
        'rwkv_mu': jax.random.uniform(next(ks), (DEPTH, RWKV_PROJ), f32),
        'rwkv_w0': 0.5 + nrm((DEPTH, RWKV_WIDTH), 0.5),
        'rwkv_w2': nrm((DEPTH, DECAY_LORA, RWKV_WIDTH), 0.5 * DECAY_LORA ** -0.5),
        'rwkv_a0': nrm((DEPTH, RWKV_WIDTH), 0.1),
        'rwkv_a2': nrm((DEPTH, ICLR_LORA, RWKV_WIDTH), 0.5 * ICLR_LORA ** -0.5),
        'rwkv_g2': nrm((DEPTH, GATE_LORA, RWKV_WIDTH), GATE_LORA ** -0.5),
        'rwkv_k_k': 0.85 + nrm((DEPTH, RWKV_WIDTH), 0.05),
        'rwkv_k_a': gain((DEPTH, RWKV_WIDTH)),
        'rwkv_r_k': nrm((DEPTH, RWKV_HEADS, RWKV_HEAD), 0.1),
        'rwkv_gn_g': gain((DEPTH, RWKV_WIDTH)),
        'rwkv_gn_b': nrm((DEPTH, RWKV_WIDTH), 0.02),
        'w_rwkv_out': nrm((DEPTH, RWKV_WIDTH, D_MODEL), RWKV_WIDTH ** -0.5),
        'w_o': nrm((DEPTH, D_MODEL, D_MODEL), D_MODEL ** -0.5),
        'ln2_g': gain((DEPTH, D_MODEL)),
        'w_up': nrm((DEPTH, D_MODEL, 2 * D_FF), D_MODEL ** -0.5),
        'conv_w': nrm((DEPTH, CONV_W, 2 * D_FF), CONV_W ** -0.5),
        'conv_b': nrm((DEPTH, 2 * D_FF), 0.02),
        'w_down': nrm((DEPTH, D_FF, D_MODEL), D_FF ** -0.5),
    }

def reference(x_prompt, x_sample, cache_k_w128, cache_v_w128, cache_k_w512, cache_v_w512, cache_k_w2048, cache_v_w2048,
              state_rwkv_shift, state_rwkv_wkv, state_ffn_conv, ln1_g, w_in, q_norm_g, k_norm_g, w_attn_out,
              rwkv_mu, rwkv_w0, rwkv_w2, rwkv_a0, rwkv_a2, rwkv_g2, rwkv_k_k, rwkv_k_a, rwkv_r_k, rwkv_gn_g, rwkv_gn_b,
              w_rwkv_out, w_o, ln2_g, w_up, conv_w, conv_b, w_down):
    k_caches = (cache_k_w128, cache_k_w512, cache_k_w2048)
    v_caches = (cache_v_w128, cache_v_w512, cache_v_w2048)
    pk = [[] for _ in ATT_GROUPS]
    pv = [[] for _ in ATT_GROUPS]
    sk = [[] for _ in ATT_GROUPS]
    sv = [[] for _ in ATT_GROUPS]
    p_shift, s_shift, p_wkv, s_wkv, p_conv, s_conv = [], [], [], [], [], []
    xp, xs = x_prompt, x_sample
    bp = xp.shape[0]
    for l in range(DEPTH):
        lw = dict(ln1_g=ln1_g[l], w_in=w_in[l], q_norm_g=q_norm_g[l], k_norm_g=k_norm_g[l], w_attn_out=w_attn_out[l],
                  rwkv_mu=rwkv_mu[l], rwkv_w0=rwkv_w0[l], rwkv_w2=rwkv_w2[l], rwkv_a0=rwkv_a0[l], rwkv_a2=rwkv_a2[l],
                  rwkv_g2=rwkv_g2[l], rwkv_k_k=rwkv_k_k[l], rwkv_k_a=rwkv_k_a[l], rwkv_r_k=rwkv_r_k[l],
                  rwkv_gn_g=rwkv_gn_g[l], rwkv_gn_b=rwkv_gn_b[l], w_rwkv_out=w_rwkv_out[l], w_o=w_o[l],
                  ln2_g=ln2_g[l], w_up=w_up[l], conv_w=conv_w[l], conv_b=conv_b[l], w_down=w_down[l])
        xp, kr, vr, sh, wkv, cv = decoder_layer(
            xp, attend_prompt,
            jnp.zeros((bp, RWKV_PROJ), xp.dtype),
            jnp.zeros((bp, RWKV_HEADS, RWKV_HEAD, RWKV_HEAD), jnp.float32),
            jnp.zeros((bp, CONV_W - 1, 2 * D_FF), xp.dtype), lw)
        for gi in range(N_GROUPS):
            pk[gi].append(kr[gi])
            pv[gi].append(vr[gi])
        p_shift.append(sh)
        p_wkv.append(wkv)
        p_conv.append(cv)
        attend_s = functools.partial(attend_cached, k_bufs=tuple(c[l] for c in k_caches),
                                     v_bufs=tuple(c[l] for c in v_caches))
        xs, kr, vr, sh, wkv, cv = decoder_layer(xs, attend_s, state_rwkv_shift[l], state_rwkv_wkv[l],
                                                state_ffn_conv[l], lw)
        for gi in range(N_GROUPS):
            sk[gi].append(kr[gi])
            sv[gi].append(vr[gi])
        s_shift.append(sh)
        s_wkv.append(wkv)
        s_conv.append(cv)
    st = functools.partial(jnp.stack, axis=0)
    return (xp, xs,
            st(pk[0]), st(sk[0]), st(pv[0]), st(sv[0]),
            st(pk[1]), st(sk[1]), st(pv[1]), st(sv[1]),
            st(pk[2]), st(sk[2]), st(pv[2]), st(sv[2]),
            st(p_shift), st(s_shift), st(p_wkv), st(s_wkv), st(p_conv), st(s_conv))


_drawn_inputs = setup_inputs


def setup_inputs(seed=0):
    import zlib

    import numpy as np

    out = dict(_drawn_inputs(seed))
    spreads = {}
    factors = {'q_norm_g': 8.0, 'rwkv_k_k': 6.044, 'rwkv_gn_g': 3.423, 'rwkv_gn_b': 8.0, 'conv_b': 3.957}
    for name, (base, spread) in spreads.items():
        noise = np.random.default_rng([zlib.crc32(name.encode()), seed]).standard_normal(out[name].shape)
        drawn = base * np.exp(spread * noise) if base else spread * noise
        out[name] = __import__('jax').numpy.asarray(drawn.astype(out[name].dtype))
    for name, factor in factors.items():
        out[name] = (out[name] * factor).astype(out[name].dtype)
    return out
```

```python
from contextlib import ExitStack

import numpy as np

import concourse.bass as bass
from concourse import mybir

F32 = mybir.dt.float32
F32R = mybir.dt.float32r
ALU = mybir.AluOpType
ACT = mybir.ActivationFunctionType
AX = mybir.AxisListType

P = 128
D = 1024
KD = D // P
S = 1024
NS = 8
T = S + NS
PC = T // 3
HD = 64
G, H = 3, 4
AW = G * H * HD
RH = 8
RW = RH * HD
RP = 3 * RW + 256
FF = 2816
KF = FF // P
RMS_EPS, GN_EPS, L2_EPS = 1e-6, 64e-5, 1e-12
DECAY = float(np.exp(-0.5))
NEG = -1e30
DIL = (1, 4, 16)
HLO_PARTS = ((0, 1), (1, 4), (4, 11), (11, KF))
NT = S // P

N_RW, N_QK, N_GA, N_V = RP // P, 2 * AW // P, 2 * D // P, AW // P
N_AO, N_RO, N_WO, N_UP, N_DN = 2, 4, KD, 2 * KF, 3 * KD
B_RW = 0
B_QK = B_RW + N_RW
B_V = B_QK + N_QK
B_GA = B_V + N_V
B_AO = B_GA + N_GA
B_RO = B_AO + N_AO
B_WO = B_RO + N_RO
B_UP = B_WO + N_WO
B_DN = B_UP + N_UP
NB = B_DN + N_DN
P_AO = 3 * B_AO
P_RO = P_AO + 12 * N_AO
P_WO = P_RO + 6 * N_RO
P_UP = P_WO + 3 * N_WO
P_DN = P_UP + 3 * N_UP

PAR = {}
_at = 0
for _n, _w in (("g1", KD), ("g2", KD), ("qkg", N_QK), ("mu", N_RW), ("w0", 4), ("a0", 4), ("kk", 4), ("ka", 4),
               ("rk", 4), ("gng", 4), ("gnb", 4), ("cw0", 2 * KF), ("cw1", 2 * KF), ("cw2", 2 * KF), ("cb", 2 * KF)):
    PAR[_n] = (_at, _w)
    _at += _w
N_PAR = _at

CST = {}
_at = 0
for _n, _w in (("ident", P), ("bd", P), ("su", P), ("iu", P), ("sl", P), ("lv0", P), ("lv0t", P), ("lvl", 6 * P),
               ("prev", P), ("cur", P), ("cur2", P), ("prevcur", 0), ("scan", 4 * P), ("eps", 4), ("mones", P)):
    CST[_n] = (_at, _w)
    _at += _w
N_CST = _at

STEPS = (
    ("r_tanh", "r_sgl", "r_sgw", "r_sga", "r_gate", "kk_squared", "kk_len", "e_w", "e_wi", "e_wm", "e_wp", "p1_ready", "gv_ready", "u_ready", "y_ready", "y_squared", "y_dev", ),
    ("x_diff", "x_mixed", "xs_ready", "kk_raw", "kk_clamped", "kk_inv", "kk_ready", "c_sum", "c_mid", "c_ready", "cp_ready", "b_raw", "k_gain", "k_ready", "rk_raw", "rk_ready", "bt_ready", "kt_ready", "at_ready", "rt_ready", "wend_ready", "rk_summed", "sm_ready", "s_sum", "s_ready", "y_centred", "y_normed", "y_gained", "y_bonus", "o_ready", ),
    ("mm_kk", "mm_bonus", "mm_p1", "mm_gv", "mm_u", "mm_s", "mm_y", "mm_mean", "mm_var", ),
)


def step(name, i):
    steps = next(x for x in STEPS if name in x)
    return len(steps) * i + steps.index(name) + 1


def constants():
    c = np.zeros((P, N_CST), np.float32)
    i, j = np.arange(P)[:, None], np.arange(P)[None, :]

    def put(name, value, off=0):
        a = CST[name][0] + off
        c[:, a:a + np.broadcast_to(value, (P, value.shape[-1])).shape[1]] = value

    put("ident", (i == j) * 1.0)
    put("bd", (i // HD == j // HD) * 1.0)
    put("su", (i < j) * 1.0)
    put("iu", (i <= j) * 1.0)
    put("sl", (i > j) * 1.0)
    low = (i // 2 == j // 2) & (i > j)
    put("lv0", low * 1.0)
    put("lv0t", low.T * 1.0)
    for k in range(1, 7):
        b = 1 << k
        put("lvl", ((i // (2 * b) == j // (2 * b)) & (i // b > j // b)) * 1.0, (k - 1) * P)
    put("prev", np.where(j >= i, 0.0, NEG))
    put("cur", np.where(j <= i, 0.0, NEG))
    put("cur2", np.where((j <= i) & (i // HD == j // HD), 0.0, NEG))
    scan = np.ones((P, 4 * P))
    scan[:, ::P] = 0
    put("scan", scan)
    put("eps", np.broadcast_to(np.array([RMS_EPS, GN_EPS, 0.0, 0.0]), (P, 4)))
    put("mones", np.full((P, P), 1.0))
    return c


def rup(x):
    return (x + 31) // 32 * 32


class Map:

    def __init__(self, nc, start):
        self.nc, self.at = nc, start

    def put(self, name, shape, dt=F32):
        n = int(np.prod(shape[1:])) * 4
        t = self.nc.alloc_sbuf_tensor_at(name, list(shape), dt, offset=self.at)
        self.at = rup(self.at + n)
        return t


def program(nc, ins, outs):
    xT, wst, cst_d, par_d = ins["xT"], ins["wst"], ins["cst"], ins["par"]
    sems = {}
    ctx = ExitStack()

    def sem(name):
        if name not in sems:
            sems[name] = ctx.enter_context(nc.semaphore(name))
        return sems[name]

    with ctx:
        m = Map(nc, 16512)
        wraw = m.put("wraw", [P, 2, KD, P])
        whi = m.put("whi", [P, 2, KD, P], F32R)
        wlo = m.put("wlo", [P, 2, KD, P], F32R)
        par = m.put("par", [P, N_PAR])
        big = m.at
        after_big = rup(big + KF * T * 4)
        m.at = after_big
        cst = m.put("cst", [P, N_CST])
        gap = m.at
        ahi_at = 229344 - 2 * rup(KD * T * 4)
        m.at = ahi_at
        ahi = m.put("ahi", [P, KD, T], F32R)
        alo = m.put("alo", [P, KD, T], F32R)
        m.at = stage_at = gap
        stage = m.put("stage", [P, 2, T])
        gap2 = m.at
        mb = Map(nc, big)
        xraw = mb.put("xraw", [P, KD, T])
        nsum = mb.put("nsum", [P, T])
        ntmp = mb.put("ntmp", [P, 2, T])
        nrt = mb.put("nrt", [P, T])
        nrs = mb.put("nrs", [P, T])
        mb = Map(nc, big)
        pin = mb.put("pin", [P, N_RW, 1 + P])
        xs = mb.put("xs", [P, N_RW, P])
        sg = mb.put("sg", [P, 9, P])
        kkn = mb.put("kkn", [P, 4, P])
        tmp = mb.put("tmp", [P, 4, P])
        kt = mb.put("kt", [P, 4, P])
        bt = mb.put("bt", [P, 4, P])
        cs = mb.put("cs", [P, 4, P])
        cp = mb.put("cp", [P, 4, P])
        ew = mb.put("ew", [P, 4, P])
        ewp = mb.put("ewp", [P, 4, P])
        ewi = mb.put("ewi", [P, 4, P])
        gg = mb.put("gg", [P, 4, P])
        bon = mb.put("bon", [P, 4, P])
        ar = mb.put("ar", [P, 4, 2, P])
        vtm = mb.put("vtm", [P, RW])
        atm = mb.put("atm", [P, RW])
        btm = mb.put("btm", [P, RW])
        ktm = mb.put("ktm", [P, RW])
        gq = mb.put("gq", [P, RH, 2, P])
        nq = mb.put("nq", [P, RH, 2, P])
        ti = mb.put("ti", [P, RH, P])
        tt = mb.put("tt", [P, RH, P])
        tiles_end = mb.at
        mb = Map(nc, gap2)
        xx = mb.put("xx", [P, RH, P])
        p1 = mb.put("p1", [P, 4, P])
        small = mb.at
        mb = Map(nc, tiles_end)
        gv = mb.put("gv", [P, RW])
        uu = mb.put("uu", [P, RW])
        st = mb.put("st", [P, 4, P])
        sm = mb.put("sm", [P, 4, P])
        assert mb.at <= after_big, mb.at - after_big
        mb = Map(nc, small)
        cm = mb.put("cm", [P, 4])
        wm = mb.put("wm", [P, 4])
        wend = mb.put("wend", [P, 4])
        lora = mb.put("lora", [P, 2, RW])
        assert mb.at <= ahi_at, mb.at - ahi_at

        mb = Map(nc, big + 16384)
        svec = mb.put("svec", [NS, 6, RW])
        srow = mb.put("srow", [P, 6, HD])
        sst = mb.put("sst", [P, 32, HD])
        stp = mb.put("stp", [P, 32, HD])
        ssa = mb.put("ssa", [P, 32])
        syo = mb.put("syo", [P, 32])
        sym = mb.put("sym", [NS, RW])
        s4 = mb.put("s4", [P, 12, 4, NS])
        ssg = mb.put("ssg", [P, 9, NS])
        assert mb.at <= after_big

        mb = Map(nc, big)
        qgs = [mb.put(f"qg{n}", [P, 2, S]) for n in range(2)]
        kgs = [mb.put(f"kg{n}", [P, 2, S]) for n in range(2)]
        vgs = [mb.put(f"vg{n}", [P, 8, H * HD]) for n in range(2)]
        qz = mb.put("qz", [P, 2, H, P])
        sc = mb.put("sc", [P, 2, H, 2, P])
        pt = mb.put("pt", [P, 2, 2, H, P])
        ob = mb.put("ob", [P, 2, 264])
        assert mb.at <= after_big
        mb = Map(nc, big)
        skc = mb.put("skc", [96, 129, HD])
        svc = mb.put("svc", [96, 129, HD])
        sq = mb.put("sq", [96, HD])
        ssc = mb.put("ssc", [96, 129])
        sso = mb.put("sso", [96, HD])
        snm = mb.put("snm", [96, 2])
        mb = Map(nc, big)
        oah = mb.put("oah", [P, 2, T], F32R)
        oal = mb.put("oal", [P, 2, T], F32R)
        orh = mb.put("orh", [P, 4, T], F32R)
        orl = mb.put("orl", [P, 4, T], F32R)
        ym = mb.put("ym", [P, KD, T])
        mo_at = big + 2 * 2 * T * 4
        mb = Map(nc, mo_at)
        mo = mb.put("mo", [P, 2, G, 264])
        md = mb.put("md", [P, 2, G, H])
        mn = mb.put("mn", [P, 2, 2 * H])
        om = mb.put("om", [P, 2, H * HD])
        mb = Map(nc, big)
        hhi = mb.put("hhi", [P, KF, T], F32R)
        mb = Map(nc, after_big)
        ug = mb.put("ug", [P, 2, 2 + T])
        cc = mb.put("cc", [P, 2, T])
        hlo_st = mb.put("hlo_st", [P, 1, T], F32R)
        cst8 = mb.put("cst8", [P, 2 * KF, 2, NS])
        assert mb.at <= ahi_at, mb.at - ahi_at
        hlo_at = 229344 - rup(KF * T * 4)
        mb = Map(nc, hlo_at)
        hlo = mb.put("hlo", [P, KF, T], F32R)
        mb = Map(nc, after_big)
        yst = mb.put("yst", [P, 2, PC])
        yrs = mb.put("yrs", [P, 2, PC])
        assert mb.at <= hlo_at, mb.at - hlo_at

        mb = Map(nc, big)
        qsq = mb.put("qsq", [P, 2, PC])
        qrt = mb.put("qrt", [P, 6, PC])
        vst = mb.put("vst", [P, 2, 9, P])

        bank = [ctx.enter_context(nc.psum_tensor(f"bank{i}", [P, 512], F32)) for i in range(8)]

        def C(name, off=0, width=P):
            a = CST[name][0] + off
            return cst[:, a:a + width]

        def par1(name, i):
            a = PAR[name][0]
            return par[:, bass.ds(a + i, 1)]

        eps_rms = cst[:, CST["eps"][0]:CST["eps"][0] + 1]
        eps_gn = cst[:, CST["eps"][0] + 1:CST["eps"][0] + 2]

        qkT_v = outs["qkT"].rearrange("(c p) t -> c p t", p=P)
        gT_v = nc.dram_tensor("gT", [2 * D, T], F32, kind="Internal").ap().rearrange("(c p) t -> c p t", p=P)
        ao = nc.dram_tensor("ao", [G, T, 264], F32, kind="Internal").ap()
        x1T = nc.dram_tensor("x1T", [D, T], F32, kind="Internal").ap().rearrange("(c p) t -> c p t", p=P)
        hloT = nc.dram_tensor("hloT", [FF, T], F32, kind="Internal").ap().rearrange("(c p) t -> c p t", p=P)
        orwT_d = nc.dram_tensor("orwT", [RW, T], F32, kind="Internal").ap()
        xT_c = xT.rearrange("(c p) t -> c p t", p=P)
        yT_c = outs["yT"].rearrange("(c p) t -> c p t", p=P)
        orwT = orwT_d.rearrange("(c p) t -> p c t", p=P)
        rwT = nc.dram_tensor("rwT", [RP, 1 + T], F32, kind="Internal").ap()
        rwT_v = rwT.rearrange("(c p) t -> c p t", p=P)
        rwlast_v = outs["rwlast"].rearrange("(c p) t -> c p t", p=P)
        v_prompt_v = outs["vtok"][0:S].rearrange("(t p) c -> p t c", p=P)
        v_sample_v = outs["vtok"][S:T]

        def stored_before(base, i):
            if base == B_RW:
                return 32 * i
            return 16 * N_RW + (0 if base == B_QK else 8 * N_QK) + 16 * i

        def peeled(engine, count, body):
            body(0)
            with engine.Fori(1, count) as i:
                body(i)

        def looped(engine, count, body):
            with engine.Fori(0, count) as i:
                body(i)

        def units(engine, g, begin, finish):
            def pair(i, more):
                begin(g, i, 1)
                finish(g, i, 0)
                if more:
                    begin(g, i + 1, 0)
                finish(g, i, 1)

            begin(g, 0, 0)
            if g == 0:
                pair(0, True)
            with engine.Fori(1 if g == 0 else 0, 3) as i:
                pair(i, True)
            pair(3, False)

        def has_previous(g, i, s):
            return (not (isinstance(i, int) and i == s == 0), s == 1, False)[g]

        block = ctx.enter_context(nc.Block())

        @block.sync
        def _(sp):
            sp.dma_start(lora[0:HD, 0], ins["w2"]).then_inc(sem("lora_loaded"), 16)
            sp.dma_start(lora[HD:P, 0], ins["a2"]).then_inc(sem("lora_loaded"), 16)
            sp.dma_start(lora[:, 1], ins["g2"]).then_inc(sem("lora_loaded"), 16)
            sp.dma_start(rwT[:, 0:1], ins["zeros"], allow_slow_non_contiguous=True).then_inc(sem("zero_col"), 16)
            sp.dma_start(par[:], par_d).then_inc(sem("par_loaded"), 16)
            sp.dma_start(cst[:], cst_d).then_inc(sem("cst_loaded"), 16)
            for half in range(2):
                c = slice(4 * half, 4 * half + 4)
                sp.dma_start(xraw[:, c], xT.rearrange("(c p) t -> p c t", p=P)[:, c]).then_inc(sem(f"x_loaded{half}"), 16)
            for s in range(2):
                sp.dma_start(wraw[:, s], wst[s]).then_inc(sem(f"w_loaded{s}"), 16)
            def weights(lo, hi):
                with sp.Fori(lo, hi) as i:
                    for s in range(2):
                        sp.wait_ge(sem("w_split"), 2 * i + s - 1)
                        sp.dma_start(wraw[:, s], wst[2 * i + s]).then_inc(sem(f"w_loaded{s}"), 16)

            weights(1, 24)
            for g in range(G):
                n = (128, 512, 512)[g]
                drop = (1, 1, 0)[g]
                for kv in "kv":
                    sp.dma_start(outs[f"{kv}c{g}"][:, 0:n - drop], ins[f"{kv}c{g}"][:, drop:n])\
                        .then_inc(sem("caches_moved"), 16)
            sp.dma_start(outs["convs0"], ins["sconv1"]).then_inc(sem("caches_moved"), 16)
            weights(24, NB // 2)
            sp.wait_ge(sem("caches_moved"), 16 * 7)

        @block.gpsimd
        def _(pool):
            def split(i, s):
                pool.wait_ge(sem(f"w_loaded{s}"), 16 * i + 16)
                pool.sem_inc(sem("w_turn"), 1)
                nc.gpsimd.tensor_scalar(whi[:, s], wraw[:, s], 1.0, 0.0, ALU.mult, ALU.add).then_inc(sem("w_hi"), 1)
                pool.wait_ge(sem("w_hi"), 2 * i + s + 1)
                nc.gpsimd.tensor_tensor(wlo[:, s], wraw[:, s], whi[:, s].bitcast(F32), ALU.subtract)\
                    .then_inc(sem("w_split"), 1)

            split(0, 0)
            split(0, 1)
            with pool.Fori(1, 24) as i:
                for s in range(2):
                    pool.wait_ge(sem("mm_piece"), 6 * i + 3 * s - 3)
                    split(i, s)

            pool.wait_ge(sem("mm_piece"), 3 * B_AO - 3)
            split(B_AO // 2, 0)
            pool.wait_ge(sem("mm_piece"), 3 * B_AO)
            split(B_AO // 2, 1)
            pool.wait_ge(sem("qz_zero"), 1)
            pool.wait_ge(sem("w_split"), B_AO + 2)

            def queries(g, i, s):
                u = 8 * g + 2 * i + s
                qg = qgs[g % 2]
                pool.wait_ge(sem("mm_score"), u - 1)
                for hh in range(2):
                    pool.wait_ge(sem("qz_ready"), 2 * u + hh)
                    pool.wait_ge(sem("qz_zero"), 1)
                    q = slice(hh * HD, (hh + 1) * HD)
                    if g == 0:
                        src, dst = qg[q, :, bass.ds((2 * i + s) * P, P)], qz[q, s, hh::2]
                    elif g == 1:
                        src = qg[q].rearrange("p c (b i r) -> p c b r i", b=2, r=4)[:, :, s, bass.ds(i, 1)]
                        dst = qz[q, s, hh::2].unsqueeze(2)
                    else:
                        src = qg[q].rearrange("p c (i r) -> p c r i", r=16)[:, :, bass.ds(4 * i + 2 * s, 2)]
                        dst = qz[q, s, hh::2].rearrange("p h (r i) -> p h r i", r=2)
                    nc.gpsimd.tensor_copy(dst, src).then_inc(sem("qz_ready"), 1)

            for g in range(G):
                pool.wait_ge(sem(f"qg_loaded{g}"), 16)
                if g == 0:
                    for s in range(2):
                        for hh in range(2):
                            q = slice(hh * HD, (hh + 1) * HD)
                            pool.wait_ge(sem("qz_ready"), 2 * s + hh)
                            nc.gpsimd.tensor_copy(qz[q, s, hh::2], qgs[0][q, :, s * P:(s + 1) * P])\
                                .then_inc(sem("qz_ready"), 1)
                with pool.Fori(1 if g == 0 else 0, 4) as i:
                    for s in range(2):
                        queries(g, i, s)
            ends = [P_AO + 12 * (n + 1) for n in range(N_AO)] + [P_RO + 6 * (n + 1) for n in range(N_RO)]
            for n in range(2, N_AO + N_RO + 2):
                pool.wait_ge(sem("mm_piece"), ends[n - 2])
                split((B_AO + n) // 2, n % 2)
            with pool.Fori((B_WO + 2) // 2, B_DN // 2) as i:
                for s in range(2):
                    pool.wait_ge(sem("mm_piece"), P_WO + 3 * (2 * i + s - 1 - B_WO))
                    split(i, s)
            for s in range(2):
                pool.wait_ge(sem("mm_piece"), P_DN - 3 + 3 * s)
                split(B_DN // 2, s)
            with pool.Fori(B_DN // 2 + 1, NB // 2) as i:
                for s in range(2):
                    pool.wait_ge(sem("mm_down"), 2 * i + s - 1 - B_DN)
                    split(i, s)

        @block.scalar
        def _(act):
            act.wait_ge(sem("cst_loaded"), 16)
            for k in range(KD):
                act.wait_ge(sem(f"x_loaded{k // 4}"), 16)
                if k >= 2:
                    act.wait_ge(sem("n_added"), k - 1)
                nc.scalar.activation(ntmp[:, k % 2], xraw[:, k], ACT.Square).then_inc(sem("n_squared"), 1)
            for n in range(3):
                act.wait_ge(sem("n_summed"), n + 1)
                nc.scalar.activation(nrt[:, n * PC:(n + 1) * PC], bank[n][:, 0:PC], ACT.Sqrt, bias=eps_rms,
                                     scale=1.0 / D).then_inc(sem("n_root"), 1)
            for k in range(KD):
                act.wait_ge(sem("n_scaled"), k + 1)
                nc.scalar.activation(ahi[:, k], xraw[:, k], ACT.Copy).then_inc(sem("a_hi"), 1)

            def rows(base, count, func, dst, last=None):
                def pair(i):
                    for s in range(2):
                        act.wait_ge(sem(f"stored{s}"), stored_before(base, i))
                        for n in range(3):
                            q = 3 * s + n
                            act.wait_ge(sem("mm_piece"), 3 * base + 6 * i + q + 1)
                            nc.scalar.activation(stage[:, s, n * PC:(n + 1) * PC], bank[q % 2][:, 0:PC], func)\
                                .then_inc(sem(f"bank_free{q % 2}"), 1)
                        act.wait_ge(sem("bank_free0"), 3 * base // 2 + 3 * i + (3 * s + 3 + 1) // 2)
                        act.wait_ge(sem("bank_free1"), 3 * base // 2 + 3 * i + (3 * s + 3) // 2)
                        act.dma_start(dst(2 * i + s), stage[:, s]).then_inc(sem(f"stored{s}"), 16)
                        if last:
                            act.dma_start(last(2 * i + s), stage[:, s, S - 1:T]).then_inc(sem(f"stored{s}"), 16)

                (looped if base else peeled)(act, count // 2, pair)

            rows(B_RW, N_RW, ACT.Copy, lambda c: rwT_v[c, :, 1:1 + T], lambda c: rwlast_v[c])
            with act.Fori(0, N_QK // 2) as i:
                for q in range(6):
                    s, n = q // 3, q % 3
                    if n == 0:
                        act.wait_ge(sem(f"stored{s}"), stored_before(B_QK, i))
                    act.wait_ge(sem("mm_piece"), 3 * B_QK + 6 * i + q + 1)
                    nc.scalar.activation(stage[:, s, n * PC:(n + 1) * PC], bank[q % 2][:, 0:PC], ACT.Copy)\
                        .then_inc(sem(f"bank_free{q % 2}"), 1)
                    act.wait_ge(sem(f"bank_free{q % 2}"), 3 * B_QK // 2 + 3 * i + q // 2 + 1)
                    nc.scalar.activation(qsq[:, q % 2], stage[:, s, n * PC:(n + 1) * PC], ACT.Square)\
                        .then_inc(sem("q_squared"), 1)
                    if q:
                        act.wait_ge(sem("q_summed"), 6 * i + q)
                        nc.scalar.activation(qrt[:, q - 1], bank[2 + (q - 1) % 2][:, 0:PC], ACT.Sqrt,
                                             bias=eps_rms, scale=1.0 / HD).then_inc(sem("q_root"), 1)
                    if q == 3:
                        act.wait_ge(sem("q_scaled"), 6 * i + 3)
                        act.dma_start(qkT_v[2 * i], stage[:, 0]).then_inc(sem("stored0"), 16)
                act.wait_ge(sem("q_summed"), 6 * i + 6)
                nc.scalar.activation(qrt[:, 5], bank[3][:, 0:PC], ACT.Sqrt, bias=eps_rms, scale=1.0 / HD)\
                    .then_inc(sem("q_root"), 1)
                act.wait_ge(sem("q_scaled"), 6 * i + 6)
                act.dma_start(qkT_v[2 * i + 1], stage[:, 1]).then_inc(sem("stored1"), 16)

            def v_pair(i):
                for s in range(2):
                    act.wait_ge(sem(f"v_stored{s}"), 32 * i)
                    for n in range(3):
                        q = 3 * s + n
                        act.wait_ge(sem("mm_piece"), 3 * B_V + 6 * i + q + 1)
                        if n < 2:
                            nc.scalar.activation(vst[:, s, 4 * n:4 * n + 4], bank[q % 2][:, :]
                                                 .rearrange("p (t c) -> p t c", c=P), ACT.Copy)\
                                .then_inc(sem(f"bank_free{q % 2}"), 1)
                        else:
                            nc.scalar.activation(vst[0:NS, s, 8], bank[q % 2][0:NS, 0:P], ACT.Copy)\
                                .then_inc(sem(f"bank_free{q % 2}"), 1)
                    act.wait_ge(sem("bank_free0"), 3 * B_V // 2 + 3 * i + (3 * s + 3 + 1) // 2)
                    act.wait_ge(sem("bank_free1"), 3 * B_V // 2 + 3 * i + (3 * s + 3) // 2)
                    act.dma_start(v_prompt_v[:, :, bass.ds((2 * i + s) * P, P)], vst[:, s, 0:8])\
                        .then_inc(sem(f"v_stored{s}"), 16)
                    act.dma_start(v_sample_v[:, bass.ds((2 * i + s) * P, P)], vst[0:NS, s, 8])\
                        .then_inc(sem(f"v_stored{s}"), 16)

            peeled(act, N_V // 2, v_pair)
            for s in range(2):
                act.wait_ge(sem(f"v_stored{s}"), 32 * (N_V // 2))

            act.wait_ge(sem("lora_loaded"), 48)
            act.wait_ge(sem("zero_col"), 16)
            rwT_t = rwT[:, :].rearrange("(c p) t -> p c t", p=P)

            def load_tile(i):
                act.dma_start(pin[:], rwT_t[:, :, bass.ds(i * P, P + 1)]).then_inc(sem("pin_loaded"), 16)

            act.sem_inc(sem("o_free"), 16)

            def gates(i, q):
                s, n = q // 3, q % 3
                if n == 0:
                    act.wait_ge(sem(f"stored{s}"), stored_before(B_GA, i))
                act.wait_ge(sem("mm_piece"), 3 * B_GA + 6 * i + q + 1)
                nc.scalar.activation(stage[:, s, n * PC:(n + 1) * PC], bank[q % 2][:, 0:PC], ACT.Copy)\
                    .then_inc(sem(f"bank_free{q % 2}"), 1)
                if n == 2:
                    act.wait_ge(sem("bank_free0"), 3 * B_GA // 2 + 3 * i + (q + 2) // 2)
                    act.wait_ge(sem("bank_free1"), 3 * B_GA // 2 + 3 * i + (q + 1) // 2)
                    act.dma_start(gT_v[2 * i + s], stage[:, s]).then_inc(sem(f"stored{s}"), 16)

            def rwkv(i, more):
                gates(i, 0)
                act.wait_ge(sem("dve_tile"), step("xs_ready", i))
                nc.scalar.activation(xs[0:HD, 12], xs[0:HD, 12], ACT.Tanh).then_inc(sem("act_tile"), 1)
                nc.scalar.activation(sg[:, 8], xs[:, 13], ACT.Sigmoid).then_inc(sem("act_tile"), 1)
                if more:
                    load_tile(i + 1)
                gates(i, 1)
                act.wait_ge(sem("mm_lora"), 3 * i + 1)
                for c in range(4):
                    last = nc.scalar.activation(sg[:, c], bank[2][:, c * P:(c + 1) * P], ACT.Sigmoid, bias=par1("w0", c))
                last.then_inc(sem("act_tile"), 1)
                act.wait_ge(sem("mm_lora"), 3 * i + 2)
                for c in range(4):
                    last = nc.scalar.activation(sg[:, 4 + c], bank[3][:, c * P:(c + 1) * P], ACT.Sigmoid,
                                                bias=par1("a0", c))
                last.then_inc(sem("act_tile"), 1)
                act.wait_ge(sem("mm_lora"), 3 * i + 3)
                nc.scalar.activation(gg[:], bank[4][:].rearrange("p (c t) -> p c t", c=4), ACT.Copy)\
                    .then_inc(sem("act_tile"), 1)
                act.wait_ge(sem("dve_tile"), step("kk_raw", i))
                nc.scalar.activation(tmp[:], kkn[:], ACT.Square).then_inc(sem("act_tile"), 1)
                act.wait_ge(sem("pe_tile"), step("mm_kk", i))
                nc.scalar.activation(tmp[:], bank[5][:].rearrange("p (c t) -> p c t", c=4), ACT.Sqrt)\
                    .then_inc(sem("act_tile"), 1)
                act.wait_ge(sem("dve_tile"), step("c_ready", i))
                nc.scalar.activation(ew[:], cs[:], ACT.Exp, scale=-DECAY).then_inc(sem("act_tile"), 1)
                nc.scalar.activation(ewi[:], cs[:], ACT.Exp, scale=DECAY).then_inc(sem("act_tile"), 1)
                nc.scalar.activation(wm[:], cm[:], ACT.Exp, scale=-DECAY).then_inc(sem("act_tile"), 1)
                act.wait_ge(sem("dve_tile"), step("cp_ready", i))
                nc.scalar.activation(ewp[:], cp[:], ACT.Exp, scale=-DECAY).then_inc(sem("act_tile"), 1)
                gates(i, 2)
                for n, (dst, b) in enumerate(((vtm, 6), (atm, 7), (btm, 2), (ktm, 3))):
                    if n == 1:
                        gates(i, 3)
                    act.wait_ge(sem("mm_turn"), 4 * i + n + 1)
                    nc.scalar.activation(dst[:], bank[b][:], ACT.Copy).then_inc(sem("turned"), 1)
                act.wait_ge(sem("pe_tile"), step("mm_p1", i))
                nc.scalar.activation(p1[:], bank[2][:].rearrange("p (c t) -> p c t", c=4), ACT.Copy)\
                    .then_inc(sem("act_tile"), 1)
                act.wait_ge(sem("pe_tile"), step("mm_gv", i))
                nc.scalar.activation(gv[:], bank[3][:], ACT.Copy).then_inc(sem("act_tile"), 1)
                act.wait_ge(sem("pe_tile"), step("mm_u", i))
                nc.scalar.activation(uu[:], bank[4][:], ACT.Copy).then_inc(sem("act_tile"), 1)
                act.wait_ge(sem("pe_tile"), step("mm_y", i))
                nc.scalar.activation(cs[:], bank[5][:].rearrange("p (c t) -> p c t", c=4), ACT.Copy)\
                    .then_inc(sem("act_tile"), 1)
                act.wait_ge(sem("dve_tile"), step("y_centred", i))
                nc.scalar.activation(ew[:], cp[:], ACT.Square).then_inc(sem("act_tile"), 1)
                act.wait_ge(sem("pe_tile"), step("mm_var", i))
                nc.scalar.activation(ewi[:], bank[3][:].rearrange("p (c t) -> p c t", c=4), ACT.Sqrt, bias=eps_gn,
                                     scale=1.0 / HD).then_inc(sem("act_tile"), 1)
                gates(i, 4)
                act.wait_ge(sem("dve_tile"), step("o_ready", i))
                act.dma_start(orwT[:, :, bass.ds(i * P, P)], cp[:]).then_inc(sem("o_free"), 16)
                gates(i, 5)

            load_tile(0)
            with act.Fori(0, NT - 1) as i:
                rwkv(i, True)
            rwkv(NT - 1, False)
            act.wait_ge(sem("o_free"), 16 * NT + 16)
            for s in range(2):
                act.wait_ge(sem(f"stored{s}"), stored_before(B_GA, NT))
            act.wait_ge(sem("dve_tile"), step("s_ready", NT - 1))
            for hh in range(2):
                act.dma_start(outs["wkvp"][hh], st[hh * HD:(hh + 1) * HD, :, hh * HD:(hh + 1) * HD])\
                    .then_inc(sem("wkvp_stored"), 16)
            act.wait_ge(sem("wkvp_stored"), 32)

            slow = dict(allow_slow_non_contiguous=True)
            act.dma_start(pin[:, :, 0:NS], ins["shT"].rearrange("(c p) t -> p c t", p=P)).then_inc(sem("u_loaded"), 16)
            act.dma_start(pin[:, :, NS:2 * NS], rwT_t[:, :, 1 + S:1 + T]).then_inc(sem("u_loaded"), 16)
            act.dma_start(sst[:].rearrange("p i j -> p (i j)"), ins["wkvs"]).then_inc(sem("u_state"), 16)
            act.wait_ge(sem("u_xs"), 1)
            nc.scalar.activation(xs[0:HD, 12, 0:NS], xs[0:HD, 12, 0:NS], ACT.Tanh).then_inc(sem("u_tanh"), 1)
            nc.scalar.activation(ssg[:, 8], xs[:, 13, 0:NS], ACT.Sigmoid).then_inc(sem("u_sgl"), 1)
            act.wait_ge(sem("mm_ulora"), 3)
            for c in range(4):
                nc.scalar.activation(ssg[:, c], bank[2][:, c * NS:(c + 1) * NS], ACT.Sigmoid, bias=par1("w0", c))\
                    .then_inc(sem("u_sg"), 1)
            for c in range(4):
                nc.scalar.activation(ssg[:, 4 + c], bank[3][:, c * NS:(c + 1) * NS], ACT.Sigmoid, bias=par1("a0", c))\
                    .then_inc(sem("u_sg"), 1)
            nc.scalar.activation(s4[:, 6], bank[4][:, 0:4 * NS].rearrange("p (c t) -> p c t", c=4), ACT.Copy)\
                .then_inc(sem("u_gate"), 1)
            act.wait_ge(sem("u_kk"), 2)
            act.wait_ge(sem("mm_ukk"), 1)
            nc.scalar.activation(s4[:, 7], bank[5][:, 0:4 * NS].rearrange("p (c t) -> p c t", c=4), ACT.Sqrt)\
                .then_inc(sem("u_len"), 1)
            act.wait_ge(sem("u_sg"), 8)
            nc.scalar.activation(s4[:, 1], ssg[:, 0:4], ACT.Exp, scale=-DECAY).then_inc(sem("u_decay"), 1)
            for q in range(6):
                act.wait_ge(sem("mm_urow"), q + 1)
                nc.scalar.activation(svec[:, q], bank[2 + q][0:NS, :], ACT.Copy).then_inc(sem("u_row"), 1)
            act.wait_ge(sem("u_row"), 6)
            for half in range(2):
                for q in range(6):
                    act.dma_start(srow[half * HD:(half + 1) * HD, q],
                                  svec[:, q].rearrange("b (h j) -> b h j", j=HD)).then_inc(sem("u_spread"), 16)
            act.wait_ge(sem("u_step"), 9)
            act.dma_start(outs["wkvs"], sst[:].rearrange("p i j -> p (i j)")).then_inc(sem("wkvs_stored"), 16)
            for half in range(2):
                act.dma_start(sym[:].rearrange("b (h i) -> b h i", i=HD)[:, :, half * 32:(half + 1) * 32],
                              syo[half * HD:(half + 1) * HD]).then_inc(sem("u_ygathered"), 16)
            act.wait_ge(sem("mm_uy"), 1)
            nc.scalar.activation(s4[:, 8], bank[2][:, 0:4 * NS].rearrange("p (c t) -> p c t", c=4), ACT.Copy)\
                .then_inc(sem("u_y"), 1)
            act.wait_ge(sem("u_centred"), 2)
            act.wait_ge(sem("mm_uvar"), 1)
            nc.scalar.activation(s4[:, 10], bank[4][:, 0:4 * NS].rearrange("p (c t) -> p c t", c=4), ACT.Sqrt,
                                 bias=eps_gn, scale=1.0 / HD).then_inc(sem("u_dev"), 1)
            act.wait_ge(sem("u_out"), 1)
            act.dma_start(orwT[:, :, S:T], s4[:, 9]).then_inc(sem("uo_stored"), 16)
            act.wait_ge(sem("uo_stored"), 16)
            act.wait_ge(sem("wkvs_stored"), 16)

            qk_c = outs["qkT"].rearrange("(a g c p) t -> a g p c t", a=2, g=G, p=P)

            def load_group(g):
                if g == 2:
                    act.wait_ge(sem("qz_ready"), 16)
                    act.wait_ge(sem("mm_att"), 8)
                act.dma_start(qgs[g % 2][:], qk_c[0, g, :, :, 0:S]).then_inc(sem(f"qg_loaded{g}"), 16)
                act.dma_start(kgs[g % 2][:], qk_c[1, g, :, :, 0:S]).then_inc(sem(f"kv_loaded{g}"), 16)
                rows_, vg = outs["vtok"][0:S, g * 256:(g + 1) * 256], vgs[g % 2]
                if g == 0:
                    act.dma_start(vg[:], rows_.rearrange("(u p) c -> p u c", p=P)).then_inc(sem("kv_loaded0"), 16)
                elif g == 1:
                    for b in range(2):
                        act.dma_start(vg[:, b::2], rows_[512 * b:512 * (b + 1)].rearrange("(p r) c -> p r c", r=4))\
                            .then_inc(sem("kv_loaded1"), 16)
                else:
                    for rr in range(2):
                        act.dma_start(vg[rr * HD:(rr + 1) * HD],
                                      rows_.rearrange("(p u r) c -> r p u c", u=8, r=2)[rr])\
                            .then_inc(sem("kv_loaded2"), 16)

            def begin(g, i, s):
                u = 8 * g + 2 * i + s
                half = slice(0, 2) if has_previous(g, i, s) else slice(1, 2)
                act.wait_ge(sem("a_max"), u + 1)
                for h in range(H):
                    nc.scalar.activation(sc[:, s, h, half], sc[:, s, h, half], ACT.Exp, bias=ob[:, s, 256 + h:257 + h],
                                         accum_out=ob[:, s, 260 + h:261 + h]).then_inc(sem("a_exp"), 1)

            def finish(g, i, s):
                u = 8 * g + 2 * i + s
                act.wait_ge(sem("mm_pt"), u + 1)
                nc.scalar.activation(pt[:, s, 1], bank[4][:].rearrange("p (h t) -> p h t", h=H), ACT.Copy)\
                    .then_inc(sem("a_pt_cur"), 1)

            def store(g, i, s):
                u = 8 * g + 2 * i + s
                act.wait_ge(sem("a_out"), u + 1)
                row = ao[g]
                if g == 0:
                    act.dma_start(row[bass.ds((2 * i + s) * P, P)], ob[:, s]).then_inc(sem(f"ao_stored{s}"), 16)
                elif g == 1:
                    act.dma_start(row[0:S].rearrange("(b i r) c -> b r i c", b=2, r=4)[s, bass.ds(i, 1)], ob[:, s])\
                        .then_inc(sem(f"ao_stored{s}"), 16)
                else:
                    for rr in range(2):
                        act.dma_start(row[0:S].rearrange("(i r) c -> r i c", r=16)[bass.ds(4 * i + 2 * s + rr, 1)],
                                      ob[rr * HD:(rr + 1) * HD, s]).then_inc(sem(f"ao_stored{s}"), 16)

            load_group(0)
            load_group(1)
            for g in range(G):
                def pair(i, more):
                    finish(g, i, 0)
                    begin(g, i, 1)
                    store(g, i, 0)
                    finish(g, i, 1)
                    if more:
                        begin(g, i + 1, 0)
                    store(g, i, 1)

                begin(g, 0, 0)
                if g == 0:
                    pair(0, True)
                with act.Fori(1 if g == 0 else 0, 3) as i:
                    pair(i, True)
                pair(3, False)
                if g == 0:
                    load_group(2)
            act.wait_ge(sem("mm_att"), 24)
            act.wait_ge(sem("ao_stored0"), 16 * 16)
            act.wait_ge(sem("ao_stored1"), 16 * 16)
            act.dma_start(skc[:, 0:128].rearrange("p k j -> p (k j)"), ins["skc"]).then_inc(sem("z_loaded"), 16)
            act.dma_start(svc[:, 0:128].rearrange("p k j -> p (k j)"), ins["svc"]).then_inc(sem("z_loaded"), 16)
            q4 = outs["qkT"].rearrange("(a g h j) t -> a g t h j", a=2, g=G, j=HD)
            for g in range(G):
                rows_ = slice(32 * g, 32 * g + 32)
                act.dma_start(svc[rows_, 128], outs["vtok"][S:T, g * 256:(g + 1) * 256]
                              .rearrange("b (h j) -> b h j", j=HD)).then_inc(sem("z_loaded"), 16)
                for b in range(NS):
                    r4 = slice(32 * g + 4 * b, 32 * g + 4 * b + 4)
                    act.dma_start(sq[r4], q4[0, g, S + b], **slow).then_inc(sem("z_loaded"), 16)
                    act.dma_start(skc[r4, 128], q4[1, g, S + b], **slow).then_inc(sem("z_loaded"), 16)
            act.wait_ge(sem("z_loaded"), 16 * (2 + 3 * 17))
            for g in range(G):
                rows_ = slice(32 * g, 32 * g + 32)
                for kv, t in (("k", skc), ("v", svc)):
                    act.dma_start(outs[f"{kv}c{g}"][:, (127, 511, 512)[g]].rearrange("b (h j) -> b h j", j=HD),
                                  t[rows_, 128]).then_inc(sem("z_rows_stored"), 16)
            act.wait_ge(sem("z_max"), 1)
            nc.scalar.activation(ssc[:], ssc[:], ACT.Exp, bias=snm[:, 0:1], accum_out=snm[:, 1:2]).then_inc(sem("z_exp"), 1)
            act.wait_ge(sem("z_out"), 1)
            for g in range(G):
                rows_ = slice(32 * g, 32 * g + 32)
                act.dma_start(ao[g, S:T, 0:256].rearrange("b (h j) -> b h j", j=HD), sso[rows_])\
                    .then_inc(sem("z_stored"), 16)
                for c in range(2):
                    act.dma_start(ao[g, S:T, 256 + 4 * c:260 + 4 * c].unsqueeze(2), snm[rows_, c:c + 1], **slow)\
                        .then_inc(sem("z_stored"), 16)
            act.wait_ge(sem("z_rows_stored"), 16 * 6)
            act.wait_ge(sem("z_stored"), 16 * 9)
            for t in range(9):
                s, w = t % 2, P if t < 8 else NS
                if t >= 2:
                    act.wait_ge(sem("m_sum"), t - 1)
                act.dma_start(mo[0:w, s], ao[:, t * P:t * P + w].rearrange("g p c -> p g c")).then_inc(sem(f"mo_loaded{s}"), 16)
                if t:
                    merge_act = t - 1
                    act.wait_ge(sem("m_diff"), merge_act + 1)
                    ww = P
                    nc.scalar.activation(md[0:ww, 1 - s], md[0:ww, 1 - s], ACT.Exp, scale=-1.0).then_inc(sem("m_exp"), 1)
                    act.wait_ge(sem("mm_om"), merge_act + 1)
                    nc.scalar.activation(oah[:, :, merge_act * P:merge_act * P + ww],
                                         bank[2 + (1 - s)][:, 0:2 * P].rearrange("p (c t) -> p c t", c=2), ACT.Copy)\
                        .then_inc(sem("oa_hi"), 1)
            act.wait_ge(sem("m_diff"), 9)
            nc.scalar.activation(md[0:NS, 0], md[0:NS, 0], ACT.Exp, scale=-1.0).then_inc(sem("m_exp"), 1)
            act.wait_ge(sem("mm_om"), 9)
            nc.scalar.activation(oah[:, :, S:T], bank[2][:, 0:2 * NS].rearrange("p (c t) -> p c t", c=2), ACT.Copy)\
                .then_inc(sem("oa_hi"), 1)
            act.wait_ge(sem("oa_lo"), 9)
            for c in range(4):
                if c >= 2:
                    act.wait_ge(sem("or_lo"), c - 1)
                act.dma_start(stage[:, c % 2], orwT[:, c]).then_inc(sem("or_loaded"), 16)
                act.wait_ge(sem("or_loaded"), 16 * (c + 1))
                nc.scalar.activation(orh[:, c], stage[:, c % 2], ACT.Copy).then_inc(sem("or_hi"), 1)
            def gate(n):
                act.wait_ge(sem(f"gate_loaded{n % 2}"), 16 * (n // 2 + 1))
                nc.scalar.activation(stage[:, n % 2], stage[:, n % 2], ACT.Sigmoid).then_inc(sem("gate_ready"), 1)

            act.wait_ge(sem("or_lo"), 4)
            for n in range(2):
                act.dma_start(stage[:, n], gT_v[n]).then_inc(sem(f"gate_loaded{n}"), 16)
            gate(0)
            for n in range(1, N_GA):
                gate(n)
                if n + 1 < N_GA:
                    act.wait_ge(sem("gated"), 3 * n)
                    act.dma_start(stage[:, (n + 1) % 2], gT_v[n + 1]).then_inc(sem(f"gate_loaded{(n + 1) % 2}"), 16)
            for k in range(KD):
                act.wait_ge(sem("gated"), 48)
                nc.scalar.activation(ahi[:, k], ym[:, k], ACT.Copy).then_inc(sem("m_hi"), 1)
            for k in range(KD):
                if k >= 2:
                    act.wait_ge(sem("o_added"), 3 * (k - 1))
                else:
                    act.wait_ge(sem("m_lo"), KD)
                act.dma_start(stage[:, k % 2], xT_c[k]).then_inc(sem(f"res_loaded{k % 2}"), 16)
                if k:
                    act.wait_ge(sem("o_added"), 3 * k)
                    act.dma_start(x1T[k - 1], xraw[:, k - 1]).then_inc(sem("x1_stored"), 16)
                    if k >= 3:
                        act.wait_ge(sem("n_added"), KD + k - 2)
                    nc.scalar.activation(ntmp[:, (k - 1) % 2], xraw[:, k - 1], ACT.Square).then_inc(sem("n_squared"), 1)
            act.wait_ge(sem("o_added"), 3 * KD)
            act.dma_start(x1T[KD - 1], xraw[:, KD - 1]).then_inc(sem("x1_stored"), 16)
            act.wait_ge(sem("n_added"), 2 * KD - 2)
            nc.scalar.activation(ntmp[:, 1], xraw[:, KD - 1], ACT.Square).then_inc(sem("n_squared"), 1)
            for n in range(3):
                act.wait_ge(sem("n_summed"), 3 + n + 1)
                nc.scalar.activation(nrt[:, n * PC:(n + 1) * PC], bank[2 + n][:, 0:PC], ACT.Sqrt, bias=eps_rms,
                                     scale=1.0 / D).then_inc(sem("n_root"), 1)
            for k in range(KD):
                act.wait_ge(sem("n_scaled"), KD + k + 1)
                nc.scalar.activation(ahi[:, k], xraw[:, k], ACT.Copy).then_inc(sem("a_hi"), 1)
            act.wait_ge(sem("x1_stored"), 16 * KD)
            act.wait_ge(sem("a_split"), 2 * KD)
            act.dma_start(cst8[:].rearrange("p c a b -> p (c a b)"), ins["sconvT"]).then_inc(sem("hist_loaded"), 16)
            conv_v = outs["convo"]
            def up_pair(i):
                for s in range(2):
                    act.wait_ge(sem("u_conv"), 6 * i)
                    act.wait_ge(sem("rows_stored"), 32 * i)
                    for n in range(3):
                        q = 3 * s + n
                        act.wait_ge(sem("mm_piece"), P_UP + 6 * i + q + 1)
                        nc.scalar.activation(ug[:, s, 2 + n * PC:2 + (n + 1) * PC], bank[q % 2][:, 0:PC], ACT.Copy)\
                            .then_inc(sem(f"bank_free{q % 2}"), 1)
                act.wait_ge(sem("bank_free0"), P_UP // 2 + 3 * i + 3)
                act.wait_ge(sem("bank_free1"), P_UP // 2 + 3 * i + 3)
                for s in range(2):
                    act.dma_start(conv_v[2 * i + s], ug[:, s, S:2 + T]).then_inc(sem("rows_stored"), 16)
                act.wait_ge(sem("u_conv"), 6 * i + 3)
                nc.scalar.activation(cc[:, 0], cc[:, 0], ACT.Silu).then_inc(sem("u_silu"), 1)
                act.wait_ge(sem("h_ready"), i + 1)
                nc.scalar.activation(hhi[:, bass.ds(i, 1)], cc[:, 1:2], ACT.Copy).then_inc(sem("h_hi"), 1)
                act.wait_ge(sem("h_lo"), i + 1)
                act.dma_start(hloT[bass.ds(i, 1)], hlo_st[:, 0].bitcast(F32)).then_inc(sem("hlo_stored"), 16)

            peeled(act, KF, up_pair)
            act.wait_ge(sem("hlo_stored"), 16 * KF)
            act.wait_ge(sem("mm_piece"), P_DN)
            act.wait_ge(sem("rows_stored"), 32 * KF)
            for n, (a, b) in enumerate(HLO_PARTS):
                act.dma_start(hlo[:, a:b].bitcast(F32), hloT[a:b].rearrange("c p t -> p c t"))\
                    .then_inc(sem(f"hlo_loaded{n}"), 16)
            for n in range(3 * KD):
                if n >= 2:
                    act.wait_ge(sem("y_ready2"), n - 1)
                act.dma_start(yrs[:, n % 2], x1T[n // 3, :, (n % 3) * PC:(n % 3 + 1) * PC]).then_inc(sem(f"yres_loaded{n % 2}"), 16)
                if n:
                    act.wait_ge(sem("y_ready2"), n)
                    act.dma_start(yT_c[(n - 1) // 3, :, ((n - 1) % 3) * PC:((n - 1) % 3 + 1) * PC], yst[:, (n - 1) % 2])\
                        .then_inc(sem(f"y_stored{(n - 1) % 2}"), 16)
            act.wait_ge(sem("y_ready2"), 24)
            act.dma_start(yT_c[KD - 1, :, 2 * PC:3 * PC], yst[:, 1]).then_inc(sem("y_stored1"), 16)
            for s in range(2):
                act.wait_ge(sem(f"y_stored{s}"), 16 * 12)

        @block.vector
        def _(dve):
            dve.wait_ge(sem("par_loaded"), 16)
            nc.vector.memset(nsum[:], 0.0).then_inc(sem("n_zero"), 1)
            dve.wait_ge(sem("n_zero"), 1)
            for k in range(KD):
                dve.wait_ge(sem("n_squared"), k + 1)
                if k:
                    dve.wait_ge(sem("n_added"), k)
                nc.vector.tensor_tensor(nsum[:], nsum[:], ntmp[:, k % 2], ALU.add).then_inc(sem("n_added"), 1)
            for n in range(3):
                dve.wait_ge(sem("n_root"), n + 1)
                nc.vector.reciprocal(nrs[:, n * PC:(n + 1) * PC], nrt[:, n * PC:(n + 1) * PC])\
                    .then_inc(sem("n_rstd"), 1)
            dve.wait_ge(sem("n_rstd"), 3)
            for k in range(KD):
                nc.vector.scalar_tensor_tensor(xraw[:, k], xraw[:, k], par1("g1", k), nrs[:], ALU.mult, ALU.mult)\
                    .then_inc(sem("n_scaled"), 1)
            for k in range(KD):
                dve.wait_ge(sem("a_hi"), k + 1)
                dve.wait_ge(sem("n_scaled"), k + 1)
                nc.vector.tensor_tensor(alo[:, k], xraw[:, k], ahi[:, k].bitcast(F32), ALU.subtract)\
                    .then_inc(sem("a_split"), 1)
            with dve.Fori(0, N_QK // 2) as i:
                for q in range(6):
                    s, n = q // 3, q % 3
                    dve.wait_ge(sem("q_root"), 6 * i + q + 1)
                    nc.vector.reciprocal(qrt[:, q], qrt[:, q]).then_inc(sem("q_rstd"), 1)
                    dve.wait_ge(sem("q_rstd"), 6 * i + q + 1)
                    piece = stage[:, s, n * PC:(n + 1) * PC]
                    nc.vector.scalar_tensor_tensor(piece, piece, par1("qkg", 2 * i + s), qrt[:, q],
                                                   ALU.mult, ALU.mult).then_inc(sem("q_scaled"), 1)


            def wide(name, n=4, first=0):
                a = PAR[name][0] + first
                return par[:, a:a + n].unsqueeze(2).broadcast_to([P, n, P])

            def v4(t):
                return t.unsqueeze(2).broadcast_to([P, 4, P])

            TT_ = nc.vector.tensor_tensor
            dve.wait_ge(sem("q_scaled"), 3 * N_QK)
            dve.wait_ge(sem("stored0"), stored_before(B_GA, 0))
            dve.wait_ge(sem("stored1"), stored_before(B_GA, 0))
            dve.wait_ge(sem("v_stored0"), 32 * (N_V // 2))
            dve.wait_ge(sem("v_stored1"), 32 * (N_V // 2))
            nc.vector.memset(st[:], 0.0).then_inc(sem("s_zero"), 1)
            nc.vector.memset(sm[:], 0.0).then_inc(sem("s_zero"), 1)

            def rwkv(i):
                k = i + 1
                dve.wait_ge(sem("pin_loaded"), 16 * k)
                TT_(xs[:], pin[:, :, 0:P], pin[:, :, 1:1 + P], ALU.subtract).then_inc(sem("dve_tile"), 1)
                dve.wait_ge(sem("dve_tile"), step("x_diff", i))
                TT_(xs[:], xs[:], wide("mu", N_RW), ALU.mult).then_inc(sem("dve_tile"), 1)
                dve.wait_ge(sem("dve_tile"), step("x_mixed", i))
                TT_(xs[:], xs[:], pin[:, :, 1:1 + P], ALU.add).then_inc(sem("dve_tile"), 1)
                dve.wait_ge(sem("dve_tile"), step("xs_ready", i))
                r, kr, v = xs[:, 0:4], xs[:, 4:8], xs[:, 8:12]
                TT_(kkn[:], kr, wide("kk"), ALU.mult).then_inc(sem("dve_tile"), 1)
                dve.wait_ge(sem("act_tile"), step("kk_len", i))
                nc.vector.tensor_scalar(tmp[:], tmp[:], L2_EPS, None, ALU.max).then_inc(sem("dve_tile"), 1)
                dve.wait_ge(sem("dve_tile"), step("kk_clamped", i))
                nc.vector.reciprocal(tmp[:], tmp[:]).then_inc(sem("dve_tile"), 1)
                dve.wait_ge(sem("dve_tile"), step("kk_inv", i))
                TT_(kkn[:], kkn[:], tmp[:], ALU.mult).then_inc(sem("dve_tile"), 1)
                dve.wait_ge(sem("act_tile"), step("r_sgw", i))
                nc.vector.tensor_tensor_scan(cs[:].rearrange("p c t -> p (c t)"), C("scan", 0, 4 * P),
                                             sg[:, 0:4].rearrange("p c t -> p (c t)"), 0.0, ALU.mult, ALU.add)\
                    .then_inc(sem("dve_tile"), 1)
                dve.wait_ge(sem("dve_tile"), step("c_sum", i))
                nc.vector.tensor_copy(cm[:], cs[:, :, HD - 1]).then_inc(sem("dve_tile"), 1)
                dve.wait_ge(sem("dve_tile"), step("c_mid", i))
                TT_(cs[:], cs[:], v4(cm[:]), ALU.subtract).then_inc(sem("dve_tile"), 1)
                dve.wait_ge(sem("dve_tile"), step("c_ready", i))
                dve.wait_ge(sem("o_free"), 16 * i + 16)
                TT_(cp[:], cs[:], sg[:, 0:4], ALU.subtract).then_inc(sem("dve_tile"), 1)
                dve.wait_ge(sem("act_tile"), step("r_sga", i))
                dve.wait_ge(sem("dve_tile"), step("kk_ready", i))
                TT_(bt[:], kkn[:], sg[:, 4:8], ALU.mult).then_inc(sem("dve_tile"), 1)
                nc.vector.scalar_tensor_tensor(kt[:], sg[:, 4:8], 1.0, wide("ka"), ALU.subtract, ALU.mult)\
                    .then_inc(sem("dve_tile"), 1)
                dve.wait_ge(sem("dve_tile"), step("k_gain", i))
                nc.vector.scalar_tensor_tensor(kt[:], kt[:], 1.0, kr, ALU.add, ALU.mult).then_inc(sem("dve_tile"), 1)
                dve.wait_ge(sem("dve_tile"), step("k_ready", i))
                TT_(tmp[:], r, kt[:], ALU.mult).then_inc(sem("dve_tile"), 1)
                dve.wait_ge(sem("dve_tile"), step("rk_raw", i))
                TT_(tmp[:], tmp[:], wide("rk"), ALU.mult).then_inc(sem("dve_tile"), 1)
                dve.wait_ge(sem("act_tile"), step("e_wi", i))
                dve.wait_ge(sem("dve_tile"), step("b_raw", i))
                TT_(bt[:], bt[:], ewi[:], ALU.mult).then_inc(sem("dve_tile"), 1)
                TT_(kt[:], kt[:], ewi[:], ALU.mult).then_inc(sem("dve_tile"), 1)
                dve.wait_ge(sem("act_tile"), step("e_wp", i))
                nc.vector.scalar_tensor_tensor(ar[:, :, 0], kkn[:], -1.0, ewp[:], ALU.mult, ALU.mult)\
                    .then_inc(sem("dve_tile"), 1)
                TT_(ar[:, :, 1], r, ew[:], ALU.mult).then_inc(sem("dve_tile"), 1)
                nc.vector.tensor_copy(wend[:], ew[:, :, P - 1]).then_inc(sem("dve_tile"), 1)
                dve.wait_ge(sem("pe_tile"), step("mm_bonus", i))
                TT_(bon[:], bank[5][:].rearrange("p (c t) -> p c t", c=4), v, ALU.mult).then_inc(sem("dve_tile"), 1)
                dve.wait_ge(sem("act_tile"), step("e_wm", i))
                dve.wait_ge(sem("s_zero"), 2)
                for hh in range(2):
                    q = slice(hh * HD, (hh + 1) * HD)
                    last = TT_(sm[q, :, q], st[q, :, q], wm[q].unsqueeze(2).broadcast_to([HD, 4, HD]), ALU.mult)
                last.then_inc(sem("dve_tile"), 1)
                mask = cst[:, CST["su"][0]:CST["su"][0] + 2 * P].unsqueeze(1).broadcast_to([P, 2, 2 * P])
                for dst, name, banks in ((gq, "mm_gq", (4, 5, 6, 7)), (nq, "mm_nq", (2, 3, 4, 5))):
                    for n, b in enumerate(banks):
                        dve.wait_ge(sem(name), 4 * i + n + 1)
                        TT_(dst[:, 2 * n:2 * n + 2].rearrange("p h a t -> p h (a t)"),
                            bank[b][:].rearrange("p (h x) -> p h x", h=2), mask, ALU.mult)\
                            .then_inc(sem(name + "_out"), 1)
                for g in range(2):
                    hs = slice(4 * g, 4 * g + 4)
                    dve.wait_ge(sem("mm_nq_out"), 4 * i + 2 * g + 2)
                    TT_(tt[:, hs], nq[:, hs, 0], C("lv0t").unsqueeze(1).broadcast_to([P, 4, P]), ALU.mult)\
                        .then_inc(sem("tt_low"), 1)
                    dve.wait_ge(sem("tt_low"), 2 * i + g + 1)
                    TT_(tt[:, hs], tt[:, hs], C("ident").unsqueeze(1).broadcast_to([P, 4, P]), ALU.add)\
                        .then_inc(sem(f"tt_ready{g}"), 1)
                for g in range(2):
                    dve.wait_ge(sem(f"mm_t{g}"), 6 * i + 1)
                    nc.vector.tensor_copy(ti[:, 4 * g:4 * g + 4], bank[2 + g][:].rearrange("p (h t) -> p h t", h=4))\
                        .then_inc(sem(f"t_ready{g}"), 1)
                for lv in range(6):
                    for g in range(2):
                        hs = slice(4 * g, 4 * g + 4)
                        dve.wait_ge(sem(f"mm_x{g}"), 6 * i + lv + 1)
                        TT_(xx[:, hs], bank[4 + g][:].rearrange("p (h t) -> p h t", h=4),
                            C("lvl", lv * P).unsqueeze(1).broadcast_to([P, 4, P]), ALU.mult)\
                            .then_inc(sem(f"x_ready{g}"), 1)
                    for g in range(2):
                        hs = slice(4 * g, 4 * g + 4)
                        if lv < 5:
                            dve.wait_ge(sem(f"mm_t{g}"), 6 * i + lv + 2)
                            TT_(ti[:, hs], ti[:, hs], bank[2 + g][:].rearrange("p (h t) -> p h t", h=4), ALU.add)\
                                .then_inc(sem(f"t_ready{g}"), 1)
                        dve.wait_ge(sem(f"mm_tt{g}"), 6 * i + lv + 1)
                        TT_(tt[:, hs], tt[:, hs], bank[6 + g][:].rearrange("p (h t) -> p h t", h=4), ALU.add)\
                            .then_inc(sem(f"tt_ready{g}"), 1)
                dve.wait_ge(sem("pe_tile"), step("mm_s", i))
                dve.wait_ge(sem("dve_tile"), step("sm_ready", i))
                for hh in range(2):
                    q = slice(hh * HD, (hh + 1) * HD)
                    last = TT_(st[q, :, q], sm[q, :, q],
                               bank[6][q].rearrange("p (c t) -> p c t", c=4)[:, :, q], ALU.add)
                last.then_inc(sem("dve_tile"), 1)
                dve.wait_ge(sem("dve_tile"), step("s_sum", i))
                for hh in range(2):
                    q = slice(hh * HD, (hh + 1) * HD)
                    last = TT_(st[q, :, q], st[q, :, q], wend[q].unsqueeze(2).broadcast_to([HD, 4, HD]), ALU.mult)
                last.then_inc(sem("dve_tile"), 1)
                dve.wait_ge(sem("pe_tile"), step("mm_mean", i))
                nc.vector.scalar_tensor_tensor(cp[:], bank[2][:].rearrange("p (c t) -> p c t", c=4), -1.0 / HD, cs[:],
                                               ALU.mult, ALU.add).then_inc(sem("dve_tile"), 1)
                dve.wait_ge(sem("act_tile"), step("y_dev", i))
                nc.vector.reciprocal(ewi[:], ewi[:]).then_inc(sem("y_rstd"), 1)
                dve.wait_ge(sem("y_rstd"), k)
                TT_(cp[:], cp[:], ewi[:], ALU.mult).then_inc(sem("dve_tile"), 1)
                dve.wait_ge(sem("dve_tile"), step("y_normed", i))
                for c in range(4):
                    last = nc.vector.tensor_scalar(cp[:, c], cp[:, c], par1("gng", c), par1("gnb", c),
                                                   ALU.mult, ALU.add)
                last.then_inc(sem("dve_tile"), 1)
                dve.wait_ge(sem("dve_tile"), step("y_gained", i))
                TT_(cp[:], cp[:], bon[:], ALU.add).then_inc(sem("dve_tile"), 1)
                dve.wait_ge(sem("dve_tile"), step("y_bonus", i))
                TT_(cp[:], cp[:], gg[:], ALU.mult).then_inc(sem("dve_tile"), 1)

            with dve.Fori(0, NT) as i:
                rwkv(i)

            def wide8(name, n=4):
                a = PAR[name][0]
                return par[:, a:a + n].unsqueeze(2).broadcast_to([P, n, NS])

            linked = [0]

            def link(ins):
                linked[0] += 1
                ins.then_inc(sem("u_link"), 1)
                dve.wait_ge(sem("u_link"), linked[0])

            x8 = xs[:, :, 0:NS]
            dve.wait_ge(sem("u_loaded"), 32)
            link(TT_(x8, pin[:, :, 0:NS], pin[:, :, NS:2 * NS], ALU.subtract))
            link(TT_(x8, x8, wide8("mu", N_RW), ALU.mult))
            TT_(x8, x8, pin[:, :, NS:2 * NS], ALU.add).then_inc(sem("u_xs"), 1)
            dve.wait_ge(sem("u_xs"), 1)
            r8, k8, v8 = x8[:, 0:4], x8[:, 4:8], x8[:, 8:12]
            TT_(s4[:, 3], k8, wide8("kk"), ALU.mult).then_inc(sem("u_kk"), 1)
            dve.wait_ge(sem("u_kk"), 1)
            TT_(s4[:, 0], s4[:, 3], s4[:, 3], ALU.mult).then_inc(sem("u_kk"), 1)
            dve.wait_ge(sem("u_len"), 1)
            link(nc.vector.tensor_scalar(s4[:, 7], s4[:, 7], L2_EPS, None, ALU.max))
            link(nc.vector.reciprocal(s4[:, 7], s4[:, 7]))
            link(TT_(s4[:, 3], s4[:, 3], s4[:, 7], ALU.mult))
            dve.wait_ge(sem("u_sg"), 8)
            link(TT_(s4[:, 4], s4[:, 3], ssg[:, 4:8], ALU.mult))
            link(nc.vector.tensor_scalar(s4[:, 3], s4[:, 3], -1.0, None, ALU.mult))
            link(nc.vector.scalar_tensor_tensor(s4[:, 2], ssg[:, 4:8], 1.0, wide8("ka"), ALU.subtract, ALU.mult))
            link(nc.vector.scalar_tensor_tensor(s4[:, 2], s4[:, 2], 1.0, k8, ALU.add, ALU.mult))
            link(nc.vector.tensor_copy(s4[:, 0], r8))
            link(nc.vector.tensor_copy(s4[:, 5], v8))
            link(TT_(s4[:, 11], r8, s4[:, 2], ALU.mult))
            TT_(s4[:, 11], s4[:, 11], wide8("rk"), ALU.mult).then_inc(sem("u_vectors"), 1)
            dve.wait_ge(sem("u_spread"), 16 * 12)
            dve.wait_ge(sem("u_state"), 16)
            at_step = [0]

            def rec(ins):
                at_step[0] += 1
                ins.then_inc(sem("u_step"), 1)
                dve.wait_ge(sem("u_step"), at_step[0])

            def cols(q):
                return srow[:, q].unsqueeze(1).broadcast_to([P, 32, HD])

            rec(TT_(stp[:], sst[:], cols(3), ALU.mult))
            rec(nc.vector.tensor_reduce(ssa[:], stp[:], AX.X, ALU.add))
            rec(TT_(sst[:], sst[:], cols(1), ALU.mult))
            rec(TT_(stp[:], ssa[:].unsqueeze(2).broadcast_to([P, 32, HD]), cols(4), ALU.mult))
            rec(TT_(sst[:], sst[:], stp[:], ALU.add))
            for half in range(2):
                q = slice(half * HD, (half + 1) * HD)
                ins = TT_(stp[q], srow[q, 5, half * 32:(half + 1) * 32].unsqueeze(2).broadcast_to([HD, 32, HD]),
                          srow[q, 2].unsqueeze(1).broadcast_to([HD, 32, HD]), ALU.mult)
            rec(ins)
            rec(TT_(sst[:], sst[:], stp[:], ALU.add))
            rec(TT_(stp[:], sst[:], cols(0), ALU.mult))
            rec(nc.vector.tensor_reduce(syo[:], stp[:], AX.X, ALU.add))
            dve.wait_ge(sem("u_y"), 1)
            dve.wait_ge(sem("mm_umean"), 1)
            c4 = lambda b: bank[b][:, 0:4 * NS].rearrange("p (c t) -> p c t", c=4)
            nc.vector.scalar_tensor_tensor(s4[:, 9], c4(3), -1.0 / HD, s4[:, 8], ALU.mult, ALU.add)\
                .then_inc(sem("u_centred"), 1)
            dve.wait_ge(sem("u_centred"), 1)
            TT_(s4[:, 0], s4[:, 9], s4[:, 9], ALU.mult).then_inc(sem("u_centred"), 1)
            dve.wait_ge(sem("u_dev"), 1)
            link(nc.vector.reciprocal(s4[:, 10], s4[:, 10]))
            link(TT_(s4[:, 9], s4[:, 9], s4[:, 10], ALU.mult))
            link(TT_(s4[:, 9], s4[:, 9], wide8("gng"), ALU.mult))
            link(TT_(s4[:, 9], s4[:, 9], wide8("gnb"), ALU.add))
            dve.wait_ge(sem("mm_ubonus"), 1)
            link(TT_(s4[:, 11], c4(5), v8, ALU.mult))
            link(TT_(s4[:, 9], s4[:, 9], s4[:, 11], ALU.add))
            TT_(s4[:, 9], s4[:, 9], s4[:, 6], ALU.mult).then_inc(sem("u_out"), 1)
            dve.wait_ge(sem("uo_stored"), 16)
            dve.wait_ge(sem("wkvs_stored"), 16)

            nc.vector.memset(qz[:], 0.0).then_inc(sem("qz_zero"), 1)

            def begin(g, i, s):
                u, prev = 8 * g + 2 * i + s, has_previous(g, i, s)
                half = slice(0, 2) if prev else slice(1, 2)
                dve.wait_ge(sem("mm_score"), u + 1)
                if not (isinstance(u, int) and u < 2):
                    dve.wait_ge(sem("mm_pt"), u - 1)
                m = "cur2" if g == 2 else "cur"
                nc.vector.scalar_tensor_tensor(
                    sc[:, s, :, 1], bank[2][:].rearrange("p (h t) -> p h t", h=H), HD ** -0.5,
                    C(m).unsqueeze(1).broadcast_to([P, H, P]), ALU.mult, ALU.add).then_inc(sem("a_masked"), 1)
                if prev:
                    nc.vector.scalar_tensor_tensor(
                        sc[:, s, :, 0], bank[3][:].rearrange("p (h t) -> p h t", h=H), HD ** -0.5,
                        C("prev").unsqueeze(1).broadcast_to([P, H, P]), ALU.mult, ALU.add).then_inc(sem("a_masked"), 1)
                else:
                    dve.sem_inc(sem("a_masked"), 1)
                dve.wait_ge(sem("a_masked"), 2 * u + 2)
                dve.wait_ge(sem(f"ao_stored{s}"), 16 * (4 * g + (i if g < 2 else 2 * i)))
                nc.vector.tensor_reduce(ob[:, s, 256:260], sc[:, s, :, half], AX.XY, ALU.max, negate=True)\
                    .then_inc(sem("a_max"), 1)

            def finish(g, i, s):
                u = 8 * g + 2 * i + s
                if has_previous(g, i, s):
                    dve.wait_ge(sem("mm_pt"), u + 1)
                    nc.vector.tensor_copy(pt[:, s, 0], bank[5][:].rearrange("p (h t) -> p h t", h=H))\
                        .then_inc(sem("a_pt_prev"), 1)
                else:
                    dve.sem_inc(sem("a_pt_prev"), 1)
                dve.wait_ge(sem("mm_att"), u + 1)
                nc.vector.tensor_copy(ob[:, s, 0:256], bank[6][:, 0:256]).then_inc(sem("a_out"), 1)

            for g in range(G):
                units(dve, g, begin, finish)
            dve.wait_ge(sem("z_loaded"), 16 * (2 + 3 * 17))
            link(nc.vector.tensor_scalar(sq[:], sq[:], HD ** -0.5, None, ALU.mult))
            dve.wait_ge(sem("z_rows_stored"), 16 * 6)
            link(TT_(skc[:], skc[:], sq[:].unsqueeze(1).broadcast_to([96, 129, HD]), ALU.mult))
            link(nc.vector.tensor_reduce(ssc[:], skc[:], AX.X, ALU.add))
            link(nc.vector.memset(ssc[64:96, 32:128], NEG))
            nc.vector.tensor_reduce(snm[:, 0:1], ssc[:], AX.X, ALU.max, negate=True).then_inc(sem("z_max"), 1)
            dve.wait_ge(sem("z_exp"), 1)
            link(TT_(svc[:], svc[:], ssc[:].unsqueeze(2).broadcast_to([96, 129, HD]), ALU.mult))
            nc.vector.tensor_reduce(sso[:], svc[:].rearrange("p k j -> p j k"), AX.X, ALU.add).then_inc(sem("z_out"), 1)
            for t in range(9):
                s, w = t % 2, P if t < 8 else NS
                dve.wait_ge(sem(f"mo_loaded{s}"), 16 * (t // 2 + 1))
                nm, den = mo[0:w, s, :, 256:260], mo[0:w, s, :, 260:264]
                link(nc.vector.tensor_reduce(mn[0:w, s, 0:H], nm.rearrange("p g h -> p h g"), AX.X, ALU.min))
                TT_(md[0:w, s], nm, mn[0:w, s, 0:H].unsqueeze(1).broadcast_to([w, G, H]), ALU.subtract)\
                    .then_inc(sem("m_diff"), 1)
                dve.wait_ge(sem("m_exp"), t + 1)
                link(TT_(den, den, md[0:w, s], ALU.mult))
                link(nc.vector.tensor_reduce(mn[0:w, s, 0:H], den.rearrange("p g h -> p h g"), AX.X, ALU.add))
                link(nc.vector.reciprocal(mn[0:w, s, H:2 * H], mn[0:w, s, 0:H]))
                link(TT_(md[0:w, s], md[0:w, s], mn[0:w, s, H:2 * H].unsqueeze(1).broadcast_to([w, G, H]), ALU.mult))
                o = mo[0:w, s, :, 0:256].rearrange("p g (h j) -> p g h j", h=H)
                link(TT_(o, o, md[0:w, s].unsqueeze(3).broadcast_to([w, G, H, HD]), ALU.mult))
                if t >= 2:
                    dve.wait_ge(sem("mm_om"), t - 1)
                link(TT_(om[0:w, s], mo[0:w, s, 0, 0:256], mo[0:w, s, 1, 0:256], ALU.add))
                TT_(om[0:w, s], om[0:w, s], mo[0:w, s, 2, 0:256], ALU.add).then_inc(sem("m_sum"), 1)
                dve.wait_ge(sem("oa_hi"), t + 1)
                TT_(oal[:, :, t * P:t * P + w], bank[2 + s][:, 0:2 * w].rearrange("p (c t) -> p c t", c=2),
                    oah[:, :, t * P:t * P + w].bitcast(F32), ALU.subtract).then_inc(sem("oa_lo"), 1)
            for c in range(4):
                dve.wait_ge(sem("or_hi"), c + 1)
                TT_(orl[:, c], stage[:, c % 2], orh[:, c].bitcast(F32), ALU.subtract).then_inc(sem("or_lo"), 1)
            for n in range(16):
                k, s = n % 8, n % 2
                dve.wait_ge(sem("gate_ready"), n + 1)
                for c in range(3):
                    q = 3 * n + c
                    dve.wait_ge(sem("mm_piece"), P_AO + q + 1)
                    piece = ym[:, k, c * PC:(c + 1) * PC]
                    gate = stage[:, s, c * PC:(c + 1) * PC]
                    if n < 8:
                        TT_(piece, bank[q % 2][:, 0:PC], gate, ALU.mult).then_inc(sem("gated"), 1)
                        dve.wait_ge(sem("gated"), q + 1)
                        dve.sem_inc(sem(f"bank_free{q % 2}"), 1)
                    else:
                        TT_(gate, bank[q % 2][:, 0:PC], gate, ALU.mult).then_inc(sem(f"bank_free{q % 2}"), 1)
                        dve.wait_ge(sem(f"bank_free{q % 2}"), (P_AO + q) // 2 + 1)
                        TT_(piece, piece, gate, ALU.add).then_inc(sem("gated"), 1)
            for k in range(KD):
                dve.wait_ge(sem("m_hi"), k + 1)
                TT_(alo[:, k], ym[:, k], ahi[:, k].bitcast(F32), ALU.subtract).then_inc(sem("m_lo"), 1)
            dve.wait_ge(sem("m_lo"), KD)
            nc.vector.memset(nsum[:], 0.0).then_inc(sem("n_zero"), 1)
            for k in range(KD):
                dve.wait_ge(sem(f"res_loaded{k % 2}"), 16 * (k // 2 + 1))
                for c in range(3):
                    q = 3 * k + c
                    dve.wait_ge(sem("mm_piece"), P_WO + q + 1)
                    TT_(xraw[:, k, c * PC:(c + 1) * PC], bank[q % 2][:, 0:PC], stage[:, k % 2, c * PC:(c + 1) * PC],
                        ALU.add).then_inc(sem("o_added"), 1)
                    dve.wait_ge(sem("o_added"), q + 1)
                    dve.sem_inc(sem(f"bank_free{q % 2}"), 1)
                if k:
                    dve.wait_ge(sem("n_squared"), KD + k)
                    dve.wait_ge(sem("n_zero"), 2)
                    if k > 1:
                        dve.wait_ge(sem("n_added"), KD + k - 1)
                    TT_(nsum[:], nsum[:], ntmp[:, (k - 1) % 2], ALU.add).then_inc(sem("n_added"), 1)
            dve.wait_ge(sem("n_squared"), 2 * KD)
            dve.wait_ge(sem("n_added"), 2 * KD - 1)
            TT_(nsum[:], nsum[:], ntmp[:, 1], ALU.add).then_inc(sem("n_added"), 1)
            dve.wait_ge(sem("bank_free0"), P_UP // 2)
            dve.wait_ge(sem("bank_free1"), P_UP // 2)
            for n in range(3):
                dve.wait_ge(sem("n_root"), 3 + n + 1)
                nc.vector.reciprocal(nrs[:, n * PC:(n + 1) * PC], nrt[:, n * PC:(n + 1) * PC])\
                    .then_inc(sem("n_rstd"), 1)
            dve.wait_ge(sem("n_rstd"), 6)
            dve.wait_ge(sem("x1_stored"), 16 * KD)
            for k in range(KD):
                nc.vector.scalar_tensor_tensor(xraw[:, k], xraw[:, k], par1("g2", k), nrs[:], ALU.mult, ALU.mult)\
                    .then_inc(sem("n_scaled"), 1)
            for k in range(KD):
                dve.wait_ge(sem("a_hi"), KD + k + 1)
                dve.wait_ge(sem("n_scaled"), KD + k + 1)
                TT_(alo[:, k], xraw[:, k], ahi[:, k].bitcast(F32), ALU.subtract).then_inc(sem("a_split"), 1)
            dve.wait_ge(sem("a_split"), 2 * KD)
            nc.vector.memset(ug[:, :, 0:2], 0.0).then_inc(sem("hist_zero"), 1)
            dve.wait_ge(sem("hist_zero"), 1)
            dve.wait_ge(sem("hist_loaded"), 16)
            def up_pair(i):
                for s in range(2):
                    if s == 0:
                        dve.wait_ge(sem("bank_free0"), P_UP // 2 + 3 * i + 2)
                        dve.wait_ge(sem("bank_free1"), P_UP // 2 + 3 * i + 1)
                        dve.wait_ge(sem("h_hi"), i)
                    else:
                        dve.wait_ge(sem("bank_free0"), P_UP // 2 + 3 * i + 3)
                        dve.wait_ge(sem("bank_free1"), P_UP // 2 + 3 * i + 3)
                    w = [par1(f"cw{n}", 2 * i + s) for n in range(3)]
                    hist = cst8[:, bass.ds(2 * i + s, 1)].rearrange("p o a b -> p (o a) b")
                    c, u8 = cc[:, s], ug[:, s, 2 + S:2 + T]
                    nc.vector.tensor_scalar(c, ug[:, s, 2:2 + T], w[2], par1("cb", 2 * i + s), ALU.mult, ALU.add)\
                        .then_inc(sem("u_conv"), 1)
                    dve.wait_ge(sem("u_conv"), 6 * i + 3 * s + 1)
                    nc.vector.scalar_tensor_tensor(c[:, 0:S], ug[:, s, 1:1 + S], w[1], c[:, 0:S], ALU.mult, ALU.add)\
                        .then_inc(sem("u_tap"), 1)
                    nc.vector.scalar_tensor_tensor(c[:, S:T], hist[:, 1], w[1], c[:, S:T], ALU.mult, ALU.add)\
                        .then_inc(sem("u_conv"), 1)
                    dve.wait_ge(sem("u_tap"), 2 * i + s + 1)
                    dve.wait_ge(sem("u_conv"), 6 * i + 3 * s + 2)
                    nc.vector.scalar_tensor_tensor(c[:, 0:S], ug[:, s, 0:S], w[0], c[:, 0:S], ALU.mult, ALU.add)\
                        .then_inc(sem("u_tap2"), 1)
                    dve.wait_ge(sem("u_tap2"), 2 * i + s + 1)
                    nc.vector.scalar_tensor_tensor(c[:, S:T], hist[:, 0], w[0], c[:, S:T], ALU.mult, ALU.add)\
                        .then_inc(sem("u_conv"), 1)
                dve.wait_ge(sem("u_conv"), 6 * i + 6)
                dve.wait_ge(sem("u_silu"), i + 1)
                TT_(cc[:, 1], cc[:, 0], cc[:, 1], ALU.mult).then_inc(sem("h_ready"), 1)
                dve.wait_ge(sem("h_hi"), i + 1)
                dve.wait_ge(sem("hlo_stored"), 16 * i)
                TT_(hlo_st[:], cc[:, 1:2], hhi[:, bass.ds(i, 1)].bitcast(F32), ALU.subtract).then_inc(sem("h_lo"), 1)

            peeled(dve, KF, up_pair)
            for n in range(3 * KD):
                o = n // 3
                dve.wait_ge(sem(f"yres_loaded{n % 2}"), 16 * (n // 2 + 1))
                if n >= 2:
                    dve.wait_ge(sem(f"y_stored{n % 2}"), 16 * (n // 2))
                dve.wait_ge(sem("mm_down"), 3 * o + 3)
                TT_(yst[:, n % 2], bank[3 * (o % 2) + n % 3][:, 0:PC], yrs[:, n % 2], ALU.add)\
                    .then_inc(sem("y_ready2"), 1)

        @block.tensor
        def _(pe):
            pe.wait_ge(sem("cst_loaded"), 16)
            pe.wait_ge(sem("n_added"), KD)
            for n in range(3):
                pe.matmul(bank[n][:, 0:PC], C("mones"), nsum[:, n * PC:(n + 1) * PC], start=True, stop=True)\
                    .then_inc(sem("n_summed"), 1)
            pe.wait_ge(sem("a_split"), KD)
            pe.wait_ge(sem("n_root"), 3)

            parts = ((0, 0), (0, 1), (1, 0))
            wpart, apart = (whi, wlo), (ahi, alo)

            def rows_piece(s, n, out):
                for k in range(KD):
                    for a, b in parts:
                        last = pe.matmul(out[:, 0:PC], wpart[a][:, s, k], apart[b][:, k, n * PC:(n + 1) * PC],
                                         start=(k == 0 and (a, b) == (0, 0)), stop=(k == KD - 1 and a == 1))
                last.then_inc(sem("mm_piece"), 1)

            def rows(base, pbase, count):
                def pair(i):
                    for s in range(2):
                        pe.wait_ge(sem("w_split"), base + 2 * i + s + 1)
                        for n in range(3):
                            q = 3 * s + n
                            pe.wait_ge(sem(f"bank_free{q % 2}"), pbase // 2 + 3 * i + q // 2)
                            rows_piece(s, n, bank[q % 2])

                (looped if base else peeled)(pe, count // 2, pair)

            rows(B_RW, 0, N_RW)

            def head_sums(i, q):
                pe.wait_ge(sem("q_squared"), 6 * i + q + 1)
                pe.matmul(bank[2 + q % 2][:, 0:PC], C("bd"), qsq[:, q % 2], start=True, stop=True)\
                    .then_inc(sem("q_summed"), 1)

            with pe.Fori(0, N_QK // 2) as i:
                for s in range(2):
                    pe.wait_ge(sem("w_split"), B_QK + 2 * i + s + 1)
                    for n in range(3):
                        q = 3 * s + n
                        pe.wait_ge(sem(f"bank_free{q % 2}"), 3 * B_QK // 2 + 3 * i + q // 2)
                        rows_piece(s, n, bank[q % 2])
                        if q:
                            head_sums(i, q - 1)
                head_sums(i, 5)
            with pe.Fori(0, N_V // 2) as i:
                for s in range(2):
                    pe.wait_ge(sem("w_split"), B_V + 2 * i + s + 1)
                    for n in range(3):
                        q = 3 * s + n
                        pe.wait_ge(sem(f"bank_free{q % 2}"), 3 * B_V // 2 + 3 * i + q // 2)
                        for t in range(4) if n < 2 else (0,):
                            a0, w = 512 * n + P * t, P if n < 2 else NS
                            for k in range(KD):
                                for a, b in parts:
                                    last = pe.matmul(bank[q % 2][0:w, t * P:(t + 1) * P], apart[b][:, k, a0:a0 + w],
                                                     wpart[a][:, s, k], start=(k == 0 and (a, b) == (0, 0)),
                                                     stop=(k == KD - 1 and a == 1))
                        last.then_inc(sem("mm_piece"), 1)


            def slot(h):
                return 4 * (h // 4) + 2 * (h % 2) + (h // 2) % 2

            def gates(i, q):
                s = q // 3
                if q % 3 == 0:
                    pe.wait_ge(sem("w_split"), B_GA + 2 * i + s + 1)
                pe.wait_ge(sem(f"bank_free{q % 2}"), 3 * B_GA // 2 + 3 * i + q // 2)
                rows_piece(s, q % 3, bank[q % 2])

            def rwkv(i):
                f = slice(0, HD), slice(HD, P)
                gates(i, 0)
                gates(i, 1)
                pe.wait_ge(sem("act_tile"), step("r_tanh", i))
                for c in range(4):
                    last = pe.matmul(bank[2][:, c * P:(c + 1) * P], lora[f[0], 0, c * P:(c + 1) * P], xs[f[0], 12],
                                     start=True, stop=True)
                last.then_inc(sem("mm_lora"), 1)
                for c in range(4):
                    last = pe.matmul(bank[3][:, c * P:(c + 1) * P], lora[f[1], 0, c * P:(c + 1) * P], xs[f[1], 12],
                                     start=True, stop=True)
                last.then_inc(sem("mm_lora"), 1)
                pe.wait_ge(sem("act_tile"), step("r_sgl", i))
                for c in range(4):
                    last = pe.matmul(bank[4][:, c * P:(c + 1) * P], lora[:, 1, c * P:(c + 1) * P], sg[:, 8],
                                     start=True, stop=True)
                last.then_inc(sem("mm_lora"), 1)
                pe.wait_ge(sem("act_tile"), step("kk_squared", i))
                pe.matmul(bank[5][:], C("bd"), tmp[:].rearrange("p c t -> p (c t)"), start=True, stop=True)\
                    .then_inc(sem("pe_tile"), 1)
                for c in range(4):
                    last = pe.transpose(bank[6][:, c * P:(c + 1) * P], xs[:, 8 + c], C("ident"))
                last.then_inc(sem("mm_turn"), 1)
                gates(i, 2)
                pe.wait_ge(sem("act_tile"), step("kk_len", i))
                pe.wait_ge(sem("dve_tile"), step("rk_ready", i))
                pe.matmul(bank[5][:], C("bd"), tmp[:].rearrange("p c t -> p (c t)"), start=True, stop=True)\
                    .then_inc(sem("pe_tile"), 1)
                gates(i, 3)
                pe.wait_ge(sem("dve_tile"), step("at_ready", i))
                for c in range(4):
                    last = pe.transpose(bank[7][:, c * P:(c + 1) * P], ar[:, c, 0], C("ident"))
                last.then_inc(sem("mm_turn"), 1)
                pe.wait_ge(sem("act_tile"), step("r_sga", i))
                for c in range(4):
                    last = pe.transpose(bank[2][:, c * P:(c + 1) * P], bt[:, c], C("ident"))
                last.then_inc(sem("mm_turn"), 1)
                for c in range(4):
                    last = pe.transpose(bank[3][:, c * P:(c + 1) * P], kt[:, c], C("ident"))
                last.then_inc(sem("mm_turn"), 1)
                pe.wait_ge(sem("dve_tile"), step("rt_ready", i))
                pe.wait_ge(sem("act_tile"), step("r_gate", i))
                for src, name, banks in ((kt, "mm_gq", (4, 5, 6, 7)), (bt, "mm_nq", (2, 3, 4, 5))):
                    for n in range(2):
                        if name == "mm_gq":
                            pe.wait_ge(*((sem("dve_tile"), step("rk_summed", i)) if n == 0 else (sem("turned"), 4 * i + 2)))
                        else:
                            pe.wait_ge(sem("turned" if n == 0 else "mm_gq_out"), 4 * i + (4 if n == 0 else 2))
                        for h in (4 * n, 4 * n + 1, 4 * n + 2, 4 * n + 3):
                            b = banks[2 * n + h % 2]
                            c = (h // 2) % 2
                            last = pe.matmul(bank[b][:, 2 * P * c:2 * P * (c + 1)], src[f[h % 2], h // 2],
                                             ar[f[h % 2], h // 2].rearrange("p a t -> p (a t)"),
                                             start=True, stop=True)
                            if c:
                                last.then_inc(sem(name), 1)
                for g in range(2):
                    pe.wait_ge(sem(f"tt_ready{g}"), 7 * i + 1)
                    for h in range(4):
                        last = pe.transpose(bank[2 + g][:, h * P:(h + 1) * P], tt[:, 4 * g + h], C("ident"))
                    last.then_inc(sem(f"mm_t{g}"), 1)
                for lv in range(6):
                    for g in range(2):
                        pe.wait_ge(sem(f"t_ready{g}"), 6 * i + lv + 1)
                        if lv == 0:
                            pe.wait_ge(sem("mm_nq_out"), 4 * i + 4)
                        for h in range(4):
                            last = pe.matmul(bank[4 + g][:, h * P:(h + 1) * P], nq[:, 4 * g + h, 0], ti[:, 4 * g + h],
                                             start=True, stop=True)
                        last.then_inc(sem(f"mm_x{g}"), 1)
                    for g in range(2):
                        pe.wait_ge(sem(f"x_ready{g}"), 6 * i + lv + 1)
                        pe.wait_ge(sem(f"tt_ready{g}"), 7 * i + lv + 1)
                        if lv < 5:
                            for h in range(4):
                                last = pe.matmul(bank[2 + g][:, h * P:(h + 1) * P], tt[:, 4 * g + h], xx[:, 4 * g + h],
                                                 start=True, stop=True)
                            last.then_inc(sem(f"mm_t{g}"), 1)
                        for h in range(4):
                            last = pe.matmul(bank[6 + g][:, h * P:(h + 1) * P], xx[:, 4 * g + h], tt[:, 4 * g + h],
                                             start=True, stop=True)
                        last.then_inc(sem(f"mm_tt{g}"), 1)
                for g in range(2):
                    pe.wait_ge(sem(f"tt_ready{g}"), 7 * i + 7)
                for h in range(RH):
                    last = pe.matmul(bank[2][f[h % 2], (h // 2) * P:(h // 2 + 1) * P], atm[:, h * HD:(h + 1) * HD],
                                     tt[:, slot(h)], start=True, stop=True)
                last.then_inc(sem("pe_tile"), 1)
                for h in range(RH):
                    last = pe.matmul(bank[3][:, h * HD:(h + 1) * HD], gq[:, slot(h), 0], vtm[:, h * HD:(h + 1) * HD],
                                     start=True, stop=True)
                last.then_inc(sem("pe_tile"), 1)
                pe.wait_ge(sem("act_tile"), step("gv_ready", i))
                for h in range(RH):
                    pe.matmul(bank[4][:, h * HD:(h + 1) * HD], tt[:, slot(h)], gv[:, h * HD:(h + 1) * HD],
                              start=(h == 0), stop=False, skip_group_check=True)
                pe.wait_ge(sem("act_tile"), step("p1_ready", i))
                pe.wait_ge(sem("dve_tile"), step("sm_ready", i))
                for c in range(4):
                    last = pe.matmul(bank[4][:, c * P:(c + 1) * P], p1[:, c], sm[:, c], start=False, stop=(c == 3),
                                     skip_group_check=True)
                last.then_inc(sem("pe_tile"), 1)
                for c in range(4):
                    pe.matmul(bank[5][:, c * P:(c + 1) * P], sm[:, c], ar[:, c, 1], start=(c == 0), stop=False,
                              skip_group_check=True)
                for h in range(RH):
                    pe.matmul(bank[5][f[h % 2], (h // 2) * P:(h // 2 + 1) * P], vtm[:, h * HD:(h + 1) * HD],
                              gq[:, slot(h), 1], start=False, stop=False, skip_group_check=True)
                for c in range(4):
                    pe.matmul(bank[6][:, c * P:(c + 1) * P], ktm[:, c * P:(c + 1) * P], vtm[:, c * P:(c + 1) * P],
                              start=(c == 0), stop=False, skip_group_check=True)
                pe.wait_ge(sem("act_tile"), step("u_ready", i))
                for c in range(4):
                    last = pe.matmul(bank[6][:, c * P:(c + 1) * P], btm[:, c * P:(c + 1) * P],
                                     uu[:, c * P:(c + 1) * P], start=False, stop=(c == 3), skip_group_check=True)
                last.then_inc(sem("pe_tile"), 1)
                for h in range(RH):
                    last = pe.matmul(bank[5][f[h % 2], (h // 2) * P:(h // 2 + 1) * P], uu[:, h * HD:(h + 1) * HD],
                                     nq[:, slot(h), 1], start=False, stop=(h == RH - 1), skip_group_check=True)
                last.then_inc(sem("pe_tile"), 1)
                pe.wait_ge(sem("act_tile"), step("y_ready", i))
                pe.matmul(bank[2][:], C("bd"), cs[:].rearrange("p c t -> p (c t)"), start=True, stop=True)\
                    .then_inc(sem("pe_tile"), 1)
                pe.wait_ge(sem("act_tile"), step("y_squared", i))
                pe.matmul(bank[3][:], C("bd"), ew[:].rearrange("p c t -> p (c t)"), start=True, stop=True)\
                    .then_inc(sem("pe_tile"), 1)
                gates(i, 4)
                gates(i, 5)

            with pe.Fori(0, NT) as i:
                rwkv(i)
            pe.wait_ge(sem("u_tanh"), 1)
            pe.wait_ge(sem("u_sgl"), 1)
            pe.wait_ge(sem("act_tile"), step("y_dev", NT - 1))
            f = slice(0, HD), slice(HD, P)
            for n, (w, rhs) in enumerate(((lora[f[0], 0], xs[f[0], 12, 0:NS]), (lora[f[1], 0], xs[f[1], 12, 0:NS]),
                                          (lora[:, 1], ssg[:, 8]))):
                for c in range(4):
                    last = pe.matmul(bank[2 + n][:, c * NS:(c + 1) * NS], w[:, c * P:(c + 1) * P], rhs,
                                     start=True, stop=True)
                last.then_inc(sem("mm_ulora"), 1)
            pe.wait_ge(sem("u_kk"), 2)
            flat = lambda q: s4[:, q].rearrange("p c t -> p (c t)")
            pe.matmul(bank[5][:, 0:4 * NS], C("bd"), flat(0), start=True, stop=True).then_inc(sem("mm_ukk"), 1)
            pe.wait_ge(sem("u_vectors"), 1)
            pe.wait_ge(sem("u_decay"), 1)
            for q in range(6):
                for c in range(4):
                    last = pe.transpose(bank[2 + q][0:NS, c * P:(c + 1) * P], s4[:, q, c], C("ident"))
                last.then_inc(sem("mm_urow"), 1)
            pe.wait_ge(sem("u_row"), 6)
            pe.matmul(bank[5][:, 0:4 * NS], C("bd"), flat(11), start=True, stop=True).then_inc(sem("mm_ubonus"), 1)
            pe.wait_ge(sem("u_ygathered"), 32)
            for c in range(4):
                last = pe.transpose(bank[2][:, c * NS:(c + 1) * NS], sym[:, c * P:(c + 1) * P], C("ident")[0:NS, 0:NS])
            last.then_inc(sem("mm_uy"), 1)
            pe.wait_ge(sem("u_y"), 1)
            pe.matmul(bank[3][:, 0:4 * NS], C("bd"), flat(8), start=True, stop=True).then_inc(sem("mm_umean"), 1)
            pe.wait_ge(sem("u_centred"), 2)
            pe.matmul(bank[4][:, 0:4 * NS], C("bd"), flat(0), start=True, stop=True).then_inc(sem("mm_uvar"), 1)

            def begin(g, i, s):
                u, prev, kg = 8 * g + 2 * i + s, has_previous(g, i, s), kgs[g % 2]
                pe.wait_ge(sem("a_masked"), 2 * u)
                pe.wait_ge(sem("qz_ready"), 2 * u + 2)

                def keys(c, back):
                    if g == 0:
                        return kg[:, c, bass.ds((2 * i + s - back) * P, P)]
                    if g == 1:
                        return kg[:, c].rearrange("p (b i r) -> p b r i", b=2, r=4)[:, s - back, bass.ds(i, 1)]
                    return kg[:, c].rearrange("p (i r) -> p r i", r=16)[:, bass.ds(4 * i + 2 * s, 2)]

                shape = ("p (r i) -> p r i", 2) if g == 2 else ("p (r i) -> p r i", 1)
                for back in (1, 0) if prev else (0,):
                    for h in range(H):
                        out = bank[2 + back][:, h * P:(h + 1) * P]
                        if g:
                            out = out.rearrange(shape[0], r=shape[1])
                        last = pe.matmul(out, qz[:, s, h], keys(h // 2, back), start=True, stop=True)
                last.then_inc(sem("mm_score"), 1)

            def finish(g, i, s):
                u, prev, vg = 8 * g + 2 * i + s, has_previous(g, i, s), vgs[g % 2]
                pe.wait_ge(sem("a_exp"), 4 * u + 4)
                for back in (1, 0) if prev else (0,):
                    for h in range(H):
                        last = pe.transpose(bank[4 + back][:, h * P:(h + 1) * P], sc[:, s, h, 1 - back], C("ident"))
                last.then_inc(sem("mm_pt"), 1)
                pe.wait_ge(sem("a_pt_cur"), u + 1)
                pe.wait_ge(sem("a_pt_prev"), u + 1)
                pe.wait_ge(sem("a_out"), u)
                for back in (1, 0) if prev else (0,):
                    for h in range(H):
                        last = pe.matmul(bank[6][:, h * HD:(h + 1) * HD], pt[:, s, 1 - back, h],
                                         vg[:, bass.ds(2 * i + s - back, 1), h * HD:(h + 1) * HD],
                                         start=(h == 0 and back == prev), stop=(h == H - 1 and back == 0),
                                         skip_group_check=True)
                last.then_inc(sem("mm_att"), 1)

            for g in range(G):
                pe.wait_ge(sem(f"kv_loaded{g}"), 32 if g == 0 else 48)
                units(pe, g, begin, finish)
            pe.wait_ge(sem("a_out"), 24)
            for t in range(9):
                s, w = t % 2, P if t < 8 else NS
                pe.wait_ge(sem("m_sum"), t + 1)
                if t >= 2:
                    pe.wait_ge(sem("oa_lo"), t - 1)
                for c in range(2):
                    last = pe.transpose(bank[2 + s][:, c * w:(c + 1) * w], om[0:w, s, c * P:(c + 1) * P],
                                        C("ident")[0:w, 0:w])
                last.then_inc(sem("mm_om"), 1)
            piece = [P_AO]

            def narrow(base, blocks_, kk, hi, lo):
                for n in range(blocks_):
                    pe.wait_ge(sem("w_split"), base + n + 1)
                    for o in range(KD // kk):
                        for c in range(3):
                            q = piece[0]
                            piece[0] += 1
                            pe.wait_ge(sem(f"bank_free{q % 2}"), q // 2)
                            for k in range(kk):
                                for a, b in parts:
                                    last = pe.matmul(bank[q % 2][:, 0:PC], wpart[a][:, n % 2, o * kk + k],
                                                     (hi, lo)[b][:, k, c * PC:(c + 1) * PC],
                                                     start=(k == 0 and (a, b) == (0, 0)),
                                                     stop=(k == kk - 1 and a == 1))
                            last.then_inc(sem("mm_piece"), 1)

            pe.wait_ge(sem("oa_lo"), 9)
            narrow(B_AO, N_AO, 2, oah, oal)
            pe.wait_ge(sem("or_lo"), 4)
            narrow(B_RO, N_RO, 4, orh, orl)
            pe.wait_ge(sem("m_lo"), KD)
            rows(B_WO, P_WO, N_WO)
            pe.wait_ge(sem("n_added"), 2 * KD)
            for n in range(3):
                pe.matmul(bank[2 + n][:, 0:PC], C("mones"), nsum[:, n * PC:(n + 1) * PC], start=True, stop=True)\
                    .then_inc(sem("n_summed"), 1)
            pe.wait_ge(sem("a_split"), 2 * KD)
            rows(B_UP, P_UP, N_UP)
            pe.wait_ge(sem("h_hi"), KF)
            pe.wait_ge(sem("bank_free0"), P_DN // 2)
            pe.wait_ge(sem("bank_free1"), P_DN // 2)
            hpart = (hhi, hlo)
            for o in range(KD):
                for j in range(3):
                    n = 3 * o + j
                    pe.wait_ge(sem("w_split"), B_DN + n + 1)
                    if j == 0 and o >= 2:
                        pe.wait_ge(sem("y_ready2"), 3 * (o - 1))
                    for k in range(8 * j, min(8 * j + 8, KF)):
                        for m_, (a_, _) in enumerate(HLO_PARTS):
                            if o == 0 and k == a_:
                                pe.wait_ge(sem(f"hlo_loaded{m_}"), 16)
                        for c in range(3):
                            for a, b in parts:
                                last = pe.matmul(bank[3 * (o % 2) + c][:, 0:PC], wpart[a][:, n % 2, k - 8 * j],
                                                 hpart[b][:, k, c * PC:(c + 1) * PC],
                                                 start=(k == 0 and (a, b) == (0, 0)), stop=(k == KF - 1 and a == 1))
                    last.then_inc(sem("mm_down"), 1)


def lay_out(x):
    f = np.float32
    a = {k: np.asarray(v) for k, v in x.items()}
    xT = np.concatenate([a["x_prompt"][0], a["x_sample"][:, 0]], 0).T
    w_in = a["w_in"][0]

    def blocks(w):
        kk, nn = w.shape[0] // P, w.shape[1] // P
        return w.reshape(kk, P, nn, P).transpose(2, 1, 0, 3)

    def pack(w, per):
        b = blocks(w)
        n, _, kk, _ = b.shape
        return b.reshape(n // per, per, P, kk, P).transpose(0, 2, 1, 3, 4).reshape(n // per, P, per * kk, P)

    c0 = 3 * AW
    up = blocks(a["w_up"][0])
    up = up.reshape(2, KF, P, KD, P).transpose(1, 0, 2, 3, 4).reshape(2 * KF, P, KD, P)
    dn = blocks(a["w_down"][0])
    dn = np.concatenate([dn, np.zeros((KD, P, 24 - KF, P), f)], 2).reshape(KD, P, 3, 8, P)\
        .transpose(0, 2, 1, 3, 4).reshape(3 * KD, P, 8, P)
    wst = np.concatenate([
        blocks(w_in[:, c0:c0 + RP]), blocks(w_in[:, 0:2 * AW]), blocks(w_in[:, 2 * AW:3 * AW]),
        blocks(w_in[:, c0 + RP:]), pack(a["w_attn_out"][0], 4), pack(a["w_rwkv_out"][0], 2),
        blocks(a["w_o"][0]), up, dn], 0)
    assert wst.shape[0] == NB

    def col(v):
        return v.reshape(-1, P).T

    cw, cb = a["conv_w"][0], a["conv_b"][0]

    def pair(v):
        return v.reshape(2, KF, P).transpose(1, 0, 2).reshape(-1)

    par = np.concatenate([
        col(a["ln1_g"][0]), col(a["ln2_g"][0]),
        np.tile(a["q_norm_g"][0], 2)[:, None].repeat(6, 1), np.tile(a["k_norm_g"][0], 2)[:, None].repeat(6, 1),
        col(a["rwkv_mu"][0]), col(a["rwkv_w0"][0]), col(a["rwkv_a0"][0]), col(a["rwkv_k_k"][0]),
        col(a["rwkv_k_a"][0]), col(a["rwkv_r_k"][0].reshape(-1)), col(a["rwkv_gn_g"][0]), col(a["rwkv_gn_b"][0]),
        col(pair(cw[0])), col(pair(cw[1])), col(pair(cw[2])), col(pair(cb))], 1)
    assert par.shape[1] == N_PAR
    st = a["state_rwkv_wkv"][0].reshape(NS, RH, 2, 32, HD).transpose(2, 0, 1, 3, 4).reshape(P, 32 * HD)
    sc = a["state_ffn_conv"][0]
    hist = np.stack([pair(sc[b, i]) for i in range(2) for b in range(NS)]).reshape(2 * NS, 2 * KF, P)
    caches = {f"{kv}c{g}": a[f"cache_{kv}_w{w}"][0].reshape(NS, -1, 256) for kv in "kv"
              for g, w in enumerate((128, 512, 2048))}

    def picked(kv):
        rows = [caches[f"{kv}c{g}"][:, ::d] for g, d in enumerate(DIL)]
        rows[2] = np.concatenate([rows[2], np.zeros((NS, 96, 256), f)], 1)
        return np.stack(rows).reshape(G, NS, 128, H, HD).transpose(0, 1, 3, 2, 4).reshape(96, 128 * HD)

    more0 = {"wkvs": st, "shT": a["state_rwkv_shift"][0].T, "sconvT": hist.transpose(2, 1, 0).reshape(P, -1),
             "sconv1": sc[:, 1], "skc": picked("k"), "svc": picked("v")} | caches
    more = more0 | {"w2": a["rwkv_w2"][0], "a2": a["rwkv_a2"][0], "g2": a["rwkv_g2"][0], "zeros": np.zeros((RP, 1), f)}
    arrays = more | {"xT": xT, "wst": wst.reshape(NB, P, KD * P), "cst": constants(), "par": par}
    return {k: np.ascontiguousarray(v) for k, v in arrays.items()}


def kernel(**x):
    import concourse.bacc as bacc
    from concourse.bass_utils import run_bass_kernel_spmd

    arrays = {f"in_{k}": v for k, v in lay_out(x).items()}
    nc = bacc.Bacc("TRN2", target_bir_lowering=False, num_devices=1)
    ins = {k[3:]: nc.dram_tensor(k, v.shape, F32, kind="ExternalInput").ap() for k, v in arrays.items()}
    outs = {k: nc.dram_tensor(f"out_{k}", v, F32, kind="ExternalOutput").ap() for k, v in OUTS.items()}
    program(nc, ins, outs)
    r = run_bass_kernel_spmd(nc, [arrays], core_ids=[0]).results[0]
    return returned({k: r[f"out_{k}"] for k in OUTS})


def returned(r):
    y = r["yT"].T
    k = r["qkT"][AW:].T.reshape(T, G, H, HD)
    v = r["vtok"].reshape(T, G, H, HD)
    out = [y[:S][None], y[S:][:, None]]
    for g, keep in enumerate((128, 512, 1024)):
        out += [k[S - keep:S, g][None, None], r[f"kc{g}"].reshape(1, NS, -1, H, HD),
                v[S - keep:S, g][None, None], r[f"vc{g}"].reshape(1, NS, -1, H, HD)]
    out += [r["rwlast"][:, 0][None, None], r["rwlast"][:, 1:].T[None]]
    out.append(r["wkvp"].transpose(2, 0, 3, 1).reshape(1, 1, RH, HD, HD))
    out.append(r["wkvs"].reshape(2, NS, RH, 32, HD).transpose(1, 2, 0, 3, 4).reshape(1, NS, RH, HD, HD))
    u = r["convo"].reshape(KF, 2, P, 2 + NS).transpose(3, 1, 0, 2).reshape(2 + NS, 2 * FF)
    out.append(u[0:2][None, None])
    out.append(np.concatenate([r["convs0"][:, None], u[2:][:, None]], 1)[None])
    return tuple(np.ascontiguousarray(o) for o in out)


OUTS = {"yT": [D, T], "wkvs": [P, 32 * HD], "convo": [2 * KF, P, 2 + NS], "convs0": [NS, 2 * FF],
        "kc0": [NS, 128, 256], "kc1": [NS, 512, 256], "kc2": [NS, 513, 256],
        "vc0": [NS, 128, 256], "vc1": [NS, 512, 256], "vc2": [NS, 513, 256], "wkvp": [2, HD, 4, HD], "qkT": [2 * AW, T], "vtok": [T, AW], "rwlast": [RP, 1 + NS]}
```

```python
from contextlib import ExitStack

import numpy as np

import concourse.bass as bass
from concourse import mybir

F32 = mybir.dt.float32
F32R = mybir.dt.float32r
ALU = mybir.AluOpType
ACT = mybir.ActivationFunctionType
AX = mybir.AxisListType

P = 128
D = 1024
KD = D // P
S = 1024
NS = 8
T = S + NS
PC = T // 3
HD = 64
G, H = 3, 4
AW = G * H * HD
RH = 8
RW = RH * HD
RP = 3 * RW + 256
FF = 2816
KF = FF // P
RMS_EPS, GN_EPS, L2_EPS = 1e-6, 64e-5, 1e-12
DECAY = float(np.exp(-0.5))
NEG = -1e30
DIL = (1, 4, 16)
HLO_PARTS = ((0, 1), (1, 4), (4, 11), (11, KF))
NT = S // P

N_RW, N_QK, N_GA, N_V = RP // P, 2 * AW // P, 2 * D // P, AW // P
N_AO, N_RO, N_WO, N_UP, N_DN = 2, 4, KD, 2 * KF, 3 * KD
B_QK = 0
B_V = B_QK + N_QK
B_RW = B_V + N_V
B_GA = B_RW + N_RW
B_RO = B_GA + N_GA
B_AO = B_RO + N_RO
B_WO = B_AO + N_AO
B_UP = B_WO + N_WO
B_DN = B_UP + N_UP
NB = B_DN + N_DN
P_RO = 3 * B_RO
P_AO = P_RO + 6 * N_RO
P_WO = P_AO + 12 * N_AO
P_UP = P_WO + 3 * N_WO
P_DN = P_UP + 3 * N_UP

PAR = {}
_at = 0
for _n, _w in (("g1", KD), ("g2", KD), ("qkg", N_QK), ("mu", N_RW), ("w0", 4), ("a0", 4), ("kk", 4), ("ka", 4),
               ("rk", 4), ("gng", 4), ("gnb", 4), ("cw0", 2 * KF), ("cw1", 2 * KF), ("cw2", 2 * KF), ("cb", 2 * KF)):
    PAR[_n] = (_at, _w)
    _at += _w
N_PAR = _at

CST = {}
_at = 0
for _n, _w in (("ident", P), ("bd", P), ("su", P), ("iu", P), ("sl", P), ("lv0", P), ("lv0t", P), ("lvl", 6 * P),
               ("prev", P), ("cur", P), ("cur2", P), ("prevcur", 0), ("scan", 4 * P), ("eps", 4), ("mones", P)):
    CST[_n] = (_at, _w)
    _at += _w
N_CST = _at

STEPS = (
    ("e_w", "e_wi", "e_wm", "e_wp", "r_gate", "p1_ready", "gv_ready", "u_ready", "y_ready", "y_squared", "y_dev"),
    ("c_sum", "c_mid", "c_ready", "cp_ready", "b_raw", "k_gain", "k_ready", "rk_raw", "rk_ready", "bt_ready",
     "kt_ready", "at_ready", "rt_ready", "wend_ready", "rk_summed", "sm_ready", "s_sum", "s_ready", "y_centred"),
    ("mm_bonus", "mm_p1", "mm_gv", "mm_u", "mm_s", "mm_y", "mm_mean", "mm_var"),
    ("r_tanh", "r_sgl", "kk_squared", "kk_len", "r_sgw", "r_sga"),
    ("kk_raw", "kk_clamped", "kk_inv", "kk_ready"),
    ("mm_kk", "mm_lora_w", "mm_lora_a", "mm_lora_g"),
    ("x_diff", "x_mixed", "xs_ready"),
    ("y_rstd", "y_normed", "y_gained", "y_bonus", "o_ready"),
    ("mm_ulora_w", "mm_ulora_a", "mm_ulora_g", "mm_ukk", "mm_urow0", "mm_urow1", "mm_urow2", "mm_urow3", "mm_urow4",
     "mm_urow5", "mm_ubonus", "mm_uy", "mm_umean", "mm_uvar"),
)


def step(name, i):
    steps = next(x for x in STEPS if name in x)
    return len(steps) * i + steps.index(name) + 1


def constants():
    c = np.zeros((P, N_CST), np.float32)
    i, j = np.arange(P)[:, None], np.arange(P)[None, :]

    def put(name, value, off=0):
        a = CST[name][0] + off
        c[:, a:a + np.broadcast_to(value, (P, value.shape[-1])).shape[1]] = value

    put("ident", (i == j) * 1.0)
    put("bd", (i // HD == j // HD) * 1.0)
    put("su", (i < j) * 1.0)
    put("iu", (i <= j) * 1.0)
    put("sl", (i > j) * 1.0)
    low = (i // 2 == j // 2) & (i > j)
    put("lv0", low * 1.0)
    put("lv0t", low.T * 1.0)
    for k in range(1, 7):
        b = 1 << k
        put("lvl", ((i // (2 * b) == j // (2 * b)) & (i // b > j // b)) * 1.0, (k - 1) * P)
    put("prev", np.where(j >= i, 0.0, NEG))
    put("cur", np.where(j <= i, 0.0, NEG))
    put("cur2", np.where((j <= i) & (i // HD == j // HD), 0.0, NEG))
    scan = np.ones((P, 4 * P))
    scan[:, ::P] = 0
    put("scan", scan)
    put("eps", np.broadcast_to(np.array([RMS_EPS, GN_EPS, 0.0, 0.0]), (P, 4)))
    put("mones", np.full((P, P), 1.0))
    return c


def rup(x):
    return (x + 31) // 32 * 32


class Map:

    def __init__(self, nc, start):
        self.nc, self.at = nc, start

    def put(self, name, shape, dt=F32):
        n = int(np.prod(shape[1:])) * 4
        t = self.nc.alloc_sbuf_tensor_at(name, list(shape), dt, offset=self.at)
        self.at = rup(self.at + n)
        return t


def program(nc, ins, outs):
    xT, wst, cst_d, par_d = ins["xT"], ins["wst"], ins["cst"], ins["par"]
    sems = {}
    ctx = ExitStack()

    def sem(name):
        if name not in sems:
            sems[name] = ctx.enter_context(nc.semaphore(name))
        return sems[name]

    with ctx:
        m = Map(nc, 16512)
        wraw = m.put("wraw", [P, 2, KD, P])
        whi = m.put("whi", [P, 2, KD, P], F32R)
        wlo = m.put("wlo", [P, 2, KD, P], F32R)
        par = m.put("par", [P, N_PAR])
        big = m.at
        after_big = rup(big + KF * T * 4)
        m.at = after_big
        cst = m.put("cst", [P, N_CST])
        gap = m.at
        ahi_at = 229344 - 2 * rup(KD * T * 4)
        m.at = ahi_at
        ahi = m.put("ahi", [P, KD, T], F32R)
        alo = m.put("alo", [P, KD, T], F32R)
        m.at = gap
        stage = m.put("stage", [P, 2, T])
        gap2 = m.at
        mb = Map(nc, big)
        xraw = mb.put("xraw", [P, KD, T])
        nsum = mb.put("nsum", [P, T])
        ntmp = mb.put("ntmp", [P, 2, T])
        nrt = mb.put("nrt", [P, T])
        nrs = mb.put("nrs", [P, T])
        mb = Map(nc, big)
        pin = mb.put("pin", [P, N_RW, 1 + P])
        xs = mb.put("xs", [P, N_RW, P])
        sg = mb.put("sg", [P, 9, P])
        kkn = mb.put("kkn", [P, 4, P])
        tmp = mb.put("tmp", [P, 4, P])
        kt = mb.put("kt", [P, 4, P])
        bt = mb.put("bt", [P, 4, P])
        cs = mb.put("cs", [P, 4, P])
        cp = mb.put("cp", [P, 4, P])
        ew = mb.put("ew", [P, 4, P])
        ewp = mb.put("ewp", [P, 4, P])
        ewi = mb.put("ewi", [P, 4, P])
        gg = mb.put("gg", [P, 4, P])
        bon = mb.put("bon", [P, 4, P])
        ar = mb.put("ar", [P, 4, 2, P])
        vtm = mb.put("vtm", [P, RW])
        atm = mb.put("atm", [P, RW])
        btm = mb.put("btm", [P, RW])
        ktm = mb.put("ktm", [P, RW])
        gq = mb.put("gq", [P, RH, 2, P])
        nq = mb.put("nq", [P, RH, 2, P])
        ti = mb.put("ti", [P, RH, P])
        tt = mb.put("tt", [P, RH, P])
        tiles_end = mb.at
        mb = Map(nc, gap2)
        xx = mb.put("xx", [P, RH, P])
        p1 = mb.put("p1", [P, 4, P])
        ysq, ydev = xx[:, 0:4], xx[:, 4:8]
        small = mb.at
        mb = Map(nc, tiles_end)
        gv = mb.put("gv", [P, RW])
        uu = mb.put("uu", [P, RW])
        st = mb.put("st", [P, 4, P])
        sm = mb.put("sm", [P, 4, P])
        yv = mb.put("yv", [P, 4, P])
        yc = mb.put("yc", [P, 4, P])
        assert mb.at <= after_big, mb.at - after_big
        mb = Map(nc, small)
        cm = mb.put("cm", [P, 4])
        wm = mb.put("wm", [P, 4])
        wend = mb.put("wend", [P, 4])
        lora = mb.put("lora", [P, 2, RW])
        assert mb.at <= ahi_at, mb.at - ahi_at

        mb = Map(nc, big + 16384)
        svec = mb.put("svec", [NS, 6, RW])
        srow = mb.put("srow", [P, 6, HD])
        sst = mb.put("sst", [P, 32, HD])
        stp = mb.put("stp", [P, 32, HD])
        ssa = mb.put("ssa", [P, 32])
        syo = mb.put("syo", [P, 32])
        sym = mb.put("sym", [NS, RW])
        s4 = mb.put("s4", [P, 12, 4, NS])
        ssg = mb.put("ssg", [P, 9, NS])
        assert mb.at <= after_big

        mb = Map(nc, big)
        qgs = [mb.put(f"qg{n}", [P, 2, S]) for n in range(2)]
        kgs = [mb.put(f"kg{n}", [P, 2, S]) for n in range(2)]
        vgs = [mb.put(f"vg{n}", [P, 8, H * HD]) for n in range(2)]
        qz = mb.put("qz", [P, 2, H, P])
        sc = mb.put("sc", [P, 2, H, 2, P])
        pt = mb.put("pt", [P, 2, 2, H, P])
        ob = mb.put("ob", [P, 2, 264])
        assert mb.at <= after_big
        mb = Map(nc, big)
        oah = mb.put("oah", [P, 2, T], F32R)
        oal = mb.put("oal", [P, 2, T], F32R)
        ym = mb.put("ym", [P, KD, T])
        assert mb.at <= after_big
        mb = Map(nc, ahi_at)
        orh = mb.put("orh", [P, 4, T], F32R)
        orl = mb.put("orl", [P, 4, T], F32R)
        mo = mb.put("mo", [P, NT, G, 264])
        mo9 = mb.put("mo9", [NS, 1, G, 264])
        md = mb.put("md", [P, NT, G, H])
        md9 = mb.put("md9", [NS, 1, G, H])
        mn = mb.put("mn", [P, 2, NT, H])
        mn9 = mb.put("mn9", [NS, 2, 1, H])
        om = mb.put("om", [P, 2, H * HD])
        assert mb.at <= 229344
        mb = Map(nc, big)
        hhi = mb.put("hhi", [P, KF, T], F32R)
        mb = Map(nc, after_big)
        ug = mb.put("ug", [P, 2, 2 + T])
        cc = mb.put("cc", [P, 2, T])
        hlo_st = mb.put("hlo_st", [P, 1, T], F32R)
        cst8 = mb.put("cst8", [P, 2 * KF, 2, NS])
        assert mb.at <= ahi_at, mb.at - ahi_at
        hlo_at = 229344 - rup(KF * T * 4)
        mb = Map(nc, hlo_at)
        hlo = mb.put("hlo", [P, KF, T], F32R)
        mb = Map(nc, after_big)
        yst = mb.put("yst", [P, 2, PC])
        yrs = mb.put("yrs", [P, 2, PC])
        assert mb.at <= hlo_at, mb.at - hlo_at

        mb = Map(nc, big)
        qsq = mb.put("qsq", [P, 2, PC])
        qrt = mb.put("qrt", [P, 6, PC])
        vst = mb.put("vst", [P, 9, H * HD])
        skc = mb.put("skc", [96, 129, HD])
        svc = mb.put("svc", [96, 129, HD])
        sq = mb.put("sq", [96, HD])
        ssc = mb.put("ssc", [96, 129])
        sso = mb.put("sso", [96, HD])
        snm = mb.put("snm", [96, 2])
        assert mb.at <= after_big, mb.at - after_big

        bank = [ctx.enter_context(nc.psum_tensor(f"bank{i}", [P, 512], F32)) for i in range(8)]

        def C(name, off=0, width=P):
            a = CST[name][0] + off
            return cst[:, a:a + width]

        def par1(name, i):
            a = PAR[name][0]
            return par[:, bass.ds(a + i, 1)]

        eps_rms = cst[:, CST["eps"][0]:CST["eps"][0] + 1]
        eps_gn = cst[:, CST["eps"][0] + 1:CST["eps"][0] + 2]

        qkT_v = outs["qkT"].rearrange("(c p) t -> c p t", p=P)
        gT_v = nc.dram_tensor("gT", [2 * D, T], F32, kind="Internal").ap().rearrange("(c p) t -> c p t", p=P)
        ao = nc.dram_tensor("ao", [G, T, 264], F32, kind="Internal").ap()
        x1T = nc.dram_tensor("x1T", [D, T], F32, kind="Internal").ap().rearrange("(c p) t -> c p t", p=P)
        hloT = nc.dram_tensor("hloT", [FF, T], F32, kind="Internal").ap().rearrange("(c p) t -> c p t", p=P)
        orwT_d = nc.dram_tensor("orwT", [RW, T], F32, kind="Internal").ap()
        xT_c = xT.rearrange("(c p) t -> c p t", p=P)
        yT_c = outs["yT"].rearrange("(c p) t -> c p t", p=P)
        orwT = orwT_d.rearrange("(c p) t -> p c t", p=P)
        rwT = nc.dram_tensor("rwT", [RP, 1 + T], F32, kind="Internal").ap()
        rwT_v = rwT.rearrange("(c p) t -> c p t", p=P)
        rwlast_v = outs["rwlast"].rearrange("(c p) t -> c p t", p=P)
        v_prompt_v = outs["vtok"][0:S].rearrange("(t p) c -> p t c", p=P)
        v_sample_v = outs["vtok"][S:T]

        def stored_before(base, i):
            if base == B_QK:
                return 16 * i
            return 8 * N_QK + (32 * i if base == B_RW else 16 * N_RW + 16 * i)

        def peeled(engine, count, body):
            body(0)
            with engine.Fori(1, count) as i:
                body(i)

        def units(engine, g, begin, finish):
            def pair(i, more):
                begin(g, i, 1)
                finish(g, i, 0)
                if more:
                    begin(g, i + 1, 0)
                finish(g, i, 1)

            begin(g, 0, 0)
            if g == 0:
                pair(0, True)
            with engine.Fori(1 if g == 0 else 0, 3) as i:
                pair(i, True)
            pair(3, False)

        def has_previous(g, i, s):
            return (not (isinstance(i, int) and i == s == 0), s == 1, False)[g]

        block = ctx.enter_context(nc.Block())

        @block.sync
        def _(sp):
            sp.dma_start(lora[0:HD, 0], ins["w2"]).then_inc(sem("lora_loaded"), 16)
            sp.dma_start(lora[HD:P, 0], ins["a2"]).then_inc(sem("lora_loaded"), 16)
            sp.dma_start(lora[:, 1], ins["g2"]).then_inc(sem("lora_loaded"), 16)
            sp.dma_start(rwT[:, 0:1], ins["zeros"], allow_slow_non_contiguous=True).then_inc(sem("zero_col"), 16)
            sp.dma_start(par[:], par_d).then_inc(sem("par_loaded"), 16)
            sp.dma_start(cst[:], cst_d).then_inc(sem("cst_loaded"), 16)
            for half in range(2):
                c = slice(4 * half, 4 * half + 4)
                sp.dma_start(xraw[:, c], xT.rearrange("(c p) t -> p c t", p=P)[:, c]).then_inc(sem(f"x_loaded{half}"), 16)
            for s in range(2):
                sp.dma_start(wraw[:, s], wst[s]).then_inc(sem(f"w_loaded{s}"), 16)
            def weights(lo, hi):
                with sp.Fori(lo, hi) as i:
                    for s in range(2):
                        sp.wait_ge(sem("w_split"), 2 * i + s - 1)
                        sp.dma_start(wraw[:, s], wst[2 * i + s]).then_inc(sem(f"w_loaded{s}"), 16)

            weights(1, B_RO // 2)
            for g in range(G):
                n = (128, 512, 512)[g]
                drop = (1, 1, 0)[g]
                for kv in "kv":
                    sp.dma_start(outs[f"{kv}c{g}"][:, 0:n - drop], ins[f"{kv}c{g}"][:, drop:n])\
                        .then_inc(sem("caches_moved"), 16)
            sp.dma_start(outs["convs0"], ins["sconv1"]).then_inc(sem("caches_moved"), 16)
            weights(B_RO // 2, NB // 2)
            sp.wait_ge(sem("caches_moved"), 16 * 7)

        @block.gpsimd
        def _(pool):
            def split(i, s):
                pool.wait_ge(sem(f"w_loaded{s}"), 16 * i + 16)
                pool.sem_inc(sem("w_turn"), 1)
                nc.gpsimd.tensor_scalar(whi[:, s], wraw[:, s], 1.0, 0.0, ALU.mult, ALU.add).then_inc(sem("w_hi"), 1)
                pool.wait_ge(sem("w_hi"), 2 * i + s + 1)
                nc.gpsimd.tensor_tensor(wlo[:, s], wraw[:, s], whi[:, s].bitcast(F32), ALU.subtract)\
                    .then_inc(sem("w_split"), 1)

            split(0, 0)
            split(0, 1)
            def pairs(lo, hi):
                with pool.Fori(lo, hi) as i:
                    for s in range(2):
                        pool.wait_ge(sem("mm_piece"), 6 * i + 3 * s - 3)
                        split(i, s)

            pairs(1, B_GA // 2 + 1)

            mu = PAR["mu"][0]

            def shift(i):
                pool.wait_ge(sem("pin_loaded"), 16 * i + 16)
                nc.gpsimd.tensor_tensor(xs[:], pin[:, :, 0:P], pin[:, :, 1:1 + P], ALU.subtract)\
                    .then_inc(sem("pool_next"), 1)
                pool.wait_ge(sem("pool_next"), step("x_diff", i))
                nc.gpsimd.tensor_tensor(xs[:], xs[:], par[:, mu:mu + N_RW].unsqueeze(2).broadcast_to([P, N_RW, P]),
                                        ALU.mult).then_inc(sem("pool_next"), 1)
                pool.wait_ge(sem("pool_next"), step("x_mixed", i))
                nc.gpsimd.tensor_tensor(xs[:], xs[:], pin[:, :, 1:1 + P], ALU.add).then_inc(sem("pool_next"), 1)

            shift(0)
            with pool.Fori(0, NT - 1) as i:
                pool.wait_ge(sem("mm_piece"), 3 * B_GA + 6 * i + 3)
                split(B_GA // 2 + 1 + i, 0)
                pool.wait_ge(sem("dve_tile"), step("rk_summed", i))
                shift(i + 1)
                pool.wait_ge(sem("mm_piece"), 3 * B_GA + 6 * i + 6)
                split(B_GA // 2 + 1 + i, 1)
            for s in range(2):
                pool.wait_ge(sem("mm_piece"), 3 * B_RO - 3 + 3 * s)
                split(B_RO // 2, s)
            pool.wait_ge(sem("qz_zero"), 1)
            pool.wait_ge(sem("w_split"), B_RO + 2)

            def queries(g, i, s):
                u = 8 * g + 2 * i + s
                qg = qgs[g % 2]
                pool.wait_ge(sem("mm_score"), u - 1)
                for hh in range(2):
                    pool.wait_ge(sem("qz_ready"), 2 * u + hh)
                    pool.wait_ge(sem("qz_zero"), 1)
                    q = slice(hh * HD, (hh + 1) * HD)
                    if g == 0:
                        src, dst = qg[q, :, bass.ds((2 * i + s) * P, P)], qz[q, s, hh::2]
                    elif g == 1:
                        src = qg[q].rearrange("p c (b i r) -> p c b r i", b=2, r=4)[:, :, s, bass.ds(i, 1)]
                        dst = qz[q, s, hh::2].unsqueeze(2)
                    else:
                        src = qg[q].rearrange("p c (i r) -> p c r i", r=16)[:, :, bass.ds(4 * i + 2 * s, 2)]
                        dst = qz[q, s, hh::2].rearrange("p h (r i) -> p h r i", r=2)
                    nc.gpsimd.tensor_copy(dst, src).then_inc(sem("qz_ready"), 1)

            for g in range(G):
                pool.wait_ge(sem(f"qg_loaded{g}"), 16)
                if g == 0:
                    for s in range(2):
                        for hh in range(2):
                            q = slice(hh * HD, (hh + 1) * HD)
                            pool.wait_ge(sem("qz_ready"), 2 * s + hh)
                            nc.gpsimd.tensor_copy(qz[q, s, hh::2], qgs[0][q, :, s * P:(s + 1) * P])\
                                .then_inc(sem("qz_ready"), 1)
                with pool.Fori(1 if g == 0 else 0, 4) as i:
                    for s in range(2):
                        queries(g, i, s)
            ends = [P_RO + 6 * (n + 1) for n in range(N_RO)] + [P_AO + 12 * (n + 1) for n in range(N_AO)]
            for n in range(2, N_AO + N_RO + 2):
                pool.wait_ge(sem("mm_piece"), ends[n - 2])
                split((B_RO + n) // 2, n % 2)
            with pool.Fori((B_WO + 2) // 2, B_DN // 2) as i:
                for s in range(2):
                    pool.wait_ge(sem("mm_piece"), P_WO + 3 * (2 * i + s - 1 - B_WO))
                    split(i, s)
            for s in range(2):
                pool.wait_ge(sem("mm_piece"), P_DN - 3 + 3 * s)
                split(B_DN // 2, s)
            with pool.Fori(B_DN // 2 + 1, NB // 2) as i:
                for s in range(2):
                    pool.wait_ge(sem("mm_down"), 2 * i + s - 1 - B_DN)
                    split(i, s)

        @block.scalar
        def _(act):
            act.wait_ge(sem("cst_loaded"), 16)
            slow = dict(allow_slow_non_contiguous=True)
            for k in range(KD):
                act.wait_ge(sem(f"x_loaded{k // 4}"), 16)
                if k >= 2:
                    act.wait_ge(sem("n_added"), k - 1)
                nc.scalar.activation(ntmp[:, k % 2], xraw[:, k], ACT.Square).then_inc(sem("n_squared"), 1)
            for n in range(3):
                act.wait_ge(sem("n_summed"), n + 1)
                nc.scalar.activation(nrt[:, n * PC:(n + 1) * PC], bank[n][:, 0:PC], ACT.Sqrt, bias=eps_rms,
                                     scale=1.0 / D).then_inc(sem("n_root"), 1)
            for k in range(KD):
                act.wait_ge(sem("n_scaled"), k + 1)
                nc.scalar.activation(ahi[:, k], xraw[:, k], ACT.Copy).then_inc(sem("a_hi"), 1)

            def rows(base, lo, hi, func, dst, last=None):
                def pair(i):
                    for s in range(2):
                        act.wait_ge(sem(f"stored{s}"), stored_before(base, i))
                        for n in range(3):
                            q = 3 * s + n
                            act.wait_ge(sem("mm_piece"), 3 * base + 6 * i + q + 1)
                            nc.scalar.activation(stage[:, s, n * PC:(n + 1) * PC], bank[q % 2][:, 0:PC], func)\
                                .then_inc(sem(f"bank_free{q % 2}"), 1)
                        act.wait_ge(sem("bank_free0"), 3 * base // 2 + 3 * i + (3 * s + 3 + 1) // 2)
                        act.wait_ge(sem("bank_free1"), 3 * base // 2 + 3 * i + (3 * s + 3) // 2)
                        act.dma_start(dst(2 * i + s), stage[:, s]).then_inc(sem(f"stored{s}"), 16)
                        if last:
                            act.dma_start(last(2 * i + s), stage[:, s, S - 1:T]).then_inc(sem(f"stored{s}"), 16)

                with act.Fori(lo, hi) as i:
                    pair(i)

            act.wait_ge(sem("a_split"), KD)
            act.dma_start(skc[:, 0:128].rearrange("p k j -> p (k j)"), ins["skc"]).then_inc(sem("z_loaded"), 16)
            act.dma_start(svc[:, 0:128].rearrange("p k j -> p (k j)"), ins["svc"]).then_inc(sem("z_loaded"), 16)

            def qk_pair(i):
                for q in range(6):
                    s, n = q // 3, q % 3
                    if n == 0:
                        act.wait_ge(sem(f"stored{s}"), stored_before(B_QK, i))
                    act.wait_ge(sem("mm_piece"), 3 * B_QK + 6 * i + q + 1)
                    nc.scalar.activation(stage[:, s, n * PC:(n + 1) * PC], bank[q % 2][:, 0:PC], ACT.Copy)\
                        .then_inc(sem(f"bank_free{q % 2}"), 1)
                    act.wait_ge(sem(f"bank_free{q % 2}"), 3 * B_QK // 2 + 3 * i + q // 2 + 1)
                    nc.scalar.activation(qsq[:, q % 2], stage[:, s, n * PC:(n + 1) * PC], ACT.Square)\
                        .then_inc(sem("q_squared"), 1)
                    if q:
                        act.wait_ge(sem("q_summed"), 6 * i + q)
                        nc.scalar.activation(qrt[:, q - 1], bank[2 + (q - 1) % 2][:, 0:PC], ACT.Sqrt,
                                             bias=eps_rms, scale=1.0 / HD).then_inc(sem("q_root"), 1)
                    if q == 3:
                        act.wait_ge(sem("q_scaled"), 6 * i + 3)
                        act.dma_start(qkT_v[2 * i], stage[:, 0]).then_inc(sem("stored0"), 16)
                act.wait_ge(sem("q_summed"), 6 * i + 6)
                nc.scalar.activation(qrt[:, 5], bank[3][:, 0:PC], ACT.Sqrt, bias=eps_rms, scale=1.0 / HD)\
                    .then_inc(sem("q_root"), 1)
                act.wait_ge(sem("q_scaled"), 6 * i + 6)
                act.dma_start(qkT_v[2 * i + 1], stage[:, 1]).then_inc(sem("stored1"), 16)

            peeled(act, N_QK // 2, qk_pair)

            def v_pair(i):
                act.wait_ge(sem("v_stored"), 32 * i)
                for q in range(6):
                    if q % 2 == 0:
                        act.wait_ge(sem("mm_piece"), 3 * B_V + 6 * i + 4 + q // 2)
                    if q < 4:
                        out, src = vst[:, 2 * q:2 * q + 2], bank[2 + q][:].rearrange("p (t c) -> p t c", t=2)
                    else:
                        c = slice((q - 4) * P, (q - 3) * P)
                        out, src = vst[0:NS, 8, c], bank[6][0:NS, c]
                    nc.scalar.activation(out, src, ACT.Copy).then_inc(sem(f"bank_free{q % 2}"), 1)
                act.wait_ge(sem("bank_free0"), 3 * B_V // 2 + 3 * i + 3)
                act.wait_ge(sem("bank_free1"), 3 * B_V // 2 + 3 * i + 3)
                cols = bass.ds(i * H * HD, H * HD)
                act.dma_start(v_prompt_v[:, :, cols], vst[:, 0:8]).then_inc(sem("v_stored"), 16)
                act.dma_start(v_sample_v[:, cols], vst[0:NS, 8]).then_inc(sem("v_stored"), 16)

            def sample_rows(g):
                for b in range(NS):
                    r4 = slice(32 * g + 4 * b, 32 * g + 4 * b + 4)
                    act.dma_start(sq[r4], q4[0, g, S + b], **slow).then_inc(sem("z_loaded"), 16)
                    act.dma_start(skc[r4, 128], q4[1, g, S + b], **slow).then_inc(sem("z_loaded"), 16)

            q4 = outs["qkT"].rearrange("(a g h j) t -> a g t h j", a=2, g=G, j=HD)
            for s in range(2):
                act.wait_ge(sem(f"stored{s}"), stored_before(B_RW, 0))
            for g in range(G):
                v_pair(g)
                sample_rows(g)
            act.wait_ge(sem("v_stored"), 32 * G)
            for g in range(G):
                act.dma_start(svc[32 * g:32 * g + 32, 128], outs["vtok"][S:T, g * 256:(g + 1) * 256]
                              .rearrange("b (h j) -> b h j", j=HD)).then_inc(sem("z_loaded"), 16)
            act.wait_ge(sem("z_loaded"), 16 * (2 + 3 * 17))
            for g in range(G):
                rows_ = slice(32 * g, 32 * g + 32)
                for kv, t in (("k", skc), ("v", svc)):
                    act.dma_start(outs[f"{kv}c{g}"][:, (127, 511, 512)[g]].rearrange("b (h j) -> b h j", j=HD),
                                  t[rows_, 128]).then_inc(sem("z_rows_stored"), 16)

            def rw_rows(lo, hi):
                rows(B_RW, lo, hi, ACT.Copy, lambda c: rwT_v[c, :, 1:1 + T], lambda c: rwlast_v[c])

            rw_rows(0, 3)
            act.wait_ge(sem("z_max"), 1)
            nc.scalar.activation(ssc[:], ssc[:], ACT.Exp, bias=snm[:, 0:1], accum_out=snm[:, 1:2]).then_inc(sem("z_exp"), 1)
            rw_rows(3, 6)
            act.wait_ge(sem("z_out"), 1)
            for g in range(G):
                rows_ = slice(32 * g, 32 * g + 32)
                act.dma_start(ao[g, S:T, 0:256].rearrange("b (h j) -> b h j", j=HD), sso[rows_])\
                    .then_inc(sem("z_stored"), 16)
                for c in range(2):
                    act.dma_start(ao[g, S:T, 256 + 4 * c:260 + 4 * c].unsqueeze(2), snm[rows_, c:c + 1], **slow)\
                        .then_inc(sem("z_stored"), 16)
            act.wait_ge(sem("z_rows_stored"), 16 * 6)
            act.wait_ge(sem("z_stored"), 16 * 9)
            rw_rows(6, N_RW // 2)
            for s in range(2):
                act.wait_ge(sem(f"stored{s}"), stored_before(B_GA, 0))

            act.wait_ge(sem("lora_loaded"), 48)
            act.wait_ge(sem("zero_col"), 16)
            rwT_t = rwT[:, :].rearrange("(c p) t -> p c t", p=P)

            def load_tile(i):
                act.dma_start(pin[:], rwT_t[:, :, bass.ds(i * P, P + 1)]).then_inc(sem("pin_loaded"), 16)

            act.sem_inc(sem("o_free"), 16)

            def gates(i, q):
                s, n = q // 3, q % 3
                if n == 0:
                    act.wait_ge(sem(f"stored{s}"), stored_before(B_GA, i))
                act.wait_ge(sem("mm_piece"), 3 * B_GA + 6 * i + q + 1)
                nc.scalar.activation(stage[:, s, n * PC:(n + 1) * PC], bank[q % 2][:, 0:PC], ACT.Copy)\
                    .then_inc(sem(f"bank_free{q % 2}"), 1)
                if n == 2:
                    act.wait_ge(sem("bank_free0"), 3 * B_GA // 2 + 3 * i + (q + 2) // 2)
                    act.wait_ge(sem("bank_free1"), 3 * B_GA // 2 + 3 * i + (q + 1) // 2)
                    act.dma_start(gT_v[2 * i + s], stage[:, s]).then_inc(sem(f"stored{s}"), 16)

            def squash(i):
                act.wait_ge(sem("pool_next"), step("xs_ready", i))
                nc.scalar.activation(xs[0:HD, 12], xs[0:HD, 12], ACT.Tanh).then_inc(sem("act_next"), 1)
                nc.scalar.activation(sg[:, 8], xs[:, 13], ACT.Sigmoid).then_inc(sem("act_next"), 1)
                act.wait_ge(sem("dve_next"), step("kk_raw", i))
                nc.scalar.activation(tmp[:], kkn[:], ACT.Square).then_inc(sem("act_next"), 1)

            def kk_length(i):
                act.wait_ge(sem("pe_next"), step("mm_kk", i))
                nc.scalar.activation(tmp[:], bank[7][:].rearrange("p (c t) -> p c t", c=4), ACT.Sqrt)\
                    .then_inc(sem("act_next"), 1)

            def sigmoids(i):
                for n, (name, wait) in enumerate((("w0", "mm_lora_w"), ("a0", "mm_lora_a"))):
                    act.wait_ge(sem("pe_next"), step(wait, i))
                    for c in range(4):
                        last = nc.scalar.activation(sg[:, 4 * n + c], bank[2 + n][:, c * P:(c + 1) * P], ACT.Sigmoid,
                                                    bias=par1(name, c))
                    last.then_inc(sem("act_next"), 1)

            def rwkv(i, before=True, more=True):
                gates(i, 0)
                if more:
                    load_tile(i + 1)
                act.wait_ge(sem("dve_tile"), step("c_ready", i))
                nc.scalar.activation(ew[:], cs[:], ACT.Exp, scale=-DECAY).then_inc(sem("act_tile"), 1)
                nc.scalar.activation(ewi[:], cs[:], ACT.Exp, scale=DECAY).then_inc(sem("act_tile"), 1)
                nc.scalar.activation(wm[:], cm[:], ACT.Exp, scale=-DECAY).then_inc(sem("act_tile"), 1)
                act.wait_ge(sem("dve_tile"), step("cp_ready", i))
                nc.scalar.activation(ewp[:], cp[:], ACT.Exp, scale=-DECAY).then_inc(sem("act_tile"), 1)
                gates(i, 1)
                gates(i, 2)
                for n, (dst, b) in enumerate(((vtm, 6), (atm, 7), (btm, 2), (ktm, 3))):
                    if n == 1:
                        gates(i, 3)
                    act.wait_ge(sem("mm_turn"), 4 * i + n + 1)
                    nc.scalar.activation(dst[:], bank[b][:], ACT.Copy).then_inc(sem("turned"), 1)
                if before:
                    store_output(i - 1)
                act.wait_ge(sem("pe_next"), step("mm_lora_g", i))
                nc.scalar.activation(gg[:], bank[4][:].rearrange("p (c t) -> p c t", c=4), ACT.Copy)\
                    .then_inc(sem("act_tile"), 1)
                if more:
                    squash(i + 1)
                act.wait_ge(sem("pe_tile"), step("mm_p1", i))
                nc.scalar.activation(p1[:], bank[2][:].rearrange("p (c t) -> p c t", c=4), ACT.Copy)\
                    .then_inc(sem("act_tile"), 1)
                act.wait_ge(sem("pe_tile"), step("mm_gv", i))
                nc.scalar.activation(gv[:], bank[3][:], ACT.Copy).then_inc(sem("act_tile"), 1)
                if more:
                    kk_length(i + 1)
                act.wait_ge(sem("pe_tile"), step("mm_u", i))
                nc.scalar.activation(uu[:], bank[4][:], ACT.Copy).then_inc(sem("act_tile"), 1)
                if more:
                    sigmoids(i + 1)
                gates(i, 4)
                act.wait_ge(sem("pe_tile"), step("mm_y", i))
                nc.scalar.activation(yv[:], bank[5][:].rearrange("p (c t) -> p c t", c=4), ACT.Copy)\
                    .then_inc(sem("act_tile"), 1)
                act.wait_ge(sem("dve_tile"), step("y_centred", i))
                nc.scalar.activation(ysq, yc[:], ACT.Square).then_inc(sem("act_tile"), 1)
                act.wait_ge(sem("pe_tile"), step("mm_var", i))
                nc.scalar.activation(ydev, bank[7][:].rearrange("p (c t) -> p c t", c=4), ACT.Sqrt, bias=eps_gn,
                                     scale=1.0 / HD).then_inc(sem("act_tile"), 1)
                gates(i, 5)

            def store_output(i):
                act.wait_ge(sem("dve_tail"), step("o_ready", i))
                act.dma_start(orwT[:, :, bass.ds(i * P, P)], yc[:]).then_inc(sem("o_free"), 16)

            load_tile(0)
            squash(0)
            kk_length(0)
            sigmoids(0)
            rwkv(0, before=False)
            with act.Fori(1, NT - 1) as i:
                rwkv(i)
            rwkv(NT - 1, more=False)
            store_output(NT - 1)
            act.wait_ge(sem("o_free"), 16 * NT + 16)
            for s in range(2):
                act.wait_ge(sem(f"stored{s}"), stored_before(B_GA, NT))
            act.wait_ge(sem("dve_tile"), step("s_ready", NT - 1))
            for hh in range(2):
                act.dma_start(outs["wkvp"][hh], st[hh * HD:(hh + 1) * HD, :, hh * HD:(hh + 1) * HD])\
                    .then_inc(sem("wkvp_stored"), 16)
            act.wait_ge(sem("wkvp_stored"), 32)

            act.dma_start(pin[:, :, 0:NS], ins["shT"].rearrange("(c p) t -> p c t", p=P)).then_inc(sem("u_loaded"), 16)
            act.dma_start(pin[:, :, NS:2 * NS], rwT_t[:, :, 1 + S:1 + T]).then_inc(sem("u_loaded"), 16)
            act.dma_start(sst[:].rearrange("p i j -> p (i j)"), ins["wkvs"]).then_inc(sem("u_state"), 16)
            act.wait_ge(sem("u_xs"), 1)
            nc.scalar.activation(xs[0:HD, 12, 0:NS], xs[0:HD, 12, 0:NS], ACT.Tanh).then_inc(sem("u_tanh"), 1)
            nc.scalar.activation(ssg[:, 8], xs[:, 13, 0:NS], ACT.Sigmoid).then_inc(sem("u_sgl"), 1)
            act.wait_ge(sem("pe_sample"), step("mm_ulora_g", 0))
            for c in range(4):
                nc.scalar.activation(ssg[:, c], bank[2][:, c * NS:(c + 1) * NS], ACT.Sigmoid, bias=par1("w0", c))\
                    .then_inc(sem("u_sg"), 1)
            for c in range(4):
                nc.scalar.activation(ssg[:, 4 + c], bank[3][:, c * NS:(c + 1) * NS], ACT.Sigmoid, bias=par1("a0", c))\
                    .then_inc(sem("u_sg"), 1)
            nc.scalar.activation(s4[:, 6], bank[4][:, 0:4 * NS].rearrange("p (c t) -> p c t", c=4), ACT.Copy)\
                .then_inc(sem("u_gate"), 1)
            act.wait_ge(sem("u_kk"), 2)
            act.wait_ge(sem("pe_sample"), step("mm_ukk", 0))
            nc.scalar.activation(s4[:, 7], bank[5][:, 0:4 * NS].rearrange("p (c t) -> p c t", c=4), ACT.Sqrt)\
                .then_inc(sem("u_len"), 1)
            act.wait_ge(sem("u_sg"), 8)
            nc.scalar.activation(s4[:, 1], ssg[:, 0:4], ACT.Exp, scale=-DECAY).then_inc(sem("u_decay"), 1)
            for q in range(6):
                act.wait_ge(sem("pe_sample"), step(f"mm_urow{q}", 0))
                nc.scalar.activation(svec[:, q], bank[2 + q][0:NS, :], ACT.Copy).then_inc(sem("u_row"), 1)
            act.wait_ge(sem("u_row"), 6)
            for half in range(2):
                for q in range(6):
                    act.dma_start(srow[half * HD:(half + 1) * HD, q],
                                  svec[:, q].rearrange("b (h j) -> b h j", j=HD)).then_inc(sem("u_spread"), 16)
            act.wait_ge(sem("u_step"), 9)
            act.dma_start(outs["wkvs"], sst[:].rearrange("p i j -> p (i j)")).then_inc(sem("wkvs_stored"), 16)
            for half in range(2):
                act.dma_start(sym[:].rearrange("b (h i) -> b h i", i=HD)[:, :, half * 32:(half + 1) * 32],
                              syo[half * HD:(half + 1) * HD]).then_inc(sem("u_ygathered"), 16)
            act.wait_ge(sem("pe_sample"), step("mm_uy", 0))
            nc.scalar.activation(s4[:, 8], bank[2][:, 0:4 * NS].rearrange("p (c t) -> p c t", c=4), ACT.Copy)\
                .then_inc(sem("u_y"), 1)
            act.wait_ge(sem("u_centred"), 2)
            act.wait_ge(sem("pe_sample"), step("mm_uvar", 0))
            nc.scalar.activation(s4[:, 10], bank[4][:, 0:4 * NS].rearrange("p (c t) -> p c t", c=4), ACT.Sqrt,
                                 bias=eps_gn, scale=1.0 / HD).then_inc(sem("u_dev"), 1)
            act.wait_ge(sem("u_out"), 1)
            act.dma_start(orwT[:, :, S:T], s4[:, 9]).then_inc(sem("uo_stored"), 16)
            act.wait_ge(sem("uo_stored"), 16)
            act.wait_ge(sem("wkvs_stored"), 16)

            qk_c = outs["qkT"].rearrange("(a g c p) t -> a g p c t", a=2, g=G, p=P)

            def load_group(g):
                if g == 2:
                    act.wait_ge(sem("qz_ready"), 16)
                    act.wait_ge(sem("mm_att"), 8)
                act.dma_start(qgs[g % 2][:], qk_c[0, g, :, :, 0:S]).then_inc(sem(f"qg_loaded{g}"), 16)
                act.dma_start(kgs[g % 2][:], qk_c[1, g, :, :, 0:S]).then_inc(sem(f"kv_loaded{g}"), 16)
                rows_, vg = outs["vtok"][0:S, g * 256:(g + 1) * 256], vgs[g % 2]
                if g == 0:
                    act.dma_start(vg[:], rows_.rearrange("(u p) c -> p u c", p=P)).then_inc(sem("kv_loaded0"), 16)
                elif g == 1:
                    for b in range(2):
                        act.dma_start(vg[:, b::2], rows_[512 * b:512 * (b + 1)].rearrange("(p r) c -> p r c", r=4))\
                            .then_inc(sem("kv_loaded1"), 16)
                else:
                    for rr in range(2):
                        act.dma_start(vg[rr * HD:(rr + 1) * HD],
                                      rows_.rearrange("(p u r) c -> r p u c", u=8, r=2)[rr])\
                            .then_inc(sem("kv_loaded2"), 16)

            def begin(g, i, s):
                u = 8 * g + 2 * i + s
                half = slice(0, 2) if has_previous(g, i, s) else slice(1, 2)
                act.wait_ge(sem("a_max"), u + 1)
                for h in range(H):
                    nc.scalar.activation(sc[:, s, h, half], sc[:, s, h, half], ACT.Exp, bias=ob[:, s, 256 + h:257 + h],
                                         accum_out=ob[:, s, 260 + h:261 + h]).then_inc(sem("a_exp"), 1)

            def finish(g, i, s):
                u = 8 * g + 2 * i + s
                act.wait_ge(sem("mm_pt"), u + 1)
                nc.scalar.activation(pt[:, s, 1], bank[4][:].rearrange("p (h t) -> p h t", h=H), ACT.Copy)\
                    .then_inc(sem("a_pt_cur"), 1)

            def store(g, i, s):
                u = 8 * g + 2 * i + s
                act.wait_ge(sem("a_out"), u + 1)
                row = ao[g]
                if g == 0:
                    act.dma_start(row[bass.ds((2 * i + s) * P, P)], ob[:, s]).then_inc(sem(f"ao_stored{s}"), 16)
                elif g == 1:
                    act.dma_start(row[0:S].rearrange("(b i r) c -> b r i c", b=2, r=4)[s, bass.ds(i, 1)], ob[:, s])\
                        .then_inc(sem(f"ao_stored{s}"), 16)
                else:
                    for rr in range(2):
                        act.dma_start(row[0:S].rearrange("(i r) c -> r i c", r=16)[bass.ds(4 * i + 2 * s + rr, 1)],
                                      ob[rr * HD:(rr + 1) * HD, s]).then_inc(sem(f"ao_stored{s}"), 16)

            load_group(0)
            load_group(1)
            act.dma_start(mo9[:, 0], ao[:, S:T].rearrange("g p c -> p g c")).then_inc(sem("mo9_loaded"), 16)

            def load_rwkv(c):
                act.dma_start(stage[:, c % 2], orwT[:, c]).then_inc(sem("or_loaded"), 16)

            load_rwkv(0)
            load_rwkv(1)
            for g in range(G):
                def pair(i, more):
                    finish(g, i, 0)
                    begin(g, i, 1)
                    store(g, i, 0)
                    finish(g, i, 1)
                    if more:
                        begin(g, i + 1, 0)
                    store(g, i, 1)

                begin(g, 0, 0)
                if g == 0:
                    pair(0, True)
                with act.Fori(1 if g == 0 else 0, 3) as i:
                    pair(i, True)
                pair(3, False)
                if g == 0:
                    load_group(2)
                if g < 2:
                    act.wait_ge(sem("or_loaded"), 32 * (g + 1))
                    for c in (2 * g, 2 * g + 1):
                        nc.scalar.activation(orh[:, c], stage[:, c % 2], ACT.Copy).then_inc(sem("or_hi"), 1)
                    if g == 0:
                        act.wait_ge(sem("or_lo"), 2)
                        load_rwkv(2)
                        load_rwkv(3)
                for s in range(2):
                    act.wait_ge(sem(f"ao_stored{s}"), (64, 128, 256)[g])
                act.dma_start(mo[:, :, g], ao[g, 0:S].rearrange("(t p) c -> p t c", p=P)).then_inc(sem("mo_loaded"), 16)
            act.wait_ge(sem("mm_att"), 24)
            def gate(n):
                act.wait_ge(sem(f"gate_loaded{n % 2}"), 16 * (n // 2 + 1))
                nc.scalar.activation(stage[:, n % 2], stage[:, n % 2], ACT.Sigmoid).then_inc(sem("gate_ready"), 1)

            def load_gate(n):
                act.dma_start(stage[:, n % 2], gT_v[(n + KD) % N_GA]).then_inc(sem(f"gate_loaded{n % 2}"), 16)

            act.wait_ge(sem("or_lo"), 4)
            load_gate(0)
            load_gate(1)
            for n, d in enumerate((md9, md)):
                act.wait_ge(sem("m_diff"), n + 1)
                nc.scalar.activation(d[:], d[:], ACT.Exp, scale=-1.0).then_inc(sem("m_exp"), 1)
            gate(0)
            for n in range(1, N_GA):
                gate(n)
                if n <= 9:
                    t, w = n - 1, P if n < 9 else NS
                    act.wait_ge(sem("mm_om"), t + 1)
                    nc.scalar.activation(oah[:, :, t * P:t * P + w],
                                         bank[2 + t % 2][:, 0:2 * w].rearrange("p (c t) -> p c t", c=2), ACT.Copy)\
                        .then_inc(sem("oa_hi"), 1)
                act.wait_ge(sem("gated"), 3 * n)
                if n > KD:
                    nc.scalar.activation(ahi[:, n - 1 - KD], ym[:, n - 1 - KD], ACT.Copy).then_inc(sem("m_hi"), 1)
                if n + 1 < N_GA:
                    load_gate(n + 1)
            act.wait_ge(sem("gated"), 3 * N_GA)
            nc.scalar.activation(ahi[:, KD - 1], ym[:, KD - 1], ACT.Copy).then_inc(sem("m_hi"), 1)
            for k in range(KD):
                if k >= 2:
                    act.wait_ge(sem("o_added"), 3 * (k - 1))
                else:
                    act.wait_ge(sem("m_lo"), KD)
                act.dma_start(stage[:, k % 2], xT_c[k]).then_inc(sem(f"res_loaded{k % 2}"), 16)
                if k:
                    act.wait_ge(sem("o_added"), 3 * k)
                    act.dma_start(x1T[k - 1], xraw[:, k - 1]).then_inc(sem("x1_stored"), 16)
                    if k >= 3:
                        act.wait_ge(sem("n_added"), KD + k - 2)
                    nc.scalar.activation(ntmp[:, (k - 1) % 2], xraw[:, k - 1], ACT.Square).then_inc(sem("n_squared"), 1)
            act.wait_ge(sem("o_added"), 3 * KD)
            act.dma_start(x1T[KD - 1], xraw[:, KD - 1]).then_inc(sem("x1_stored"), 16)
            act.wait_ge(sem("n_added"), 2 * KD - 2)
            nc.scalar.activation(ntmp[:, 1], xraw[:, KD - 1], ACT.Square).then_inc(sem("n_squared"), 1)
            for n in range(3):
                act.wait_ge(sem("n_summed"), 3 + n + 1)
                nc.scalar.activation(nrt[:, n * PC:(n + 1) * PC], bank[2 + n][:, 0:PC], ACT.Sqrt, bias=eps_rms,
                                     scale=1.0 / D).then_inc(sem("n_root"), 1)
            for k in range(KD):
                act.wait_ge(sem("n_scaled"), KD + k + 1)
                nc.scalar.activation(ahi[:, k], xraw[:, k], ACT.Copy).then_inc(sem("a_hi"), 1)
            act.wait_ge(sem("x1_stored"), 16 * KD)
            act.wait_ge(sem("a_split"), 2 * KD)
            act.dma_start(cst8[:].rearrange("p c a b -> p (c a b)"), ins["sconvT"]).then_inc(sem("hist_loaded"), 16)
            conv_v = outs["convo"]

            def take(i, q):
                s, n = q // 3, q % 3
                if n == 0 and not (isinstance(i, int) and i == 0):
                    act.wait_ge(sem("u_conv"), 6 * i - 3 + 3 * s)
                    act.wait_ge(sem(f"row_stored{s}"), 16 * i)
                act.wait_ge(sem("mm_piece"), P_UP + 6 * i + q + 1)
                nc.scalar.activation(ug[:, s, 2 + n * PC:2 + (n + 1) * PC], bank[q % 2][:, 0:PC], ACT.Copy)\
                    .then_inc(sem(f"bank_free{q % 2}"), 1)
                if n == 2:
                    act.wait_ge(sem("bank_free0"), P_UP // 2 + 3 * i + (q + 2) // 2)
                    act.wait_ge(sem("bank_free1"), P_UP // 2 + 3 * i + (q + 1) // 2)
                    act.dma_start(conv_v[2 * i + s], ug[:, s, S:2 + T]).then_inc(sem(f"row_stored{s}"), 16)

            def high_part(i):
                act.wait_ge(sem("h_ready"), i + 1)
                nc.scalar.activation(hhi[:, bass.ds(i, 1)], cc[:, 1:2], ACT.Copy).then_inc(sem("h_hi"), 1)

            def store_low_part(i):
                act.wait_ge(sem("h_lo"), i + 1)
                act.dma_start(hloT[bass.ds(i, 1)], hlo_st[:, 0].bitcast(F32)).then_inc(sem("hlo_stored"), 16)

            def up_pair(i):
                first = isinstance(i, int)
                take(i, 0)
                if not first:
                    high_part(i - 1)
                take(i, 1)
                if not first:
                    store_low_part(i - 1)
                take(i, 2)
                take(i, 3)
                act.wait_ge(sem("u_conv"), 6 * i + 3)
                nc.scalar.activation(cc[:, 0], cc[:, 0], ACT.Silu).then_inc(sem("u_silu"), 1)
                take(i, 4)
                take(i, 5)

            peeled(act, KF, up_pair)
            high_part(KF - 1)
            store_low_part(KF - 1)
            act.wait_ge(sem("hlo_stored"), 16 * KF)
            act.wait_ge(sem("mm_piece"), P_DN)
            for s in range(2):
                act.wait_ge(sem(f"row_stored{s}"), 16 * KF)
            for n, (a, b) in enumerate(HLO_PARTS):
                act.dma_start(hlo[:, a:b].bitcast(F32), hloT[a:b].rearrange("c p t -> p c t"))\
                    .then_inc(sem(f"hlo_loaded{n}"), 16)
            for n in range(3 * KD):
                if n >= 2:
                    act.wait_ge(sem("y_ready2"), n - 1)
                act.dma_start(yrs[:, n % 2], x1T[n // 3, :, (n % 3) * PC:(n % 3 + 1) * PC]).then_inc(sem(f"yres_loaded{n % 2}"), 16)
                if n:
                    act.wait_ge(sem("y_ready2"), n)
                    act.dma_start(yT_c[(n - 1) // 3, :, ((n - 1) % 3) * PC:((n - 1) % 3 + 1) * PC], yst[:, (n - 1) % 2])\
                        .then_inc(sem(f"y_stored{(n - 1) % 2}"), 16)
            act.wait_ge(sem("y_ready2"), 24)
            act.dma_start(yT_c[KD - 1, :, 2 * PC:3 * PC], yst[:, 1]).then_inc(sem("y_stored1"), 16)
            for s in range(2):
                act.wait_ge(sem(f"y_stored{s}"), 16 * 12)

        @block.vector
        def _(dve):
            TT_ = nc.vector.tensor_tensor
            dve.wait_ge(sem("par_loaded"), 16)
            nc.vector.memset(nsum[:], 0.0).then_inc(sem("n_zero"), 1)
            dve.wait_ge(sem("n_zero"), 1)
            for k in range(KD):
                dve.wait_ge(sem("n_squared"), k + 1)
                if k:
                    dve.wait_ge(sem("n_added"), k)
                nc.vector.tensor_tensor(nsum[:], nsum[:], ntmp[:, k % 2], ALU.add).then_inc(sem("n_added"), 1)
            for n in range(3):
                dve.wait_ge(sem("n_root"), n + 1)
                nc.vector.reciprocal(nrs[:, n * PC:(n + 1) * PC], nrt[:, n * PC:(n + 1) * PC])\
                    .then_inc(sem("n_rstd"), 1)
            dve.wait_ge(sem("n_rstd"), 3)
            for k in range(KD):
                nc.vector.scalar_tensor_tensor(xraw[:, k], xraw[:, k], par1("g1", k), nrs[:], ALU.mult, ALU.mult)\
                    .then_inc(sem("n_scaled"), 1)
            for k in range(KD):
                dve.wait_ge(sem("a_hi"), k + 1)
                dve.wait_ge(sem("n_scaled"), k + 1)
                nc.vector.tensor_tensor(alo[:, k], xraw[:, k], ahi[:, k].bitcast(F32), ALU.subtract)\
                    .then_inc(sem("a_split"), 1)
            with dve.Fori(0, N_QK // 2) as i:
                for q in range(6):
                    s, n = q // 3, q % 3
                    dve.wait_ge(sem("q_root"), 6 * i + q + 1)
                    nc.vector.reciprocal(qrt[:, q], qrt[:, q]).then_inc(sem("q_rstd"), 1)
                    dve.wait_ge(sem("q_rstd"), 6 * i + q + 1)
                    piece = stage[:, s, n * PC:(n + 1) * PC]
                    nc.vector.scalar_tensor_tensor(piece, piece, par1("qkg", 2 * i + s), qrt[:, q],
                                                   ALU.mult, ALU.mult).then_inc(sem("q_scaled"), 1)


            linked = [0]

            def link(ins):
                linked[0] += 1
                ins.then_inc(sem("u_link"), 1)
                dve.wait_ge(sem("u_link"), linked[0])

            dve.wait_ge(sem("z_loaded"), 16 * (2 + 3 * 17))
            link(nc.vector.tensor_scalar(sq[:], sq[:], HD ** -0.5, None, ALU.mult))
            dve.wait_ge(sem("z_rows_stored"), 16 * 6)
            link(TT_(skc[:], skc[:], sq[:].unsqueeze(1).broadcast_to([96, 129, HD]), ALU.mult))
            link(nc.vector.tensor_reduce(ssc[:], skc[:], AX.X, ALU.add))
            link(nc.vector.memset(ssc[64:96, 32:128], NEG))
            nc.vector.tensor_reduce(snm[:, 0:1], ssc[:], AX.X, ALU.max, negate=True).then_inc(sem("z_max"), 1)
            dve.wait_ge(sem("z_exp"), 1)
            link(TT_(svc[:], svc[:], ssc[:].unsqueeze(2).broadcast_to([96, 129, HD]), ALU.mult))
            nc.vector.tensor_reduce(sso[:], svc[:].rearrange("p k j -> p j k"), AX.X, ALU.add).then_inc(sem("z_out"), 1)

            def wide(name, n=4, first=0):
                a = PAR[name][0] + first
                return par[:, a:a + n].unsqueeze(2).broadcast_to([P, n, P])

            def v4(t):
                return t.unsqueeze(2).broadcast_to([P, 4, P])

            dve.wait_ge(sem("stored0"), stored_before(B_GA, 0))
            dve.wait_ge(sem("stored1"), stored_before(B_GA, 0))
            dve.wait_ge(sem("v_stored"), 32 * G)
            nc.vector.memset(st[:], 0.0).then_inc(sem("s_zero"), 1)
            nc.vector.memset(sm[:], 0.0).then_inc(sem("s_zero"), 1)

            def kk_start(i):
                dve.wait_ge(sem("pool_next"), step("xs_ready", i))
                TT_(kkn[:], xs[:, 4:8], wide("kk"), ALU.mult).then_inc(sem("dve_next"), 1)

            def kk_finish(i):
                dve.wait_ge(sem("act_next"), step("kk_len", i))
                nc.vector.tensor_scalar(tmp[:], tmp[:], L2_EPS, None, ALU.max).then_inc(sem("dve_next"), 1)
                dve.wait_ge(sem("dve_next"), step("kk_clamped", i))
                nc.vector.reciprocal(tmp[:], tmp[:]).then_inc(sem("dve_next"), 1)
                dve.wait_ge(sem("dve_next"), step("kk_inv", i))
                TT_(kkn[:], kkn[:], tmp[:], ALU.mult).then_inc(sem("dve_next"), 1)

            def decay(i):
                dve.wait_ge(sem("act_next"), step("r_sgw", i))
                nc.vector.tensor_tensor_scan(cs[:].rearrange("p c t -> p (c t)"), C("scan", 0, 4 * P),
                                             sg[:, 0:4].rearrange("p c t -> p (c t)"), 0.0, ALU.mult, ALU.add)\
                    .then_inc(sem("dve_tile"), 1)
                dve.wait_ge(sem("dve_tile"), step("c_sum", i))
                nc.vector.tensor_copy(cm[:], cs[:, :, HD - 1]).then_inc(sem("dve_tile"), 1)
                dve.wait_ge(sem("dve_tile"), step("c_mid", i))
                TT_(cs[:], cs[:], v4(cm[:]), ALU.subtract).then_inc(sem("dve_tile"), 1)
                dve.wait_ge(sem("dve_tile"), step("c_ready", i))
                TT_(cp[:], cs[:], sg[:, 0:4], ALU.subtract).then_inc(sem("dve_tile"), 1)

            def tail(i):
                dve.wait_ge(sem("act_tile"), step("y_dev", i))
                nc.vector.reciprocal(ydev, ydev).then_inc(sem("dve_tail"), 1)
                dve.wait_ge(sem("dve_tail"), step("y_rstd", i))
                TT_(yc[:], yc[:], ydev, ALU.mult).then_inc(sem("dve_tail"), 1)
                dve.wait_ge(sem("dve_tail"), step("y_normed", i))
                for c in range(4):
                    last = nc.vector.tensor_scalar(yc[:, c], yc[:, c], par1("gng", c), par1("gnb", c),
                                                   ALU.mult, ALU.add)
                last.then_inc(sem("dve_tail"), 1)
                dve.wait_ge(sem("dve_tail"), step("y_gained", i))
                TT_(yc[:], yc[:], bon[:], ALU.add).then_inc(sem("dve_tail"), 1)
                dve.wait_ge(sem("dve_tail"), step("y_bonus", i))
                TT_(yc[:], yc[:], gg[:], ALU.mult).then_inc(sem("dve_tail"), 1)

            def rwkv(i, before=True, more=True):
                r, kr, v = xs[:, 0:4], xs[:, 4:8], xs[:, 8:12]
                dve.wait_ge(sem("act_next"), step("r_sga", i))
                dve.wait_ge(sem("dve_next"), step("kk_ready", i))
                TT_(bt[:], kkn[:], sg[:, 4:8], ALU.mult).then_inc(sem("dve_tile"), 1)
                nc.vector.scalar_tensor_tensor(kt[:], sg[:, 4:8], 1.0, wide("ka"), ALU.subtract, ALU.mult)\
                    .then_inc(sem("dve_tile"), 1)
                dve.wait_ge(sem("dve_tile"), step("k_gain", i))
                nc.vector.scalar_tensor_tensor(kt[:], kt[:], 1.0, kr, ALU.add, ALU.mult).then_inc(sem("dve_tile"), 1)
                dve.wait_ge(sem("dve_tile"), step("k_ready", i))
                TT_(tmp[:], r, kt[:], ALU.mult).then_inc(sem("dve_tile"), 1)
                dve.wait_ge(sem("dve_tile"), step("rk_raw", i))
                TT_(tmp[:], tmp[:], wide("rk"), ALU.mult).then_inc(sem("dve_tile"), 1)
                dve.wait_ge(sem("act_tile"), step("e_wi", i))
                dve.wait_ge(sem("dve_tile"), step("b_raw", i))
                TT_(bt[:], bt[:], ewi[:], ALU.mult).then_inc(sem("dve_tile"), 1)
                TT_(kt[:], kt[:], ewi[:], ALU.mult).then_inc(sem("dve_tile"), 1)
                dve.wait_ge(sem("act_tile"), step("e_wp", i))
                nc.vector.scalar_tensor_tensor(ar[:, :, 0], kkn[:], -1.0, ewp[:], ALU.mult, ALU.mult)\
                    .then_inc(sem("dve_tile"), 1)
                TT_(ar[:, :, 1], r, ew[:], ALU.mult).then_inc(sem("dve_tile"), 1)
                nc.vector.tensor_copy(wend[:], ew[:, :, P - 1]).then_inc(sem("dve_tile"), 1)
                if before:
                    tail(i - 1)
                dve.wait_ge(sem("pe_tile"), step("mm_bonus", i))
                TT_(bon[:], bank[5][:].rearrange("p (c t) -> p c t", c=4), v, ALU.mult).then_inc(sem("dve_tile"), 1)
                dve.wait_ge(sem("act_tile"), step("e_wm", i))
                dve.wait_ge(sem("s_zero"), 2)
                for hh in range(2):
                    q = slice(hh * HD, (hh + 1) * HD)
                    last = TT_(sm[q, :, q], st[q, :, q], wm[q].unsqueeze(2).broadcast_to([HD, 4, HD]), ALU.mult)
                last.then_inc(sem("dve_tile"), 1)
                mask = cst[:, CST["su"][0]:CST["su"][0] + 2 * P].unsqueeze(1).broadcast_to([P, 2, 2 * P])
                for dst, name, banks in ((gq, "mm_gq", (4, 5, 6, 7)), (nq, "mm_nq", (2, 3, 4, 5))):
                    for n, b in enumerate(banks):
                        dve.wait_ge(sem(name), 4 * i + n + 1)
                        TT_(dst[:, 2 * n:2 * n + 2].rearrange("p h a t -> p h (a t)"),
                            bank[b][:].rearrange("p (h x) -> p h x", h=2), mask, ALU.mult)\
                            .then_inc(sem(name + "_out"), 1)
                for g in range(2):
                    hs = slice(4 * g, 4 * g + 4)
                    dve.wait_ge(sem("mm_nq_out"), 4 * i + 2 * g + 2)
                    TT_(tt[:, hs], nq[:, hs, 0], C("lv0t").unsqueeze(1).broadcast_to([P, 4, P]), ALU.mult)\
                        .then_inc(sem("tt_low"), 1)
                    dve.wait_ge(sem("tt_low"), 2 * i + g + 1)
                    TT_(tt[:, hs], tt[:, hs], C("ident").unsqueeze(1).broadcast_to([P, 4, P]), ALU.add)\
                        .then_inc(sem(f"tt_ready{g}"), 1)
                for g in range(2):
                    dve.wait_ge(sem(f"mm_t{g}"), 6 * i + 1)
                    nc.vector.tensor_copy(ti[:, 4 * g:4 * g + 4], bank[2 + g][:].rearrange("p (h t) -> p h t", h=4))\
                        .then_inc(sem(f"t_ready{g}"), 1)
                for lv in range(6):
                    if lv == 4 and more:
                        kk_start(i + 1)
                    for g in range(2):
                        hs = slice(4 * g, 4 * g + 4)
                        dve.wait_ge(sem(f"mm_x{g}"), 6 * i + lv + 1)
                        TT_(xx[:, hs], bank[4 + g][:].rearrange("p (h t) -> p h t", h=4),
                            C("lvl", lv * P).unsqueeze(1).broadcast_to([P, 4, P]), ALU.mult)\
                            .then_inc(sem(f"x_ready{g}"), 1)
                    for g in range(2):
                        hs = slice(4 * g, 4 * g + 4)
                        if lv < 5:
                            dve.wait_ge(sem(f"mm_t{g}"), 6 * i + lv + 2)
                            TT_(ti[:, hs], ti[:, hs], bank[2 + g][:].rearrange("p (h t) -> p h t", h=4), ALU.add)\
                                .then_inc(sem(f"t_ready{g}"), 1)
                        dve.wait_ge(sem(f"mm_tt{g}"), 6 * i + lv + 1)
                        TT_(tt[:, hs], tt[:, hs], bank[6 + g][:].rearrange("p (h t) -> p h t", h=4), ALU.add)\
                            .then_inc(sem(f"tt_ready{g}"), 1)
                if more:
                    kk_finish(i + 1)
                dve.wait_ge(sem("pe_tile"), step("mm_s", i))
                dve.wait_ge(sem("dve_tile"), step("sm_ready", i))
                for hh in range(2):
                    q = slice(hh * HD, (hh + 1) * HD)
                    last = TT_(st[q, :, q], sm[q, :, q],
                               bank[6][q].rearrange("p (c t) -> p c t", c=4)[:, :, q], ALU.add)
                last.then_inc(sem("dve_tile"), 1)
                dve.wait_ge(sem("dve_tile"), step("s_sum", i))
                for hh in range(2):
                    q = slice(hh * HD, (hh + 1) * HD)
                    last = TT_(st[q, :, q], st[q, :, q], wend[q].unsqueeze(2).broadcast_to([HD, 4, HD]), ALU.mult)
                last.then_inc(sem("dve_tile"), 1)
                dve.wait_ge(sem("pe_tile"), step("mm_mean", i))
                dve.wait_ge(sem("o_free"), 16 * i + 16)
                nc.vector.scalar_tensor_tensor(yc[:], bank[5][:].rearrange("p (c t) -> p c t", c=4), -1.0 / HD, yv[:],
                                               ALU.mult, ALU.add).then_inc(sem("dve_tile"), 1)

            kk_start(0)
            kk_finish(0)
            decay(0)
            rwkv(0, before=False)
            with dve.Fori(1, NT - 1) as i:
                decay(i)
                rwkv(i)
            decay(NT - 1)
            rwkv(NT - 1, more=False)
            tail(NT - 1)

            def wide8(name, n=4):
                a = PAR[name][0]
                return par[:, a:a + n].unsqueeze(2).broadcast_to([P, n, NS])

            x8 = xs[:, :, 0:NS]
            dve.wait_ge(sem("u_loaded"), 32)
            link(TT_(x8, pin[:, :, 0:NS], pin[:, :, NS:2 * NS], ALU.subtract))
            link(TT_(x8, x8, wide8("mu", N_RW), ALU.mult))
            TT_(x8, x8, pin[:, :, NS:2 * NS], ALU.add).then_inc(sem("u_xs"), 1)
            dve.wait_ge(sem("u_xs"), 1)
            r8, k8, v8 = x8[:, 0:4], x8[:, 4:8], x8[:, 8:12]
            TT_(s4[:, 3], k8, wide8("kk"), ALU.mult).then_inc(sem("u_kk"), 1)
            dve.wait_ge(sem("u_kk"), 1)
            TT_(s4[:, 0], s4[:, 3], s4[:, 3], ALU.mult).then_inc(sem("u_kk"), 1)
            dve.wait_ge(sem("u_len"), 1)
            link(nc.vector.tensor_scalar(s4[:, 7], s4[:, 7], L2_EPS, None, ALU.max))
            link(nc.vector.reciprocal(s4[:, 7], s4[:, 7]))
            link(TT_(s4[:, 3], s4[:, 3], s4[:, 7], ALU.mult))
            dve.wait_ge(sem("u_sg"), 8)
            link(TT_(s4[:, 4], s4[:, 3], ssg[:, 4:8], ALU.mult))
            link(nc.vector.tensor_scalar(s4[:, 3], s4[:, 3], -1.0, None, ALU.mult))
            link(nc.vector.scalar_tensor_tensor(s4[:, 2], ssg[:, 4:8], 1.0, wide8("ka"), ALU.subtract, ALU.mult))
            link(nc.vector.scalar_tensor_tensor(s4[:, 2], s4[:, 2], 1.0, k8, ALU.add, ALU.mult))
            link(nc.vector.tensor_copy(s4[:, 0], r8))
            link(nc.vector.tensor_copy(s4[:, 5], v8))
            link(TT_(s4[:, 11], r8, s4[:, 2], ALU.mult))
            TT_(s4[:, 11], s4[:, 11], wide8("rk"), ALU.mult).then_inc(sem("u_vectors"), 1)
            dve.wait_ge(sem("u_spread"), 16 * 12)
            dve.wait_ge(sem("u_state"), 16)
            at_step = [0]

            def rec(ins):
                at_step[0] += 1
                ins.then_inc(sem("u_step"), 1)
                dve.wait_ge(sem("u_step"), at_step[0])

            def cols(q):
                return srow[:, q].unsqueeze(1).broadcast_to([P, 32, HD])

            rec(TT_(stp[:], sst[:], cols(3), ALU.mult))
            rec(nc.vector.tensor_reduce(ssa[:], stp[:], AX.X, ALU.add))
            rec(TT_(sst[:], sst[:], cols(1), ALU.mult))
            rec(TT_(stp[:], ssa[:].unsqueeze(2).broadcast_to([P, 32, HD]), cols(4), ALU.mult))
            rec(TT_(sst[:], sst[:], stp[:], ALU.add))
            for half in range(2):
                q = slice(half * HD, (half + 1) * HD)
                ins = TT_(stp[q], srow[q, 5, half * 32:(half + 1) * 32].unsqueeze(2).broadcast_to([HD, 32, HD]),
                          srow[q, 2].unsqueeze(1).broadcast_to([HD, 32, HD]), ALU.mult)
            rec(ins)
            rec(TT_(sst[:], sst[:], stp[:], ALU.add))
            rec(TT_(stp[:], sst[:], cols(0), ALU.mult))
            rec(nc.vector.tensor_reduce(syo[:], stp[:], AX.X, ALU.add))
            dve.wait_ge(sem("u_y"), 1)
            dve.wait_ge(sem("pe_sample"), step("mm_umean", 0))
            c4 = lambda b: bank[b][:, 0:4 * NS].rearrange("p (c t) -> p c t", c=4)
            nc.vector.scalar_tensor_tensor(s4[:, 9], c4(3), -1.0 / HD, s4[:, 8], ALU.mult, ALU.add)\
                .then_inc(sem("u_centred"), 1)
            dve.wait_ge(sem("u_centred"), 1)
            TT_(s4[:, 0], s4[:, 9], s4[:, 9], ALU.mult).then_inc(sem("u_centred"), 1)
            dve.wait_ge(sem("u_dev"), 1)
            link(nc.vector.reciprocal(s4[:, 10], s4[:, 10]))
            link(TT_(s4[:, 9], s4[:, 9], s4[:, 10], ALU.mult))
            link(TT_(s4[:, 9], s4[:, 9], wide8("gng"), ALU.mult))
            link(TT_(s4[:, 9], s4[:, 9], wide8("gnb"), ALU.add))
            dve.wait_ge(sem("pe_sample"), step("mm_ubonus", 0))
            link(TT_(s4[:, 11], c4(5), v8, ALU.mult))
            link(TT_(s4[:, 9], s4[:, 9], s4[:, 11], ALU.add))
            TT_(s4[:, 9], s4[:, 9], s4[:, 6], ALU.mult).then_inc(sem("u_out"), 1)
            dve.wait_ge(sem("uo_stored"), 16)
            dve.wait_ge(sem("wkvs_stored"), 16)

            nc.vector.memset(qz[:], 0.0).then_inc(sem("qz_zero"), 1)

            def begin(g, i, s):
                u, prev = 8 * g + 2 * i + s, has_previous(g, i, s)
                half = slice(0, 2) if prev else slice(1, 2)
                dve.wait_ge(sem("mm_score"), u + 1)
                if not (isinstance(u, int) and u < 2):
                    dve.wait_ge(sem("mm_pt"), u - 1)
                m = "cur2" if g == 2 else "cur"
                nc.vector.scalar_tensor_tensor(
                    sc[:, s, :, 1], bank[2][:].rearrange("p (h t) -> p h t", h=H), HD ** -0.5,
                    C(m).unsqueeze(1).broadcast_to([P, H, P]), ALU.mult, ALU.add).then_inc(sem("a_masked"), 1)
                if prev:
                    nc.vector.scalar_tensor_tensor(
                        sc[:, s, :, 0], bank[3][:].rearrange("p (h t) -> p h t", h=H), HD ** -0.5,
                        C("prev").unsqueeze(1).broadcast_to([P, H, P]), ALU.mult, ALU.add).then_inc(sem("a_masked"), 1)
                else:
                    dve.sem_inc(sem("a_masked"), 1)
                dve.wait_ge(sem("a_masked"), 2 * u + 2)
                dve.wait_ge(sem(f"ao_stored{s}"), 16 * (4 * g + (i if g < 2 else 2 * i)))
                nc.vector.tensor_reduce(ob[:, s, 256:260], sc[:, s, :, half], AX.XY, ALU.max, negate=True)\
                    .then_inc(sem("a_max"), 1)

            def finish(g, i, s):
                u = 8 * g + 2 * i + s
                if has_previous(g, i, s):
                    dve.wait_ge(sem("mm_pt"), u + 1)
                    nc.vector.tensor_copy(pt[:, s, 0], bank[5][:].rearrange("p (h t) -> p h t", h=H))\
                        .then_inc(sem("a_pt_prev"), 1)
                else:
                    dve.sem_inc(sem("a_pt_prev"), 1)
                dve.wait_ge(sem("mm_att"), u + 1)
                nc.vector.tensor_copy(ob[:, s, 0:256], bank[6][:, 0:256]).then_inc(sem("a_out"), 1)

            for g in range(G):
                units(dve, g, begin, finish)
                if g < 2:
                    for c in (2 * g, 2 * g + 1):
                        dve.wait_ge(sem("or_hi"), c + 1)
                        TT_(orl[:, c], stage[:, c % 2], orh[:, c].bitcast(F32), ALU.subtract)\
                            .then_inc(sem("or_lo"), 1)
            def weights(n, m, d, x, shape):
                nm, den = m[:, :, :, 256:260], m[:, :, :, 260:264]
                link(nc.vector.tensor_reduce(x[:, 0], nm.rearrange("p t g h -> p t h g"), AX.X, ALU.min))
                TT_(d[:], nm, x[:, 0].unsqueeze(2).broadcast_to(shape), ALU.subtract).then_inc(sem("m_diff"), 1)
                dve.wait_ge(sem("m_exp"), n + 1)
                link(TT_(den, den, d[:], ALU.mult))
                link(nc.vector.tensor_reduce(x[:, 0], den.rearrange("p t g h -> p t h g"), AX.X, ALU.add))
                link(nc.vector.reciprocal(x[:, 1], x[:, 0]))
                link(TT_(d[:], d[:], x[:, 1].unsqueeze(2).broadcast_to(shape), ALU.mult))

            def merge(t):
                s, w = t % 2, P if t < NT else NS
                rows_, d = (mo[:, t], md[:, t]) if t < NT else (mo9[:, 0], md9[:, 0])
                o = rows_[:, :, 0:256]
                o4 = o.rearrange("p g (h j) -> p g h j", h=H)
                link(TT_(o4, o4, d.unsqueeze(3).broadcast_to([w, G, H, HD]), ALU.mult))
                if t >= 2:
                    dve.wait_ge(sem("mm_om"), t - 1)
                link(TT_(om[0:w, s], o[:, 0], o[:, 1], ALU.add))
                TT_(om[0:w, s], om[0:w, s], o[:, 2], ALU.add).then_inc(sem("m_sum"), 1)

            def attention_low(t):
                w = P if t < NT else NS
                dve.wait_ge(sem("oa_hi"), t + 1)
                TT_(oal[:, :, t * P:t * P + w], bank[2 + t % 2][:, 0:2 * w].rearrange("p (c t) -> p c t", c=2),
                    oah[:, :, t * P:t * P + w].bitcast(F32), ALU.subtract).then_inc(sem("oa_lo"), 1)

            def gated(n):
                k, s = n % KD, n % 2
                dve.wait_ge(sem("gate_ready"), n + 1)
                for c in range(3):
                    q = 3 * n + c
                    dve.wait_ge(sem("mm_piece"), P_RO + q + 1)
                    piece = ym[:, k, c * PC:(c + 1) * PC]
                    gate = stage[:, s, c * PC:(c + 1) * PC]
                    if n < KD:
                        TT_(piece, bank[q % 2][:, 0:PC], gate, ALU.mult).then_inc(sem("gated"), 1)
                        dve.wait_ge(sem("gated"), q + 1)
                        dve.sem_inc(sem(f"bank_free{q % 2}"), 1)
                    else:
                        TT_(gate, bank[q % 2][:, 0:PC], gate, ALU.mult).then_inc(sem(f"bank_free{q % 2}"), 1)
                        dve.wait_ge(sem(f"bank_free{q % 2}"), (P_RO + q) // 2 + 1)
                        TT_(piece, piece, gate, ALU.add).then_inc(sem("gated"), 1)

            def merged_low(k):
                dve.wait_ge(sem("m_hi"), k + 1)
                TT_(alo[:, k], ym[:, k], ahi[:, k].bitcast(F32), ALU.subtract).then_inc(sem("m_lo"), 1)

            dve.wait_ge(sem("mo9_loaded"), 16)
            weights(0, mo9, md9, mn9, [NS, 1, G, H])
            dve.wait_ge(sem("mo_loaded"), 16 * G)
            weights(1, mo, md, mn, [P, NT, G, H])
            for t in range(9):
                if t < KD:
                    gated(t)
                merge(t)
                if t:
                    attention_low(t - 1)
            attention_low(8)
            for n in range(KD, N_GA):
                gated(n)
                if n > KD:
                    merged_low(n - 1 - KD)
            merged_low(KD - 1)
            dve.wait_ge(sem("m_lo"), KD)
            nc.vector.memset(nsum[:], 0.0).then_inc(sem("n_zero"), 1)
            for k in range(KD):
                dve.wait_ge(sem(f"res_loaded{k % 2}"), 16 * (k // 2 + 1))
                for c in range(3):
                    q = 3 * k + c
                    dve.wait_ge(sem("mm_piece"), P_WO + q + 1)
                    TT_(xraw[:, k, c * PC:(c + 1) * PC], bank[q % 2][:, 0:PC], stage[:, k % 2, c * PC:(c + 1) * PC],
                        ALU.add).then_inc(sem("o_added"), 1)
                    dve.wait_ge(sem("o_added"), q + 1)
                    dve.sem_inc(sem(f"bank_free{q % 2}"), 1)
                if k:
                    dve.wait_ge(sem("n_squared"), KD + k)
                    dve.wait_ge(sem("n_zero"), 2)
                    if k > 1:
                        dve.wait_ge(sem("n_added"), KD + k - 1)
                    TT_(nsum[:], nsum[:], ntmp[:, (k - 1) % 2], ALU.add).then_inc(sem("n_added"), 1)
            dve.wait_ge(sem("n_squared"), 2 * KD)
            dve.wait_ge(sem("n_added"), 2 * KD - 1)
            TT_(nsum[:], nsum[:], ntmp[:, 1], ALU.add).then_inc(sem("n_added"), 1)
            dve.wait_ge(sem("bank_free0"), P_UP // 2)
            dve.wait_ge(sem("bank_free1"), P_UP // 2)
            for n in range(3):
                dve.wait_ge(sem("n_root"), 3 + n + 1)
                nc.vector.reciprocal(nrs[:, n * PC:(n + 1) * PC], nrt[:, n * PC:(n + 1) * PC])\
                    .then_inc(sem("n_rstd"), 1)
            dve.wait_ge(sem("n_rstd"), 6)
            dve.wait_ge(sem("x1_stored"), 16 * KD)
            for k in range(KD):
                nc.vector.scalar_tensor_tensor(xraw[:, k], xraw[:, k], par1("g2", k), nrs[:], ALU.mult, ALU.mult)\
                    .then_inc(sem("n_scaled"), 1)
            for k in range(KD):
                dve.wait_ge(sem("a_hi"), KD + k + 1)
                dve.wait_ge(sem("n_scaled"), KD + k + 1)
                TT_(alo[:, k], xraw[:, k], ahi[:, k].bitcast(F32), ALU.subtract).then_inc(sem("a_split"), 1)
            dve.wait_ge(sem("a_split"), 2 * KD)
            nc.vector.memset(ug[:, :, 0:2], 0.0).then_inc(sem("hist_zero"), 1)
            dve.wait_ge(sem("hist_zero"), 1)
            dve.wait_ge(sem("hist_loaded"), 16)
            def low_part(i):
                dve.wait_ge(sem("h_hi"), i + 1)
                if not (isinstance(i, int) and i == 0):
                    dve.wait_ge(sem("hlo_stored"), 16 * i)
                TT_(hlo_st[:], cc[:, 1:2], hhi[:, bass.ds(i, 1)].bitcast(F32), ALU.subtract).then_inc(sem("h_lo"), 1)

            def up_pair(i):
                for s in range(2):
                    dve.wait_ge(sem("bank_free0"), P_UP // 2 + 3 * i + 2 + s)
                    dve.wait_ge(sem("bank_free1"), P_UP // 2 + 3 * i + 1 + 2 * s)
                    w = [par1(f"cw{n}", 2 * i + s) for n in range(3)]
                    hist = cst8[:, bass.ds(2 * i + s, 1)].rearrange("p o a b -> p (o a) b")
                    c, u8 = cc[:, s], ug[:, s, 2 + S:2 + T]
                    nc.vector.tensor_scalar(c, ug[:, s, 2:2 + T], w[2], par1("cb", 2 * i + s), ALU.mult, ALU.add)\
                        .then_inc(sem("u_conv"), 1)
                    dve.wait_ge(sem("u_conv"), 6 * i + 3 * s + 1)
                    nc.vector.scalar_tensor_tensor(c[:, 0:S], ug[:, s, 1:1 + S], w[1], c[:, 0:S], ALU.mult, ALU.add)\
                        .then_inc(sem("u_tap"), 1)
                    nc.vector.scalar_tensor_tensor(c[:, S:T], hist[:, 1], w[1], c[:, S:T], ALU.mult, ALU.add)\
                        .then_inc(sem("u_conv"), 1)
                    dve.wait_ge(sem("u_tap"), 2 * i + s + 1)
                    dve.wait_ge(sem("u_conv"), 6 * i + 3 * s + 2)
                    nc.vector.scalar_tensor_tensor(c[:, 0:S], ug[:, s, 0:S], w[0], c[:, 0:S], ALU.mult, ALU.add)\
                        .then_inc(sem("u_tap2"), 1)
                    dve.wait_ge(sem("u_tap2"), 2 * i + s + 1)
                    nc.vector.scalar_tensor_tensor(c[:, S:T], hist[:, 0], w[0], c[:, S:T], ALU.mult, ALU.add)\
                        .then_inc(sem("u_conv"), 1)
                dve.wait_ge(sem("u_conv"), 6 * i + 6)
                dve.wait_ge(sem("u_silu"), i + 1)
                TT_(cc[:, 1], cc[:, 0], cc[:, 1], ALU.mult).then_inc(sem("h_ready"), 1)

            up_pair(0)
            low_part(0)
            up_pair(1)
            with dve.Fori(2, KF) as i:
                low_part(i - 1)
                up_pair(i)
            low_part(KF - 1)
            for n in range(3 * KD):
                o = n // 3
                dve.wait_ge(sem(f"yres_loaded{n % 2}"), 16 * (n // 2 + 1))
                if n >= 2:
                    dve.wait_ge(sem(f"y_stored{n % 2}"), 16 * (n // 2))
                dve.wait_ge(sem("mm_down"), 3 * o + 3)
                TT_(yst[:, n % 2], bank[3 * (o % 2) + n % 3][:, 0:PC], yrs[:, n % 2], ALU.add)\
                    .then_inc(sem("y_ready2"), 1)

        @block.tensor
        def _(pe):
            pe.wait_ge(sem("cst_loaded"), 16)
            pe.wait_ge(sem("n_added"), KD)
            for n in range(3):
                pe.matmul(bank[n][:, 0:PC], C("mones"), nsum[:, n * PC:(n + 1) * PC], start=True, stop=True)\
                    .then_inc(sem("n_summed"), 1)
            pe.wait_ge(sem("a_split"), KD)
            pe.wait_ge(sem("n_root"), 3)

            parts = ((0, 0), (0, 1), (1, 0))
            wpart, apart = (whi, wlo), (ahi, alo)

            def rows_piece(s, n, out):
                for k in range(KD):
                    for a, b in parts:
                        last = pe.matmul(out[:, 0:PC], wpart[a][:, s, k], apart[b][:, k, n * PC:(n + 1) * PC],
                                         start=(k == 0 and (a, b) == (0, 0)), stop=(k == KD - 1 and a == 1))
                last.then_inc(sem("mm_piece"), 1)

            def rows(base, pbase, count):
                def pair(i):
                    for s in range(2):
                        pe.wait_ge(sem("w_split"), base + 2 * i + s + 1)
                        for n in range(3):
                            q = 3 * s + n
                            pe.wait_ge(sem(f"bank_free{q % 2}"), pbase // 2 + 3 * i + q // 2)
                            rows_piece(s, n, bank[q % 2])

                with pe.Fori(0, count // 2) as i:
                    pair(i)

            def head_sums(i, q):
                pe.wait_ge(sem("q_squared"), 6 * i + q + 1)
                pe.matmul(bank[2 + q % 2][:, 0:PC], C("bd"), qsq[:, q % 2], start=True, stop=True)\
                    .then_inc(sem("q_summed"), 1)

            def qk_pair(i):
                for s in range(2):
                    pe.wait_ge(sem("w_split"), B_QK + 2 * i + s + 1)
                    for n in range(3):
                        q = 3 * s + n
                        pe.wait_ge(sem(f"bank_free{q % 2}"), 3 * B_QK // 2 + 3 * i + q // 2)
                        rows_piece(s, n, bank[q % 2])
                        if q:
                            head_sums(i, q - 1)
                head_sums(i, 5)

            peeled(pe, N_QK // 2, qk_pair)
            pe.wait_ge(sem("q_root"), 3 * N_QK)
            with pe.Fori(0, G) as i:
                for s in range(2):
                    pe.wait_ge(sem("w_split"), B_V + 2 * i + s + 1)
                    for t in range(9):
                        a0, w = P * t, P if t < 8 else NS
                        if s == 0 and t % 2 == 0:
                            q = t // 2
                            pe.wait_ge(sem(f"bank_free{q % 2}"), 3 * B_V // 2 + 3 * i - 2 + q // 2)
                            if t == 8:
                                pe.wait_ge(sem("bank_free1"), 3 * B_V // 2 + 3 * i)
                        for k in range(4):
                            for a, b in parts:
                                last = pe.matmul(bank[2 + t // 2][0:w, (t % 2) * 256:(t % 2 + 1) * 256],
                                                 apart[b][:, 4 * s + k, a0:a0 + w],
                                                 wpart[a][:, s, 2 * k:2 * k + 2].rearrange("p a c -> p (a c)"),
                                                 start=(s == 0 and k == 0 and (a, b) == (0, 0) and t % 2 == 0),
                                                 stop=(s == 1 and k == 3 and a == 1 and (t % 2 == 1 or t == 8)),
                                                 skip_group_check=True)
                        if t in (3, 7, 8):
                            last.then_inc(sem("mm_piece"), 1)

            rows(B_RW, 3 * B_RW, N_RW)

            def slot(h):
                return 4 * (h // 4) + 2 * (h % 2) + (h // 2) % 2

            def gates(i, q):
                s = q // 3
                if q % 3 == 0:
                    pe.wait_ge(sem("w_split"), B_GA + 2 * i + s + 1)
                pe.wait_ge(sem(f"bank_free{q % 2}"), 3 * B_GA // 2 + 3 * i + q // 2)
                rows_piece(s, q % 3, bank[q % 2])

            f = slice(0, HD), slice(HD, P)

            def kk_sums(i):
                pe.wait_ge(sem("act_next"), step("kk_squared", i))
                pe.matmul(bank[7][:], C("bd"), tmp[:].rearrange("p c t -> p (c t)"), start=True, stop=True)\
                    .then_inc(sem("pe_next"), 1)

            def loras(i, which):
                pe.wait_ge(sem("act_next"), step("r_sgl", i))
                for n in which:
                    w, rhs = ((lora[f[0], 0], xs[f[0], 12]), (lora[f[1], 0], xs[f[1], 12]), (lora[:, 1], sg[:, 8]))[n]
                    for c in range(4):
                        last = pe.matmul(bank[2 + n][:, c * P:(c + 1) * P], w[:, c * P:(c + 1) * P], rhs,
                                         start=True, stop=True)
                    last.then_inc(sem("pe_next"), 1)

            def rwkv(i, more):
                gates(i, 0)
                for c in range(4):
                    last = pe.transpose(bank[6][:, c * P:(c + 1) * P], xs[:, 8 + c], C("ident"))
                last.then_inc(sem("mm_turn"), 1)
                gates(i, 1)
                gates(i, 2)
                pe.wait_ge(sem("dve_tile"), step("rk_ready", i))
                pe.matmul(bank[5][:], C("bd"), tmp[:].rearrange("p c t -> p (c t)"), start=True, stop=True)\
                    .then_inc(sem("pe_tile"), 1)
                gates(i, 3)
                pe.wait_ge(sem("dve_tile"), step("at_ready", i))
                for c in range(4):
                    last = pe.transpose(bank[7][:, c * P:(c + 1) * P], ar[:, c, 0], C("ident"))
                last.then_inc(sem("mm_turn"), 1)
                for c in range(4):
                    last = pe.transpose(bank[2][:, c * P:(c + 1) * P], bt[:, c], C("ident"))
                last.then_inc(sem("mm_turn"), 1)
                for c in range(4):
                    last = pe.transpose(bank[3][:, c * P:(c + 1) * P], kt[:, c], C("ident"))
                last.then_inc(sem("mm_turn"), 1)
                pe.wait_ge(sem("dve_tile"), step("rt_ready", i))
                pe.wait_ge(sem("act_tile"), step("r_gate", i))
                for src, name, banks in ((kt, "mm_gq", (4, 5, 6, 7)), (bt, "mm_nq", (2, 3, 4, 5))):
                    for n in range(2):
                        if name == "mm_gq":
                            pe.wait_ge(*((sem("dve_tile"), step("rk_summed", i)) if n == 0 else (sem("turned"), 4 * i + 2)))
                        else:
                            pe.wait_ge(sem("turned" if n == 0 else "mm_gq_out"), 4 * i + (4 if n == 0 else 2))
                        for h in (4 * n, 4 * n + 1, 4 * n + 2, 4 * n + 3):
                            b = banks[2 * n + h % 2]
                            c = (h // 2) % 2
                            last = pe.matmul(bank[b][:, 2 * P * c:2 * P * (c + 1)], src[f[h % 2], h // 2],
                                             ar[f[h % 2], h // 2].rearrange("p a t -> p (a t)"),
                                             start=True, stop=True)
                            if c:
                                last.then_inc(sem(name), 1)
                for g in range(2):
                    pe.wait_ge(sem(f"tt_ready{g}"), 7 * i + 1)
                    for h in range(4):
                        last = pe.transpose(bank[2 + g][:, h * P:(h + 1) * P], tt[:, 4 * g + h], C("ident"))
                    last.then_inc(sem(f"mm_t{g}"), 1)
                for lv in range(6):
                    for g in range(2):
                        pe.wait_ge(sem(f"t_ready{g}"), 6 * i + lv + 1)
                        if lv == 0:
                            pe.wait_ge(sem("mm_nq_out"), 4 * i + 4)
                        for h in range(4):
                            last = pe.matmul(bank[4 + g][:, h * P:(h + 1) * P], nq[:, 4 * g + h, 0], ti[:, 4 * g + h],
                                             start=True, stop=True)
                        last.then_inc(sem(f"mm_x{g}"), 1)
                    for g in range(2):
                        pe.wait_ge(sem(f"x_ready{g}"), 6 * i + lv + 1)
                        pe.wait_ge(sem(f"tt_ready{g}"), 7 * i + lv + 1)
                        if lv < 5:
                            for h in range(4):
                                last = pe.matmul(bank[2 + g][:, h * P:(h + 1) * P], tt[:, 4 * g + h], xx[:, 4 * g + h],
                                                 start=True, stop=True)
                            last.then_inc(sem(f"mm_t{g}"), 1)
                        for h in range(4):
                            last = pe.matmul(bank[6 + g][:, h * P:(h + 1) * P], xx[:, 4 * g + h], tt[:, 4 * g + h],
                                             start=True, stop=True)
                        last.then_inc(sem(f"mm_tt{g}"), 1)
                for g in range(2):
                    pe.wait_ge(sem(f"tt_ready{g}"), 7 * i + 7)
                for h in range(RH):
                    last = pe.matmul(bank[2][f[h % 2], (h // 2) * P:(h // 2 + 1) * P], atm[:, h * HD:(h + 1) * HD],
                                     tt[:, slot(h)], start=True, stop=True)
                last.then_inc(sem("pe_tile"), 1)
                for h in range(RH):
                    last = pe.matmul(bank[3][:, h * HD:(h + 1) * HD], gq[:, slot(h), 0], vtm[:, h * HD:(h + 1) * HD],
                                     start=True, stop=True)
                last.then_inc(sem("pe_tile"), 1)
                if more:
                    kk_sums(i + 1)
                pe.wait_ge(sem("act_tile"), step("gv_ready", i))
                for h in range(RH):
                    pe.matmul(bank[4][:, h * HD:(h + 1) * HD], tt[:, slot(h)], gv[:, h * HD:(h + 1) * HD],
                              start=(h == 0), stop=False, skip_group_check=True)
                pe.wait_ge(sem("act_tile"), step("p1_ready", i))
                pe.wait_ge(sem("dve_tile"), step("sm_ready", i))
                for c in range(4):
                    last = pe.matmul(bank[4][:, c * P:(c + 1) * P], p1[:, c], sm[:, c], start=False, stop=(c == 3),
                                     skip_group_check=True)
                last.then_inc(sem("pe_tile"), 1)
                if more:
                    loras(i + 1, (0, 1))
                for c in range(4):
                    pe.matmul(bank[5][:, c * P:(c + 1) * P], sm[:, c], ar[:, c, 1], start=(c == 0), stop=False,
                              skip_group_check=True)
                for h in range(RH):
                    pe.matmul(bank[5][f[h % 2], (h // 2) * P:(h // 2 + 1) * P], vtm[:, h * HD:(h + 1) * HD],
                              gq[:, slot(h), 1], start=False, stop=False, skip_group_check=True)
                for c in range(4):
                    pe.matmul(bank[6][:, c * P:(c + 1) * P], ktm[:, c * P:(c + 1) * P], vtm[:, c * P:(c + 1) * P],
                              start=(c == 0), stop=False, skip_group_check=True)
                pe.wait_ge(sem("act_tile"), step("u_ready", i))
                for c in range(4):
                    last = pe.matmul(bank[6][:, c * P:(c + 1) * P], btm[:, c * P:(c + 1) * P],
                                     uu[:, c * P:(c + 1) * P], start=False, stop=(c == 3), skip_group_check=True)
                last.then_inc(sem("pe_tile"), 1)
                for h in range(RH):
                    last = pe.matmul(bank[5][f[h % 2], (h // 2) * P:(h // 2 + 1) * P], uu[:, h * HD:(h + 1) * HD],
                                     nq[:, slot(h), 1], start=False, stop=(h == RH - 1), skip_group_check=True)
                last.then_inc(sem("pe_tile"), 1)
                if more:
                    loras(i + 1, (2,))
                gates(i, 4)
                pe.wait_ge(sem("act_tile"), step("y_ready", i))
                pe.matmul(bank[5][:], C("bd"), yv[:].rearrange("p c t -> p (c t)"), start=True, stop=True)\
                    .then_inc(sem("pe_tile"), 1)
                pe.wait_ge(sem("act_tile"), step("y_squared", i))
                pe.matmul(bank[7][:], C("bd"), ysq.rearrange("p c t -> p (c t)"), start=True, stop=True)\
                    .then_inc(sem("pe_tile"), 1)
                gates(i, 5)

            kk_sums(0)
            loras(0, (0, 1, 2))
            with pe.Fori(0, NT - 1) as i:
                rwkv(i, True)
            rwkv(NT - 1, False)
            pe.wait_ge(sem("u_tanh"), 1)
            pe.wait_ge(sem("u_sgl"), 1)
            pe.wait_ge(sem("act_tile"), step("y_dev", NT - 1))
            f = slice(0, HD), slice(HD, P)
            for n, (w, rhs) in enumerate(((lora[f[0], 0], xs[f[0], 12, 0:NS]), (lora[f[1], 0], xs[f[1], 12, 0:NS]),
                                          (lora[:, 1], ssg[:, 8]))):
                for c in range(4):
                    last = pe.matmul(bank[2 + n][:, c * NS:(c + 1) * NS], w[:, c * P:(c + 1) * P], rhs,
                                     start=True, stop=True)
                last.then_inc(sem("pe_sample"), 1)
            pe.wait_ge(sem("u_kk"), 2)
            flat = lambda q: s4[:, q].rearrange("p c t -> p (c t)")
            pe.matmul(bank[5][:, 0:4 * NS], C("bd"), flat(0), start=True, stop=True).then_inc(sem("pe_sample"), 1)
            pe.wait_ge(sem("u_vectors"), 1)
            pe.wait_ge(sem("u_decay"), 1)
            for q in range(6):
                for c in range(4):
                    last = pe.transpose(bank[2 + q][0:NS, c * P:(c + 1) * P], s4[:, q, c], C("ident"))
                last.then_inc(sem("pe_sample"), 1)
            pe.wait_ge(sem("u_row"), 6)
            pe.matmul(bank[5][:, 0:4 * NS], C("bd"), flat(11), start=True, stop=True).then_inc(sem("pe_sample"), 1)
            pe.wait_ge(sem("u_ygathered"), 32)
            for c in range(4):
                last = pe.transpose(bank[2][:, c * NS:(c + 1) * NS], sym[:, c * P:(c + 1) * P], C("ident")[0:NS, 0:NS])
            last.then_inc(sem("pe_sample"), 1)
            pe.wait_ge(sem("u_y"), 1)
            pe.matmul(bank[3][:, 0:4 * NS], C("bd"), flat(8), start=True, stop=True).then_inc(sem("pe_sample"), 1)
            pe.wait_ge(sem("u_centred"), 2)
            pe.matmul(bank[4][:, 0:4 * NS], C("bd"), flat(0), start=True, stop=True).then_inc(sem("pe_sample"), 1)

            def begin(g, i, s):
                u, prev, kg = 8 * g + 2 * i + s, has_previous(g, i, s), kgs[g % 2]
                pe.wait_ge(sem("a_masked"), 2 * u)
                pe.wait_ge(sem("qz_ready"), 2 * u + 2)

                def keys(c, back):
                    if g == 0:
                        return kg[:, c, bass.ds((2 * i + s - back) * P, P)]
                    if g == 1:
                        return kg[:, c].rearrange("p (b i r) -> p b r i", b=2, r=4)[:, s - back, bass.ds(i, 1)]
                    return kg[:, c].rearrange("p (i r) -> p r i", r=16)[:, bass.ds(4 * i + 2 * s, 2)]

                shape = ("p (r i) -> p r i", 2) if g == 2 else ("p (r i) -> p r i", 1)
                for back in (1, 0) if prev else (0,):
                    for h in range(H):
                        out = bank[2 + back][:, h * P:(h + 1) * P]
                        if g:
                            out = out.rearrange(shape[0], r=shape[1])
                        last = pe.matmul(out, qz[:, s, h], keys(h // 2, back), start=True, stop=True)
                last.then_inc(sem("mm_score"), 1)

            def finish(g, i, s):
                u, prev, vg = 8 * g + 2 * i + s, has_previous(g, i, s), vgs[g % 2]
                pe.wait_ge(sem("a_exp"), 4 * u + 4)
                for back in (1, 0) if prev else (0,):
                    for h in range(H):
                        last = pe.transpose(bank[4 + back][:, h * P:(h + 1) * P], sc[:, s, h, 1 - back], C("ident"))
                last.then_inc(sem("mm_pt"), 1)
                pe.wait_ge(sem("a_pt_cur"), u + 1)
                pe.wait_ge(sem("a_pt_prev"), u + 1)
                pe.wait_ge(sem("a_out"), u)
                for back in (1, 0) if prev else (0,):
                    for h in range(H):
                        last = pe.matmul(bank[6][:, h * HD:(h + 1) * HD], pt[:, s, 1 - back, h],
                                         vg[:, bass.ds(2 * i + s - back, 1), h * HD:(h + 1) * HD],
                                         start=(h == 0 and back == prev), stop=(h == H - 1 and back == 0),
                                         skip_group_check=True)
                last.then_inc(sem("mm_att"), 1)

            for g in range(G):
                pe.wait_ge(sem(f"kv_loaded{g}"), 32 if g == 0 else 48)
                units(pe, g, begin, finish)
            def narrow(base, kk, chunk, hi, lo):
                n, o = chunk // (KD // kk), chunk % (KD // kk)
                if o == 0:
                    pe.wait_ge(sem("w_split"), base + n + 1)
                for c in range(3):
                    q = (P_RO if base == B_RO else P_AO) + 3 * chunk + c
                    pe.wait_ge(sem(f"bank_free{q % 2}"), q // 2)
                    for k in range(kk):
                        for a, b in parts:
                            last = pe.matmul(bank[q % 2][:, 0:PC], wpart[a][:, n % 2, o * kk + k],
                                             (hi, lo)[b][:, k, c * PC:(c + 1) * PC],
                                             start=(k == 0 and (a, b) == (0, 0)), stop=(k == kk - 1 and a == 1))
                    last.then_inc(sem("mm_piece"), 1)

            pe.wait_ge(sem("a_out"), 24)
            pe.wait_ge(sem("or_lo"), 4)
            narrow(B_RO, 4, 0, orh, orl)
            for t in range(9):
                if t + 1 < KD:
                    narrow(B_RO, 4, t + 1, orh, orl)
                w = P if t < NT else NS
                pe.wait_ge(sem("m_sum"), t + 1)
                if t >= 2:
                    pe.wait_ge(sem("oa_lo"), t - 1)
                for c in range(2):
                    last = pe.transpose(bank[2 + t % 2][:, c * w:(c + 1) * w], om[0:w, t % 2, c * P:(c + 1) * P],
                                        C("ident")[0:w, 0:w])
                last.then_inc(sem("mm_om"), 1)
            pe.wait_ge(sem("oa_lo"), 9)
            for chunk in range(KD):
                narrow(B_AO, 2, chunk, oah, oal)
            pe.wait_ge(sem("m_lo"), KD)
            rows(B_WO, P_WO, N_WO)
            pe.wait_ge(sem("n_added"), 2 * KD)
            for n in range(3):
                pe.matmul(bank[2 + n][:, 0:PC], C("mones"), nsum[:, n * PC:(n + 1) * PC], start=True, stop=True)\
                    .then_inc(sem("n_summed"), 1)
            pe.wait_ge(sem("a_split"), 2 * KD)
            rows(B_UP, P_UP, N_UP)
            pe.wait_ge(sem("h_hi"), KF)
            pe.wait_ge(sem("bank_free0"), P_DN // 2)
            pe.wait_ge(sem("bank_free1"), P_DN // 2)
            hpart = (hhi, hlo)
            for o in range(KD):
                for j in range(3):
                    n = 3 * o + j
                    pe.wait_ge(sem("w_split"), B_DN + n + 1)
                    if j == 0 and o >= 2:
                        pe.wait_ge(sem("y_ready2"), 3 * (o - 1))
                    for k in range(8 * j, min(8 * j + 8, KF)):
                        for m_, (a_, _) in enumerate(HLO_PARTS):
                            if o == 0 and k == a_:
                                pe.wait_ge(sem(f"hlo_loaded{m_}"), 16)
                        for c in range(3):
                            for a, b in parts:
                                last = pe.matmul(bank[3 * (o % 2) + c][:, 0:PC], wpart[a][:, n % 2, k - 8 * j],
                                                 hpart[b][:, k, c * PC:(c + 1) * PC],
                                                 start=(k == 0 and (a, b) == (0, 0)), stop=(k == KF - 1 and a == 1))
                    last.then_inc(sem("mm_down"), 1)


def lay_out(x):
    f = np.float32
    a = {k: np.asarray(v) for k, v in x.items()}
    xT = np.concatenate([a["x_prompt"][0], a["x_sample"][:, 0]], 0).T
    w_in = a["w_in"][0]

    def blocks(w):
        kk, nn = w.shape[0] // P, w.shape[1] // P
        return w.reshape(kk, P, nn, P).transpose(2, 1, 0, 3)

    def values(w):
        return w.reshape(2, 4, P, G, H * HD).transpose(3, 0, 2, 1, 4).reshape(2 * G, P, KD, P)

    def pack(w, per):
        b = blocks(w)
        n, _, kk, _ = b.shape
        return b.reshape(n // per, per, P, kk, P).transpose(0, 2, 1, 3, 4).reshape(n // per, P, per * kk, P)

    c0 = 3 * AW
    up = blocks(a["w_up"][0])
    up = up.reshape(2, KF, P, KD, P).transpose(1, 0, 2, 3, 4).reshape(2 * KF, P, KD, P)
    dn = blocks(a["w_down"][0])
    dn = np.concatenate([dn, np.zeros((KD, P, 24 - KF, P), f)], 2).reshape(KD, P, 3, 8, P)\
        .transpose(0, 2, 1, 3, 4).reshape(3 * KD, P, 8, P)
    wst = np.concatenate([
        blocks(w_in[:, 0:2 * AW]), values(w_in[:, 2 * AW:3 * AW]), blocks(w_in[:, c0:c0 + RP]),
        blocks(w_in[:, c0 + RP:]), pack(a["w_rwkv_out"][0], 2), pack(a["w_attn_out"][0], 4),
        blocks(a["w_o"][0]), up, dn], 0)
    assert wst.shape[0] == NB

    def col(v):
        return v.reshape(-1, P).T

    cw, cb = a["conv_w"][0], a["conv_b"][0]

    def pair(v):
        return v.reshape(2, KF, P).transpose(1, 0, 2).reshape(-1)

    par = np.concatenate([
        col(a["ln1_g"][0]), col(a["ln2_g"][0]),
        np.tile(a["q_norm_g"][0], 2)[:, None].repeat(6, 1), np.tile(a["k_norm_g"][0], 2)[:, None].repeat(6, 1),
        col(a["rwkv_mu"][0]), col(a["rwkv_w0"][0]), col(a["rwkv_a0"][0]), col(a["rwkv_k_k"][0]),
        col(a["rwkv_k_a"][0]), col(a["rwkv_r_k"][0].reshape(-1)), col(a["rwkv_gn_g"][0]), col(a["rwkv_gn_b"][0]),
        col(pair(cw[0])), col(pair(cw[1])), col(pair(cw[2])), col(pair(cb))], 1)
    assert par.shape[1] == N_PAR
    st = a["state_rwkv_wkv"][0].reshape(NS, RH, 2, 32, HD).transpose(2, 0, 1, 3, 4).reshape(P, 32 * HD)
    sc = a["state_ffn_conv"][0]
    hist = np.stack([pair(sc[b, i]) for i in range(2) for b in range(NS)]).reshape(2 * NS, 2 * KF, P)
    caches = {f"{kv}c{g}": a[f"cache_{kv}_w{w}"][0].reshape(NS, -1, 256) for kv in "kv"
              for g, w in enumerate((128, 512, 2048))}

    def picked(kv):
        rows = [caches[f"{kv}c{g}"][:, ::d] for g, d in enumerate(DIL)]
        rows[2] = np.concatenate([rows[2], np.zeros((NS, 96, 256), f)], 1)
        return np.stack(rows).reshape(G, NS, 128, H, HD).transpose(0, 1, 3, 2, 4).reshape(96, 128 * HD)

    more0 = {"wkvs": st, "shT": a["state_rwkv_shift"][0].T, "sconvT": hist.transpose(2, 1, 0).reshape(P, -1),
             "sconv1": sc[:, 1], "skc": picked("k"), "svc": picked("v")} | caches
    more = more0 | {"w2": a["rwkv_w2"][0], "a2": a["rwkv_a2"][0], "g2": a["rwkv_g2"][0], "zeros": np.zeros((RP, 1), f)}
    arrays = more | {"xT": xT, "wst": wst.reshape(NB, P, KD * P), "cst": constants(), "par": par}
    return {k: np.ascontiguousarray(v) for k, v in arrays.items()}


def kernel(**x):
    import concourse.bacc as bacc
    from concourse.bass_utils import run_bass_kernel_spmd

    arrays = {f"in_{k}": v for k, v in lay_out(x).items()}
    nc = bacc.Bacc("TRN2", target_bir_lowering=False, num_devices=1)
    ins = {k[3:]: nc.dram_tensor(k, v.shape, F32, kind="ExternalInput").ap() for k, v in arrays.items()}
    outs = {k: nc.dram_tensor(f"out_{k}", v, F32, kind="ExternalOutput").ap() for k, v in OUTS.items()}
    program(nc, ins, outs)
    r = run_bass_kernel_spmd(nc, [arrays], core_ids=[0]).results[0]
    return returned({k: r[f"out_{k}"] for k in OUTS})


def returned(r):
    y = r["yT"].T
    k = r["qkT"][AW:].T.reshape(T, G, H, HD)
    v = r["vtok"].reshape(T, G, H, HD)
    out = [y[:S][None], y[S:][:, None]]
    for g, keep in enumerate((128, 512, 1024)):
        out += [k[S - keep:S, g][None, None], r[f"kc{g}"].reshape(1, NS, -1, H, HD),
                v[S - keep:S, g][None, None], r[f"vc{g}"].reshape(1, NS, -1, H, HD)]
    out += [r["rwlast"][:, 0][None, None], r["rwlast"][:, 1:].T[None]]
    out.append(r["wkvp"].transpose(2, 0, 3, 1).reshape(1, 1, RH, HD, HD))
    out.append(r["wkvs"].reshape(2, NS, RH, 32, HD).transpose(1, 2, 0, 3, 4).reshape(1, NS, RH, HD, HD))
    u = r["convo"].reshape(KF, 2, P, 2 + NS).transpose(3, 1, 0, 2).reshape(2 + NS, 2 * FF)
    out.append(u[0:2][None, None])
    out.append(np.concatenate([r["convs0"][:, None], u[2:][:, None]], 1)[None])
    return tuple(np.ascontiguousarray(o) for o in out)


OUTS = {"yT": [D, T], "wkvs": [P, 32 * HD], "convo": [2 * KF, P, 2 + NS], "convs0": [NS, 2 * FF],
        "kc0": [NS, 128, 256], "kc1": [NS, 512, 256], "kc2": [NS, 513, 256],
        "vc0": [NS, 128, 256], "vc1": [NS, 512, 256], "vc2": [NS, 513, 256],
        "wkvp": [2, HD, 4, HD], "qkT": [2 * AW, T], "vtok": [T, AW], "rwlast": [RP, 1 + NS]}
```
